# Optimizing a Trainium2 kernel written in Bass

```python
import math
import jax
import jax.numpy as jnp
from jax import lax
import numpy as np
import jax, jax.numpy as jnp

D_MODEL = 1024
BATCH = 1
SEQ = 1024
DEPTH = 1

GRID_W = 64
CTX_LEN = 256
EPS = 1e-6
DA_HEADS = 4
DA_D = 64
DA_DV = 2 * DA_D
ROPE_AXIS_DIM = DA_D // 2
ROPE_THETA = 10000.0
Q_BLOCK = 128
GDN_HEADS = 4
GDN_DK = 128
GDN_DV = 128
CONV_K = 3
CHUNK = 64
N_EXPERTS = 16
EXPERT_FF = 1024
CAP_FACTOR = 2
DA_QK = DA_HEADS * 2 * DA_D
DA_V = DA_HEADS * DA_DV
GDN_QK = GDN_HEADS * GDN_DK
GDN_V = GDN_HEADS * GDN_DV
GDN_QKV = 2 * GDN_QK + GDN_V
GDN_AB = 2 * 2 * GDN_HEADS
D_MIX = DA_V + GDN_V
IN_SPLIT_POINTS = (DA_QK, 2 * DA_QK, 2 * DA_QK + DA_V, 2 * DA_QK + DA_V + GDN_QKV, 2 * DA_QK + DA_V + GDN_QKV + GDN_V)
IN_COLS = 2 * DA_QK + DA_V + GDN_QKV + GDN_V + GDN_AB


def rms_norm(x, g):
    xf = x.astype(jnp.float32)
    y = xf * lax.rsqrt(jnp.mean(xf * xf, axis=-1, keepdims=True) + EPS)
    return (y * g.astype(jnp.float32)).astype(x.dtype)

def modulate(x, g, shift, scale):
    return rms_norm(x, g) * (1.0 + scale) + shift

def l2_normalize(t):
    tf = t.astype(jnp.float32)
    return (tf * lax.rsqrt(jnp.sum(tf * tf, axis=-1, keepdims=True) + EPS)).astype(t.dtype)

def rope_axis(x, ang):
    cos = jnp.cos(ang).astype(x.dtype)[:, None, None, :]
    sin = jnp.sin(ang).astype(x.dtype)[:, None, None, :]
    x1, x2 = jnp.split(x, 2, axis=-1)
    return jnp.concatenate([x1 * cos - x2 * sin, x2 * cos + x1 * sin], axis=-1)

def rope_2d(x, ang_row, ang_col):
    xr, xc = jnp.split(x, 2, axis=-1)
    return jnp.concatenate([rope_axis(xr, ang_row), rope_axis(xc, ang_col)], axis=-1)

def diff_attn(q, k, v, lam):
    B, L = q.shape[:2]
    nblk = L // Q_BLOCK
    qb = jnp.moveaxis((q * DA_D ** -0.5).reshape(B, nblk, Q_BLOCK, DA_HEADS, 2, DA_D), 1, 0)

    def block(qi):
        s = jnp.einsum('bqhid,bkhid->bhiqk', qi, k).astype(jnp.float32)
        p = jax.nn.softmax(s, axis=-1)
        a = (p[:, :, 0] - lam * p[:, :, 1]).astype(v.dtype)
        return jnp.einsum('bhqk,bkhe->bqhe', a, v)

    o = lax.map(block, qb)
    return jnp.moveaxis(o, 0, 1).reshape(B, L, DA_HEADS, DA_DV)

def short_conv(x, w):
    L = x.shape[1]
    p = CONV_K // 2
    xp = jnp.pad(x, ((0, 0), (p, p), (0, 0)))
    return jax.nn.silu(sum(xp[:, i:i + L] * w[i] for i in range(CONV_K)))

def gdn_inputs(qkv, ab, conv_w, a_log, dt_bias):
    B, L = qkv.shape[:2]
    q, k, v = jnp.split(short_conv(qkv, conv_w), [GDN_QK, 2 * GDN_QK], axis=-1)
    q = l2_normalize(q.reshape(B, L, GDN_HEADS, GDN_DK)) * GDN_DK ** -0.5
    k = l2_normalize(k.reshape(B, L, GDN_HEADS, GDN_DK))
    v = v.reshape(B, L, GDN_HEADS, GDN_DV)
    ab = ab.reshape(B, L, 2, 2, GDN_HEADS).astype(jnp.float32)
    g = -jnp.exp(a_log.astype(jnp.float32)) * jax.nn.softplus(ab[:, :, 0] + dt_bias.astype(jnp.float32))
    beta = jax.nn.sigmoid(ab[:, :, 1])
    return q, k, v, g, beta

def gdn_chunked(q, k, v, g, beta, s0, need_out):
    B, L, H, dk = k.shape
    dv = v.shape[-1]
    n = L // CHUNK
    f32 = jnp.float32

    def chunks(t):
        t = t.astype(f32).reshape(B, n, CHUNK, *t.shape[2:])
        return jnp.moveaxis(t, (1, 3), (0, 2))

    kc, vc, gc, bc = chunks(k), chunks(v), chunks(g), chunks(beta)
    Gc = jnp.cumsum(gc, axis=-1)
    diff = Gc[..., :, None] - Gc[..., None, :]
    idx = jnp.arange(CHUNK)
    strict = idx[:, None] > idx[None, :]
    dec_strict = jnp.where(strict, jnp.exp(jnp.where(strict, diff, 0.0)), 0.0)
    a_mat = jnp.eye(CHUNK, dtype=f32) + bc[..., None] * jnp.einsum('nbhid,nbhjd->nbhij', kc, kc) * dec_strict
    rhs = jnp.concatenate([(bc * jnp.exp(Gc))[..., None] * kc, bc[..., None] * vc], axis=-1)
    sol = lax.linalg.triangular_solve(a_mat, rhs, left_side=True, lower=True, unit_diagonal=True)
    w, ub = sol[..., :dk], sol[..., dk:]
    kd = kc * jnp.exp(Gc[..., -1:] - Gc)[..., None]
    g_last = jnp.exp(Gc[..., -1])[..., None, None]

    if need_out:
        qc = chunks(q)
        incl = idx[:, None] >= idx[None, :]
        dec_incl = jnp.where(incl, jnp.exp(jnp.where(incl, diff, 0.0)), 0.0)
        qd = qc * jnp.exp(Gc)[..., None]
        aqk = jnp.einsum('nbhid,nbhjd->nbhij', qc, kc) * dec_incl

        def step(s, xs):
            w_n, ub_n, kd_n, gl_n, qd_n, aqk_n = xs
            u = ub_n - jnp.einsum('bhcd,bhde->bhce', w_n, s)
            o = jnp.einsum('bhcd,bhde->bhce', qd_n, s) + jnp.einsum('bhij,bhje->bhie', aqk_n, u)
            return gl_n * s + jnp.einsum('bhcd,bhce->bhde', kd_n, u), o

        s_fin, o = lax.scan(step, s0, (w, ub, kd, g_last, qd, aqk))
        o = jnp.moveaxis(o, (0, 2), (1, 3)).reshape(B, L, H, dv).astype(v.dtype)
        return o, s_fin

    def step_state(s, xs):
        w_n, ub_n, kd_n, gl_n = xs
        u = ub_n - jnp.einsum('bhcd,bhde->bhce', w_n, s)
        return gl_n * s + jnp.einsum('bhcd,bhce->bhde', kd_n, u), None

    s_fin, _ = lax.scan(step_state, s0, (w, ub, kd, g_last))
    return None, s_fin

def bidirectional_gdn(lat, ctx_in, need_ctx_out):
    ql, kl, vl, gl, bl = lat
    qc, kc, vc, gc, bc = ctx_in
    B = ql.shape[0]
    o_lat, o_ctx = None, None
    for d in range(2):
        rev = (lambda t: jnp.flip(t, axis=1)) if d == 1 else (lambda t: t)
        s0 = jnp.zeros((B, GDN_HEADS, GDN_DK, GDN_DV), jnp.float32)
        oc, s_ctx = gdn_chunked(rev(qc), rev(kc), rev(vc), rev(gc[:, :, d]), rev(bc[:, :, d]), s0, need_ctx_out)
        ol, _ = gdn_chunked(rev(ql), rev(kl), rev(vl), rev(gl[:, :, d]), rev(bl[:, :, d]), s_ctx, True)
        o_lat = rev(ol) if o_lat is None else o_lat + rev(ol)
        if need_ctx_out:
            o_ctx = rev(oc) if o_ctx is None else o_ctx + rev(oc)
    return o_lat, o_ctx

def gdn_output(o, gate, gdn_norm_g):
    B, L = o.shape[:2]
    y = rms_norm(o, gdn_norm_g) * jax.nn.silu(gate.reshape(B, L, GDN_HEADS, GDN_DV))
    return y.reshape(B, L, GDN_V)

def expert_choice_ffn(h, w_router, w_gate, w_up, w_down):
    def route_set(t):
        n = t.shape[0]
        cap = CAP_FACTOR * n // N_EXPERTS
        aff = jax.nn.softmax((t @ w_router).astype(jnp.float32), axis=-1)
        gate, idx = lax.top_k(aff.T, cap)
        xe = t[idx]
        hid = jax.nn.silu(jnp.einsum('ecd,edf->ecf', xe, w_gate)) * jnp.einsum('ecd,edf->ecf', xe, w_up)
        ye = jnp.einsum('ecf,efd->ecd', hid, w_down) * gate[..., None].astype(t.dtype)
        return jnp.zeros_like(t).at[idx.reshape(-1)].add(ye.reshape(-1, t.shape[-1]))

    return jax.vmap(route_set)(h)

def hybrid_layer(x, xc, c, c_ctx, ang_row, ang_col, lam_init, last,
                 w_mod, b_mod, norm1_g, w_in, conv_w, a_log, dt_bias, gdn_norm_g,
                 lam_q1, lam_k1, lam_q2, lam_k2, da_subln_g, w_out, norm2_g,
                 w_router, w_gate, w_up, w_down):
    B, L, _ = x.shape
    Lc = xc.shape[1]
    sh1, sc1, gt1, sh2, sc2, gt2 = jnp.split((jax.nn.silu(c) @ w_mod + b_mod)[:, None, :], 6, axis=-1)
    sh1c, sc1c, gt1c, sh2c, sc2c, gt2c = jnp.split(jax.nn.silu(c_ctx) @ w_mod + b_mod, 6, axis=-1)

    p = modulate(x, norm1_g, sh1, sc1) @ w_in
    pc = modulate(xc, norm1_g, sh1c, sc1c) @ w_in
    q, k, v, qkv, gate, ab = jnp.split(p, IN_SPLIT_POINTS, axis=-1)
    qc, kc, vc, qkvc, gatec, abc = jnp.split(pc, IN_SPLIT_POINTS, axis=-1)

    lam = (jnp.exp(jnp.sum(lam_q1 * lam_k1, dtype=jnp.float32))
           - jnp.exp(jnp.sum(lam_q2 * lam_k2, dtype=jnp.float32)) + lam_init)
    k_c = kc.reshape(B, Lc, DA_HEADS, 2, DA_D)
    v_c = vc.reshape(B, Lc, DA_HEADS, DA_DV)
    q_l = rope_2d(q.reshape(B, L, DA_HEADS, 2, DA_D), ang_row, ang_col)
    k_l = rope_2d(k.reshape(B, L, DA_HEADS, 2, DA_D), ang_row, ang_col)
    o_da = diff_attn(q_l, jnp.concatenate([k_c, k_l], axis=1),
                     jnp.concatenate([v_c, v.reshape(B, L, DA_HEADS, DA_DV)], axis=1), lam)
    o_da = (rms_norm(o_da, da_subln_g) * (1.0 - lam_init)).reshape(B, L, DA_V)

    o_gdn_l, o_gdn_c = bidirectional_gdn(gdn_inputs(qkv, ab, conv_w, a_log, dt_bias),
                                         gdn_inputs(qkvc, abc, conv_w, a_log, dt_bias), not last)
    o_gdn = gdn_output(o_gdn_l, gate, gdn_norm_g)

    x_new = x + gt1 * (jnp.concatenate([o_da, o_gdn], axis=-1) @ w_out)
    x_new = x_new + gt2 * expert_choice_ffn(modulate(x_new, norm2_g, sh2, sc2), w_router, w_gate, w_up, w_down)

    if not last:
        o_da_c = diff_attn(qc.reshape(B, Lc, DA_HEADS, 2, DA_D), k_c, v_c, lam)
        o_da_c = (rms_norm(o_da_c, da_subln_g) * (1.0 - lam_init)).reshape(B, Lc, DA_V)
        xc = xc + gt1c * (jnp.concatenate([o_da_c, gdn_output(o_gdn_c, gatec, gdn_norm_g)], axis=-1) @ w_out)
        xc = xc + gt2c * expert_choice_ffn(modulate(xc, norm2_g, sh2c, sc2c), w_router, w_gate, w_up, w_down)
    return x_new, xc

def first_inputs(seed: int = 0) -> dict:
    key = jax.random.key(seed)
    ks = jax.random.split(key, 24)
    D = D_MODEL
    f32 = jnp.float32

    def nrm(k, shape, s):
        return jax.random.normal(k, shape, f32) * s

    dt = jnp.exp(jax.random.uniform(ks[10], (DEPTH, 2, GDN_HEADS), f32, math.log(1e-3), math.log(1e-1)))
    return {
        'x': nrm(ks[0], (BATCH, SEQ, D), 1.0),
        'c': nrm(ks[1], (BATCH, D), 1.0),
        'ctx': nrm(ks[2], (BATCH, CTX_LEN, D), 1.0),
        'c_ctx': nrm(ks[3], (D,), 1.0),
        'w_mod': nrm(ks[4], (DEPTH, D, 6 * D), 0.5 * D ** -0.5),
        'b_mod': nrm(ks[5], (DEPTH, 6 * D), 0.01),
        'norm1_g': 1.0 + nrm(ks[6], (DEPTH, D), 0.05),
        'w_in': nrm(ks[7], (DEPTH, D, IN_COLS), D ** -0.5),
        'conv_w': nrm(ks[8], (DEPTH, CONV_K, GDN_QKV), CONV_K ** -0.5),
        'a_log': jnp.log(jax.random.uniform(ks[9], (DEPTH, 2, GDN_HEADS), f32, 1.0, 16.0)),
        'dt_bias': dt + jnp.log(-jnp.expm1(-dt)),
        'gdn_norm_g': 1.0 + nrm(ks[11], (DEPTH, GDN_DV), 0.05),
        'lam_q1': nrm(ks[12], (DEPTH, DA_D), 0.1),
        'lam_k1': nrm(ks[13], (DEPTH, DA_D), 0.1),
        'lam_q2': nrm(ks[14], (DEPTH, DA_D), 0.1),
        'lam_k2': nrm(ks[15], (DEPTH, DA_D), 0.1),
        'da_subln_g': 1.0 + nrm(ks[16], (DEPTH, DA_DV), 0.05),
        'w_out': nrm(ks[17], (DEPTH, D_MIX, D), D_MIX ** -0.5),
        'norm2_g': 1.0 + nrm(ks[18], (DEPTH, D), 0.05),
        'w_router': nrm(ks[19], (DEPTH, D, N_EXPERTS), D ** -0.5),
        'w_gate': nrm(ks[20], (DEPTH, N_EXPERTS, D, EXPERT_FF), D ** -0.5),
        'w_up': nrm(ks[21], (DEPTH, N_EXPERTS, D, EXPERT_FF), D ** -0.5),
        'w_down': nrm(ks[22], (DEPTH, N_EXPERTS, EXPERT_FF, D), EXPERT_FF ** -0.5),
        'final_g': 1.0 + nrm(ks[23], (D,), 0.05),
    }

def first_block(x, c, ctx, c_ctx, w_mod, b_mod, norm1_g, w_in, conv_w, a_log, dt_bias, gdn_norm_g,
              lam_q1, lam_k1, lam_q2, lam_k2, da_subln_g, w_out, norm2_g,
              w_router, w_gate, w_up, w_down, final_g):
    f32 = jnp.float32
    L = x.shape[1]
    ROWS = L // GRID_W
    rows = jnp.repeat(jnp.arange(ROWS, dtype=f32), GRID_W)
    cols = jnp.tile(jnp.arange(GRID_W, dtype=f32), ROWS)
    inv_freq = jnp.power(ROPE_THETA, -jnp.arange(0, ROPE_AXIS_DIM, 2, dtype=f32) / ROPE_AXIS_DIM)
    ang_row = rows[:, None] * inv_freq[None, :]
    ang_col = cols[:, None] * inv_freq[None, :]

    xc = ctx
    for layer in range(DEPTH):
        lam_init = 0.8 - 0.6 * math.exp(-0.3 * layer)
        x, xc = hybrid_layer(x, xc, c, c_ctx, ang_row, ang_col, lam_init, layer == DEPTH - 1,
                             w_mod[layer], b_mod[layer], norm1_g[layer], w_in[layer], conv_w[layer],
                             a_log[layer], dt_bias[layer], gdn_norm_g[layer],
                             lam_q1[layer], lam_k1[layer], lam_q2[layer], lam_k2[layer], da_subln_g[layer],
                             w_out[layer], norm2_g[layer], w_router[layer], w_gate[layer], w_up[layer], w_down[layer])
    return rms_norm(x, final_g)


D_RNN = 1280
RNN_BLOCKS = 10
RNN_BW = D_RNN // RNN_BLOCKS
CONV_W = 4
LRU_C = 8.0
N_HEADS = 8
HEAD_DIM = 128
D_ATT = N_HEADS * HEAD_DIM
KV_RANK = 256
IDX_HEADS = 8
IDX_DIM = 64
TOPK_MAX = 256
IDX_SCALE = IDX_DIM ** -0.5 * IDX_HEADS ** -0.5
ATT_SCALE = HEAD_DIM ** -0.5
N_GROUPS = 4
EXP_PER_GROUP = 8
N_EXPERTS_2 = N_GROUPS * EXP_PER_GROUP
TOP_K_INNER = 2
D_EXPERT = 512
MOE_BLOCK = 128
N_BRANCH = 2

SPLITS = (D_RNN, D_RNN, D_ATT, KV_RANK, IDX_HEADS * IDX_DIM, IDX_DIM, IDX_HEADS, N_BRANCH * D_MODEL)
D_IN = sum(SPLITS)


def rmsnorm(x, g):
    xf = x.astype(jnp.float32)
    y = xf * lax.rsqrt(jnp.mean(xf * xf, axis=-1, keepdims=True) + EPS)
    return (y * g.astype(jnp.float32)).astype(x.dtype)

def modulate_2(x, g, shift, scale):
    return rmsnorm(x, g) * (1 + scale[:, None, :]) + shift[:, None, :]

def causal_dwconv(x, w, b):
    y = lax.conv_general_dilated(x, w[:, None, :], window_strides=(1,), padding=[(CONV_W - 1, 0)],
                                 dimension_numbers=('NWC', 'WIO', 'NWC'), feature_group_count=x.shape[-1])
    return y + b

def rg_lru(x, w_a, b_a, w_x, b_x, lam):
    B_, S_, _ = x.shape
    xb = x.reshape(B_, S_, RNN_BLOCKS, RNN_BW)
    r = jax.nn.sigmoid(jnp.einsum('bsnc,ncd->bsnd', xb, w_a).reshape(B_, S_, D_RNN) + b_a)
    i = jax.nn.sigmoid(jnp.einsum('bsnc,ncd->bsnd', xb, w_x).reshape(B_, S_, D_RNN) + b_x)
    log_a = -LRU_C * jax.nn.softplus(-lam.astype(jnp.float32)) * r.astype(jnp.float32)
    a = jnp.exp(log_a)
    inp = jnp.sqrt(-jnp.expm1(2.0 * log_a)) * (i * x).astype(jnp.float32)

    def combine(lhs, rhs):
        a1, b1 = lhs
        a2, b2 = rhs
        return a1 * a2, a2 * b1 + b2

    _, h = lax.associative_scan(combine, (a, inp), axis=1)
    return h.astype(x.dtype)

def dsa_attention(q, c_kv, q_idx, k_idx, w_idx, w_uk, w_uv):
    B_, S_ = q.shape[0], q.shape[1]
    topk = min(TOPK_MAX, S_ // 4)
    nblk = S_ // Q_BLOCK
    slopes = 2.0 ** (-8.0 * jnp.arange(1, N_HEADS + 1, dtype=jnp.float32) / N_HEADS)
    key_pos = jnp.arange(S_)

    def to_blocks(t):
        return jnp.moveaxis(t.reshape((B_, nblk, Q_BLOCK) + t.shape[2:]), 1, 0)

    def one_block(args):
        qb, qib, wib, q0 = args
        qpos = q0 + jnp.arange(Q_BLOCK)
        causal = key_pos[None, :] <= qpos[:, None]
        rel = jax.nn.relu(jnp.einsum('bqhd,bsd->bqhs', qib, k_idx).astype(jnp.float32))
        score = jnp.einsum('bqh,bqhs->bqs', wib.astype(jnp.float32), rel) * IDX_SCALE
        score = jnp.where(causal[None], score, -jnp.inf)
        _, sel = lax.top_k(score, topk)
        c_sel = jax.vmap(lambda cb, ib: cb[ib])(c_kv, sel)
        q_lat = jnp.einsum('bqhd,rhd->bqhr', qb, w_uk)
        logits = jnp.einsum('bqhr,bqkr->bqhk', q_lat, c_sel).astype(jnp.float32) * ATT_SCALE
        dist = (qpos[None, :, None] - sel).astype(jnp.float32)
        logits = logits - slopes[None, None, :, None] * dist[:, :, None, :]
        valid = sel <= qpos[None, :, None]
        logits = jnp.where(valid[:, :, None, :], logits, -jnp.inf)
        p = jax.nn.softmax(logits, axis=-1).astype(c_sel.dtype)
        o_lat = jnp.einsum('bqhk,bqkr->bqhr', p, c_sel)
        return jnp.einsum('bqhr,rhd->bqhd', o_lat, w_uv)

    out = lax.map(one_block, (to_blocks(q), to_blocks(q_idx), to_blocks(w_idx), jnp.arange(nblk) * Q_BLOCK))
    return jnp.moveaxis(out, 0, 1).reshape(B_, S_, N_HEADS * HEAD_DIM)

def hier_moe(x, w_group, b_group, w_expert, b_expert, w1, w3, w2):
    B_, S_, D_ = x.shape
    T = B_ * S_
    xf = x.reshape(T, D_)
    g_logits = (xf @ w_group + b_group).astype(jnp.float32)
    g_sel = jnp.argmax(g_logits, axis=-1)
    g_w = jnp.take_along_axis(jax.nn.softmax(g_logits, axis=-1), g_sel[:, None], axis=-1)
    e_logits = (xf @ w_expert + b_expert).astype(jnp.float32).reshape(T, N_GROUPS, EXP_PER_GROUP)
    e_logits = jnp.take_along_axis(e_logits, g_sel[:, None, None], axis=1)[:, 0]
    e_top, e_loc = lax.top_k(e_logits, TOP_K_INNER)
    gate = (g_w * jax.nn.softmax(e_top, axis=-1)).reshape(-1)
    eid = (g_sel[:, None] * EXP_PER_GROUP + e_loc).reshape(-1)
    tok = jnp.repeat(jnp.arange(T, dtype=jnp.int32), TOP_K_INNER)
    A = T * TOP_K_INNER
    order = jnp.argsort(eid)
    eid_s = eid[order]
    counts = jnp.bincount(eid, length=N_EXPERTS_2)
    padded = (counts + MOE_BLOCK - 1) // MOE_BLOCK * MOE_BLOCK
    start = jnp.cumsum(counts) - counts
    pstart = jnp.cumsum(padded) - padded
    dest = pstart[eid_s] + jnp.arange(A) - start[eid_s]
    n_rows = A + N_EXPERTS_2 * MOE_BLOCK
    n_blk = n_rows // MOE_BLOCK
    row_tok = jnp.zeros((n_rows,), jnp.int32).at[dest].set(tok[order])
    row_gate = jnp.zeros((n_rows,), x.dtype).at[dest].set(gate[order].astype(x.dtype))
    blk_exp = jnp.minimum(jnp.searchsorted(jnp.cumsum(padded), jnp.arange(n_blk) * MOE_BLOCK, side='right'),
                          N_EXPERTS_2 - 1)
    xs = xf[row_tok].reshape(n_blk, MOE_BLOCK, D_)

    def expert_block(args):
        xb, e = args
        hid = jax.nn.silu(xb @ w1[e]) * (xb @ w3[e])
        return hid @ w2[e]

    ys = lax.map(expert_block, (xs, blk_exp)).reshape(n_rows, D_)
    out = jax.ops.segment_sum(ys * row_gate[:, None], row_tok, num_segments=T)
    return out.reshape(B_, S_, D_)

def _w(k, shape, fan_in, mult=1.0):
    return jax.random.normal(k, shape, jnp.float32) * (mult * fan_in ** -0.5)

def _small(k, shape):
    return 0.01 * jax.random.normal(k, shape, jnp.float32)

def _gain(k, shape):
    return 1.0 + 0.01 * jax.random.normal(k, shape, jnp.float32)

def second_inputs(seed: int = 0) -> dict:
    key = jax.random.key(seed)
    ks = list(jax.random.split(key, 32))
    L = DEPTH
    u = jax.random.uniform(ks.pop(), (L, D_RNN), jnp.float32, minval=0.9, maxval=0.999)
    a0 = u ** (1.0 / LRU_C)
    lru_lambda = jnp.log(a0) - jnp.log1p(-a0)
    return {
        'x': jax.random.normal(ks.pop(), (BATCH, SEQ, D_MODEL), jnp.float32),
        'c': jax.random.normal(ks.pop(), (BATCH, D_MODEL), jnp.float32),
        'w_mod': _w(ks.pop(), (L, D_MODEL, 6 * D_MODEL), D_MODEL, 0.5),
        'b_mod': _small(ks.pop(), (L, 6 * D_MODEL)),
        'norm1_g': _gain(ks.pop(), (L, D_MODEL)),
        'w_in': _w(ks.pop(), (L, D_MODEL, D_IN), D_MODEL),
        'conv_w': _w(ks.pop(), (L, CONV_W, D_RNN), CONV_W),
        'conv_b': _small(ks.pop(), (L, D_RNN)),
        'w_rg_a': _w(ks.pop(), (L, RNN_BLOCKS, RNN_BW, RNN_BW), RNN_BW),
        'b_rg_a': _small(ks.pop(), (L, D_RNN)),
        'w_rg_x': _w(ks.pop(), (L, RNN_BLOCKS, RNN_BW, RNN_BW), RNN_BW),
        'b_rg_x': _small(ks.pop(), (L, D_RNN)),
        'lru_lambda': lru_lambda,
        'kv_norm_g': _gain(ks.pop(), (L, KV_RANK)),
        'w_uk': _w(ks.pop(), (L, KV_RANK, N_HEADS, HEAD_DIM), KV_RANK),
        'w_uv': _w(ks.pop(), (L, KV_RANK, N_HEADS, HEAD_DIM), KV_RANK),
        'w_rnn_out': _w(ks.pop(), (L, D_RNN, D_MODEL), D_RNN),
        'w_att_out': _w(ks.pop(), (L, D_ATT, D_MODEL), D_ATT),
        'w_out': _w(ks.pop(), (L, D_MODEL, D_MODEL), D_MODEL),
        'norm2_g': _gain(ks.pop(), (L, D_MODEL)),
        'w_group': _w(ks.pop(), (L, D_MODEL, N_GROUPS), D_MODEL),
        'b_group': _small(ks.pop(), (L, N_GROUPS)),
        'w_expert': _w(ks.pop(), (L, D_MODEL, N_EXPERTS_2), D_MODEL),
        'b_expert': _small(ks.pop(), (L, N_EXPERTS_2)),
        'moe_w1': _w(ks.pop(), (L, N_EXPERTS_2, D_MODEL, D_EXPERT), D_MODEL),
        'moe_w3': _w(ks.pop(), (L, N_EXPERTS_2, D_MODEL, D_EXPERT), D_MODEL),
        'moe_w2': _w(ks.pop(), (L, N_EXPERTS_2, D_EXPERT, D_MODEL), D_EXPERT),
        'final_g': _gain(ks.pop(), (D_MODEL,)),
    }

def second_block(x, c, w_mod, b_mod, norm1_g, w_in, conv_w, conv_b, w_rg_a, b_rg_a, w_rg_x, b_rg_x,
              lru_lambda, kv_norm_g, w_uk, w_uv, w_rnn_out, w_att_out, w_out, norm2_g, w_group, b_group,
              w_expert, b_expert, moe_w1, moe_w3, moe_w2, final_g):
    B_, S_, _ = x.shape
    split_pts = [int(v) for v in np.cumsum(SPLITS)[:-1]]
    h = x
    for l in range(DEPTH):
        mod = jax.nn.silu(c) @ w_mod[l] + b_mod[l]
        sh1, sc1, g1, sh2, sc2, g2 = jnp.split(mod, 6, axis=-1)
        u = modulate_2(h, norm1_g[l], sh1, sc1)
        proj = u @ w_in[l]
        xr, gr, q, ckv, qi, ki, wi, mg = jnp.split(proj, split_pts, axis=-1)
        hr = rg_lru(causal_dwconv(xr, conv_w[l], conv_b[l]), w_rg_a[l], b_rg_a[l], w_rg_x[l], b_rg_x[l],
                    lru_lambda[l])
        y_a = (jax.nn.gelu(gr) * hr) @ w_rnn_out[l]
        att = dsa_attention(q.reshape(B_, S_, N_HEADS, HEAD_DIM), rmsnorm(ckv, kv_norm_g[l]),
                            qi.reshape(B_, S_, IDX_HEADS, IDX_DIM), ki, wi, w_uk[l], w_uv[l])
        y_b = att @ w_att_out[l]
        ga, gb = jnp.split(jax.nn.sigmoid(mg), N_BRANCH, axis=-1)
        mix = (ga * y_a + gb * y_b) @ w_out[l]
        h = h + g1[:, None, :] * mix
        u2 = modulate_2(h, norm2_g[l], sh2, sc2)
        h = h + g2[:, None, :] * hier_moe(u2, w_group[l], b_group[l], w_expert[l], b_expert[l],
                                          moe_w1[l], moe_w3[l], moe_w2[l])
    return rmsnorm(h, final_g)


def setup_inputs(seed=0):
    out = dict(first_inputs(seed))
    for name, value in second_inputs(seed + 1).items():
        if name != "x":
            out[name + "_2"] = value
    return out


def reference(
    x, c, ctx, c_ctx, w_mod, b_mod, norm1_g, w_in, conv_w, a_log, dt_bias, gdn_norm_g, lam_q1,
    lam_k1, lam_q2, lam_k2, da_subln_g, w_out, norm2_g, w_router, w_gate, w_up, w_down, final_g,
    c_2, w_mod_2, b_mod_2, norm1_g_2, w_in_2, conv_w_2, conv_b_2, w_rg_a_2, b_rg_a_2, w_rg_x_2,
    b_rg_x_2, lru_lambda_2, kv_norm_g_2, w_uk_2, w_uv_2, w_rnn_out_2, w_att_out_2, w_out_2,
    norm2_g_2, w_group_2, b_group_2, w_expert_2, b_expert_2, moe_w1_2, moe_w3_2, moe_w2_2,
    final_g_2,
):
    x = first_block(
        x, c, ctx, c_ctx, w_mod, b_mod, norm1_g, w_in, conv_w, a_log, dt_bias, gdn_norm_g,
        lam_q1, lam_k1, lam_q2, lam_k2, da_subln_g, w_out, norm2_g, w_router, w_gate, w_up,
        w_down, final_g,
    )
    return second_block(
        x, c_2, w_mod_2, b_mod_2, norm1_g_2, w_in_2, conv_w_2, conv_b_2, w_rg_a_2, b_rg_a_2,
        w_rg_x_2, b_rg_x_2, lru_lambda_2, kv_norm_g_2, w_uk_2, w_uv_2, w_rnn_out_2, w_att_out_2,
        w_out_2, norm2_g_2, w_group_2, b_group_2, w_expert_2, b_expert_2, moe_w1_2, moe_w3_2,
        moe_w2_2, final_g_2,
    )


_drawn_inputs = setup_inputs


def setup_inputs(seed=0):
    import zlib

    import numpy as np

    out = dict(_drawn_inputs(seed))
    spreads = {}
    factors = {'b_mod': 3.28,
     'norm1_g': 3.079,
     'gdn_norm_g': 3.755,
     'lam_q1': 5.246,
     'lam_k1': 2.7,
     'lam_q2': 8.0,
     'lam_k2': 4.639,
     'da_subln_g': 3.912,
     'norm2_g': 3.554,
     'b_mod_2': 3.333,
     'norm1_g_2': 5.954,
     'conv_b_2': 6.155,
     'b_rg_a_2': 8.0,
     'b_rg_x_2': 8.0,
     'kv_norm_g_2': 8.0,
     'norm2_g_2': 8.0,
     'b_group_2': 7.494,
     'b_expert_2': 8.0,
     'final_g_2': 5.794}
    for name, (base, spread) in spreads.items():
        noise = np.random.default_rng([zlib.crc32(name.encode()), seed]).standard_normal(out[name].shape)
        drawn = base * np.exp(spread * noise) if base else spread * noise
        out[name] = jnp.asarray(drawn.astype(out[name].dtype))
    for name, factor in factors.items():
        out[name] = (out[name] * factor).astype(out[name].dtype)
    return out
```

```python
from contextlib import ExitStack

import numpy as np

import concourse.bass as bass
from concourse import mybir

F32 = mybir.dt.float32
I32 = mybir.dt.int32
U32 = mybir.dt.uint32
ALU = mybir.AluOpType
ACT = mybir.ActivationFunctionType
AX = mybir.AxisListType
P = 128
BANK = 512
EPS = 1e-6

D = 1024
KD = D // P
SEQ = 1024
CTX = 256
T1 = CTX + SEQ
HEADS1 = 4
NMOD = 6 * D
NEG = -1e30


class Phase:

    def __init__(self, nc, name):
        self.nc, self.name = nc, name

    def __enter__(self):
        self.stack = ExitStack()
        self.stack.__enter__()
        self.sems = []
        self.passed = self.sem("passed")
        return self

    def __exit__(self, *e):
        if e[0] is not None:
            return False
        self.stack.close()
        self.nc.clear_and_free_semaphores(self.sems)
        self.nc.all_engine_barrier()
        return False

    def sb(self, name, shape, dt=F32):
        return self.stack.enter_context(self.nc.sbuf_tensor(f"{self.name}_{name}", shape, dt))

    def ps(self, name, shape):
        return self.stack.enter_context(self.nc.psum_tensor(f"{self.name}_{name}", shape, F32))

    def sem(self, name):
        s = self.nc.alloc_semaphore(f"{self.name}_{name}")
        self.sems.append(s)
        return s


def columns(row):
    return row.rearrange("(k p) -> p k", p=P)


def on_all(row, n=P):
    return row.rearrange("(a d) -> a d", a=1).to_broadcast([n, row.shape[0]])


def modulation(nc, name, conds, w, b, out):
    n = len(conds)
    COLS = BANK
    steps = NMOD // COLS
    w_v = w.rearrange("(k p) n -> p k n", p=P)
    with Phase(nc, name) as ph:
        c_in = ph.sb("c_in", [P, n, KD])
        c_act = ph.sb("c_act", [P, KD, n])
        w_buf = ph.sb("w", [P, 2, KD, COLS])
        bias = ph.sb("bias", [n, NMOD])
        rows = ph.sb("rows", [n, NMOD])
        acc = ph.ps("acc", [P, 2, BANK])
        inputs_in = ph.sem("inputs_in")
        silu_done = ph.sem("silu_done")
        w_in = [ph.sem("w_in0"), ph.sem("w_in1")]
        w_used = ph.sem("w_used")
        acc_ready = ph.sem("acc_ready")
        acc_free = ph.sem("acc_free")
        stored = ph.sem("stored")
        with nc.Block() as block:

            @block.sync
            def _(sp):
                for i in range(n):
                    sp.dma_start(c_in[:, i, :], columns(conds[i]), allow_slow_non_contiguous=True).then_inc(inputs_in, 16)
                sp.dma_start(bias[:, :], on_all(b, n)).then_inc(inputs_in, 16)
                with sp.Fori(0, steps // 2) as i:
                    for half in range(2):
                        sp.wait_ge(w_used, i * 2 + half + 1)
                        sp.dma_start(w_buf[:, half], w_v[:, :, bass.ds(i * (2 * COLS) + half * COLS, COLS)]).then_inc(w_in[half], 16)
                sp.wait_ge(acc_free, steps + 2)
                sp.dma_start(out, rows[:, :]).then_inc(stored, 16)
                sp.wait_ge(stored, 16)

            @block.scalar
            def _(act):
                act.wait_ge(inputs_in, 16 * (n + 1))
                for i in range(n):
                    last = act.activation(c_act[:, :, i], c_in[:, i, :], ACT.Silu)
                last.then_inc(silu_done, 1)

            @block.tensor
            def _(pe):
                pe.sem_inc(w_used, 2)
                pe.wait_ge(silu_done, 1)
                with pe.Fori(0, steps // 2) as i:
                    for half in range(2):
                        pe.wait_ge(w_in[half], i * 16 + 16)
                        pe.wait_ge(acc_free, i * 2 + half + 1)
                        for k in range(KD):
                            last = pe.matmul(acc[0:n, half, :], c_act[:, k, :], w_buf[:, half, k, :],
                                             start=(k == 0), stop=(k == KD - 1))
                        last.then_inc(acc_ready, 1)
                        pe.wait_ge(acc_ready, i * 2 + half + 1)
                        pe.sem_inc(w_used, 1)

            @block.vector
            def _(dve):
                dve.sem_inc(acc_free, 2)
                dve.wait_ge(inputs_in, 16 * (n + 1))
                with dve.Fori(0, steps // 2) as i:
                    for half in range(2):
                        at = bass.ds(i * (2 * COLS) + half * COLS, COLS)
                        dve.wait_ge(acc_ready, i * 2 + half + 1)
                        dve.tensor_tensor(rows[:, at], acc[0:n, half, :], bias[:, at], ALU.add).then_inc(acc_free, 1)


def norm_transpose(nc, name, k, src, g, shift, scale, out_t, out_n=None):
    n = src.shape[0] // P
    out_v = out_t.rearrange("(k p) t -> p k t", p=P)
    with Phase(nc, name) as ph:
        gain = ph.sb("gain", [P, KD])
        sh = ph.sb("sh", [P, KD])
        sc = ph.sb("sc", [P, KD])
        x = ph.sb("x", [P, 2, D])
        sq = ph.sb("sq", [P, D])
        xn = ph.sb("xn", [P, 2, D])
        ss = ph.sb("ss", [P, 2])
        ms = ph.sb("ms", [P, 2])
        rstd = ph.sb("rstd", [P, 2])
        ht = ph.sb("ht", [P, 2, KD, P])
        turned = ph.ps("turned", [P, 2, KD, P])
        vecs_in = ph.sem("vecs_in")
        gain_done = ph.sem("gain_done")
        x_in = [ph.sem("x_in0"), ph.sem("x_in1")]
        sq_done = ph.sem("sq_done")
        ms_done = ph.sem("ms_done")
        rstd_done = ph.sem("rstd_done")
        xn_done = ph.sem("xn_done")
        turned_ready = ph.sem("turned_ready")
        ht_dve = ph.sem("ht_dve")
        ht_act = ph.sem("ht_act")
        t_out = [ph.sem("t_out0"), ph.sem("t_out1")]
        n_out = [ph.sem("n_out0"), ph.sem("n_out1")]
        with nc.Block() as block:

            @block.sync
            def _(sp):
                for dst, row in ((gain, g), (sh, shift), (sc, scale)):
                    sp.dma_start(dst[:, :], columns(row), allow_slow_non_contiguous=True).then_inc(vecs_in, 16)
                with sp.Fori(0, n // 2) as i:
                    for half in range(2):
                        sp.wait_ge(xn_done, i * 2 + half + 1)
                        sp.dma_start(x[:, half, :], src[bass.ds(i * (2 * P) + half * P, P), :]).then_inc(x_in[half], 16)

            @block.scalar
            def _(act):
                act.wait_ge(gain_done, 1)
                with act.Fori(0, n // 2) as i:
                    for half in range(2):
                        t = i * 2 + half
                        act.wait_ge(x_in[half], i * 16 + 16)
                        act.wait_ge(xn_done, t + 1)
                        act.wait_ge(sq_done, t + 1)
                        act.activation(sq[:, :], x[:, half, :], ACT.Square, accum_out=ss[:, half:half + 1]).then_inc(sq_done, 1)
                        act.wait_ge(turned_ready, t + 1)
                        act.wait_ge(t_out[half], i * 16 + 16)
                        for c in range(KD // 2, KD):
                            last = act.activation(ht[:, half, c, :], turned[:, half, c, :], ACT.Identity,
                                                  bias=sh[:, c:c + 1], scale=gain[:, c:c + 1])
                        last.then_inc(ht_act, 1)
                        act.wait_ge(ht_act, t + 3)
                        act.wait_ge(ht_dve, t + 3)
                        act.dma_start(out_v[:, :, bass.ds(t * P, P)], ht[:, half]).then_inc(t_out[half], 16)
                        if out_n is not None:
                            act.dma_start(out_n[bass.ds(t * P, P), :], xn[:, half, :]).then_inc(n_out[half], 16)
                for half in range(2):
                    act.wait_ge(t_out[half], 16 * (n // 2) + 16)
                    if out_n is not None:
                        act.wait_ge(n_out[half], 16 * (n // 2) + 16)

            @block.gpsimd
            def _(pool):
                with pool.Fori(0, n // 2) as i:
                    for half in range(2):
                        t = i * 2 + half
                        pool.wait_ge(sq_done, t + 2)
                        pool.sem_inc(ph.passed, 1)
                        pool.tensor_scalar(ms[:, half:half + 1], ss[:, half:half + 1], 1.0 / D, EPS, ALU.mult, ALU.add).then_inc(ms_done, 1)
                        pool.wait_ge(ms_done, t + 1)
                        pool.tensor_tensor(rstd[:, half:half + 1], ms[:, half:half + 1], k.minus_half[:, :], ALU.pow).then_inc(rstd_done, 1)

            @block.vector
            def _(dve):
                dve.sem_inc(xn_done, 2)
                dve.sem_inc(sq_done, 1)
                dve.sem_inc(ht_dve, 2)
                dve.sem_inc(ht_act, 2)
                for half in range(2):
                    dve.sem_inc(t_out[half], 16)
                    dve.sem_inc(n_out[half], 16)
                dve.wait_ge(vecs_in, 48)
                dve.scalar_tensor_tensor(gain[:, :], sc[:, :], 1.0, gain[:, :], ALU.add, ALU.mult).then_inc(gain_done, 1)
                dve.wait_ge(gain_done, 1)
                with dve.Fori(0, n // 2) as i:
                    for half in range(2):
                        t = i * 2 + half
                        dve.wait_ge(rstd_done, t + 1)
                        if out_n is not None:
                            dve.wait_ge(n_out[half], i * 16 + 16)
                        dve.tensor_scalar(xn[:, half, :], x[:, half, :], rstd[:, half:half + 1], None, ALU.mult).then_inc(xn_done, 1)
                        dve.wait_ge(turned_ready, t + 1)
                        dve.wait_ge(t_out[half], i * 16 + 16)
                        for c in range(KD // 2):
                            last = dve.tensor_scalar(ht[:, half, c, :], turned[:, half, c, :], gain[:, c:c + 1], sh[:, c:c + 1],
                                                     ALU.mult, ALU.add)
                        last.then_inc(ht_dve, 1)

            @block.tensor
            def _(pe):
                with pe.Fori(0, n // 2) as i:
                    for half in range(2):
                        t = i * 2 + half
                        pe.wait_ge(xn_done, t + 3)
                        pe.wait_ge(ht_dve, t + 1)
                        pe.wait_ge(ht_act, t + 1)
                        for c in range(KD):
                            last = pe.transpose(turned[:, half, c, :], xn[:, half, c * P:(c + 1) * P], k.ident[:, :])
                        last.then_inc(turned_ready, 1)


def gemm_t(nc, name, act_t, w, out_t, gate_t=None, add_t=None):
    K, T = act_t.shape
    cols = w.shape[1]
    kc = K // P
    W = 2 * P
    steps = cols // W
    assert cols % W == 0
    pieces = [(a, min(BANK, T - a)) for a in range(0, T, BANK)]
    nb = len(pieces)
    act_pieces = [] if gate_t is not None else pieces[: nb // 2]
    dve_pieces = pieces if gate_t is not None else pieces[nb // 2:]
    w_v = w.rearrange("(k p) n -> p k n", p=P)
    with Phase(nc, name) as ph:
        x = ph.sb("x", [P, kc, T])
        w_buf = ph.sb("w", [P, 2, kc, W])
        o = ph.sb("o", [P, 2, T])
        acc = ph.ps("acc", [P, 2, nb * BANK])
        x_in = ph.sem("x_in")
        w_in = [ph.sem("w_in0"), ph.sem("w_in1")]
        w_used = ph.sem("w_used")
        acc_ready = ph.sem("acc_ready")
        o_act = ph.sem("o_act")
        o_dve = ph.sem("o_dve")
        stored = [ph.sem("stored0"), ph.sem("stored1")]
        if gate_t is not None:
            gate = ph.sb("gate", [P, 2, T])
            sig = ph.sb("sig", [P, 2, T])
            gate_in = [ph.sem("gate_in0"), ph.sem("gate_in1")]
            sig_done = ph.sem("sig_done")
        if add_t is not None:
            add = ph.sb("add", [P, 2, T])
            add_in = [ph.sem("add_in0"), ph.sem("add_in1")]
        with nc.Block() as block:

            @block.sync
            def _(sp):
                for c in range(kc):
                    sp.dma_start(x[:, c, :], act_t[c * P:(c + 1) * P, :]).then_inc(x_in, 16)
                with sp.Fori(0, steps // 2) as i:
                    for half in range(2):
                        sp.wait_ge(w_used, i * 2 + half + 1)
                        sp.dma_start(w_buf[:, half], w_v[:, :, bass.ds(i * (2 * W) + half * W, W)]).then_inc(w_in[half], 16)
                if steps % 2:
                    sp.wait_ge(w_used, steps)
                    sp.dma_start(w_buf[:, 0], w_v[:, :, (steps - 1) * W:steps * W]).then_inc(w_in[0], 16)

            @block.tensor
            def _(pe):
                pe.sem_inc(w_used, 2)
                pe.wait_ge(x_in, 16 * kc)

                def step(i, j, half):
                    pe.wait_ge(w_in[half], i * 16 + 16)
                    for c in range(2):
                        b = j * 2 + c
                        pe.wait_ge(o_act, b + 1)
                        pe.wait_ge(o_dve, b + 1)
                        for a, m in pieces:
                            for kk in range(kc):
                                last = pe.matmul(acc[:, c, a:a + m], w_buf[:, half, kk, c * P:(c + 1) * P], x[:, kk, a:a + m],
                                                 start=(kk == 0), stop=(kk == kc - 1))
                        last.then_inc(acc_ready, 1)
                    pe.wait_ge(acc_ready, j * 2 + 2)
                    pe.sem_inc(w_used, 1)

                with pe.Fori(0, steps // 2) as i:
                    for half in range(2):
                        step(i, i * 2 + half, half)
                if steps % 2:
                    step(steps // 2, steps - 1, 0)

            @block.scalar
            def _(act):
                act.sem_inc(o_act, 2)
                for c in range(2):
                    act.sem_inc(stored[c], 16)

                with act.Fori(0, steps) as j:
                    for c in range(2):
                        b = j * 2 + c
                        if gate_t is not None:
                            act.wait_ge(gate_in[c], j * 16 + 16)
                            act.wait_ge(o_dve, b + 1)
                            act.activation(sig[:, c, :], gate[:, c, :], ACT.Sigmoid).then_inc(sig_done, 1)
                        act.wait_ge(acc_ready, b + 1)
                        act.wait_ge(stored[c], j * 16 + 16)
                        if act_pieces:
                            for a, m in act_pieces:
                                last = act.copy(o[:, c, a:a + m], acc[:, c, a:a + m])
                            last.then_inc(o_act, 1)
                        else:
                            act.sem_inc(o_act, 1)
                        act.wait_ge(o_act, b + 3)
                        act.wait_ge(o_dve, b + 3)
                        act.dma_start(out_t[bass.ds(b * P, P), :], o[:, c, :]).then_inc(stored[c], 16)
                for c in range(2):
                    act.wait_ge(stored[c], 16 * steps + 16)

            @block.vector
            def _(dve):
                dve.sem_inc(o_dve, 2)
                with dve.Fori(0, steps) as j:
                    for c in range(2):
                        b = j * 2 + c
                        dve.wait_ge(acc_ready, b + 1)
                        dve.wait_ge(stored[c], j * 16 + 16)
                        if gate_t is not None:
                            dve.wait_ge(sig_done, b + 1)
                            if add_t is not None:
                                dve.wait_ge(add_in[c], j * 16 + 16)
                                for a, m in pieces:
                                    dve.tensor_tensor(o[:, c, a:a + m], acc[:, c, a:a + m], sig[:, c, a:a + m], ALU.mult)
                                dve.drain()
                                last = dve.tensor_tensor(o[:, c, :], o[:, c, :], add[:, c, :], ALU.add)
                            else:
                                for a, m in pieces:
                                    last = dve.tensor_tensor(o[:, c, a:a + m], acc[:, c, a:a + m], sig[:, c, a:a + m], ALU.mult)
                        else:
                            for a, m in dve_pieces:
                                last = dve.tensor_copy(o[:, c, a:a + m], acc[:, c, a:a + m])
                        last.then_inc(o_dve, 1)

            if gate_t is not None:

                @block.gpsimd
                def _(pool):
                    with pool.Fori(0, steps) as j:
                        for c in range(2):
                            b = j * 2 + c
                            pool.wait_ge(o_dve, b + 1)
                            pool.dma_start(gate[:, c, :], gate_t[bass.ds(b * P, P), :]).then_inc(gate_in[c], 16)
                            if add_t is not None:
                                pool.dma_start(add[:, c, :], add_t[bass.ds(b * P, P), :]).then_inc(add_in[c], 16)


def gemm_tok(nc, name, act_t, w, out, n0=0, residual=None, gain=None):
    K, T = act_t.shape
    cols = sum(x.shape[1] for x in w)
    kc = K // P
    n = T // P - n0
    pieces = [(a, min(BANK, cols - a)) for a in range(0, cols, BANK)]
    nb = len(pieces)
    act_v = act_t.rearrange("(k p) t -> p k t", p=P)
    with Phase(nc, name) as ph:
        wt = ph.sb("w", [P, kc, cols])
        x = ph.sb("x", [P, 2, kc, P])
        o = ph.sb("o", [P, 2, cols])
        acc = ph.ps("acc", [P, 2, nb * BANK])
        w_in = ph.sem("w_in")
        x_in = [ph.sem("x_in0"), ph.sem("x_in1")]
        acc_ready = ph.sem("acc_ready")
        o_done = ph.sem("o_done")
        stored = [ph.sem("stored0"), ph.sem("stored1")]
        if residual is not None:
            res = ph.sb("res", [P, 2, cols])
            gn = ph.sb("gn", [P, cols])
            tmp = ph.sb("tmp", [P, cols])
            res_in = [ph.sem("res_in0"), ph.sem("res_in1")]
            gn_in = ph.sem("gn_in")
        with nc.Block() as block:

            @block.sync
            def _(sp):
                if residual is not None:
                    sp.dma_start(gn[:, :], on_all(gain)).then_inc(gn_in, 16)
                at = 0
                for x_w in w:
                    sp.dma_start(wt[:, :, at:at + x_w.shape[1]], x_w.rearrange("(k p) n -> p k n", p=P)).then_inc(w_in, 16)
                    at += x_w.shape[1]
                with sp.Fori(0, n // 2) as i:
                    for half in range(2):
                        t = i * 2 + half
                        sp.wait_ge(o_done, t + 1)
                        sp.dma_start(x[:, half], act_v[:, :, bass.ds((t + n0) * P, P)]).then_inc(x_in[half], 16)
                        if residual is not None:
                            sp.dma_start(res[:, half, :], residual[bass.ds(t * P, P), :]).then_inc(res_in[half], 16)

            @block.tensor
            def _(pe):
                pe.wait_ge(w_in, 16 * len(w))
                with pe.Fori(0, n // 2) as i:
                    for half in range(2):
                        t = i * 2 + half
                        pe.wait_ge(x_in[half], i * 16 + 16)
                        for a, m in pieces:
                            for kk in range(kc):
                                last = pe.matmul(acc[:, half, a:a + m], x[:, half, kk, :], wt[:, kk, a:a + m],
                                                 start=(kk == 0), stop=(kk == kc - 1))
                        last.then_inc(acc_ready, 1)

            @block.vector
            def _(dve):
                dve.sem_inc(o_done, 2)
                for half in range(2):
                    dve.sem_inc(stored[half], 16)
                if residual is not None:
                    dve.wait_ge(gn_in, 16)
                with dve.Fori(0, n // 2) as i:
                    for half in range(2):
                        t = i * 2 + half
                        dve.wait_ge(acc_ready, t + 1)
                        dve.wait_ge(stored[half], i * 16 + 16)
                        if residual is not None:
                            dve.wait_ge(res_in[half], i * 16 + 16)
                            dve.sem_inc(ph.passed, 1)
                            dve.drain()
                            for a, m in pieces:
                                dve.tensor_tensor(tmp[:, a:a + m], acc[:, half, a:a + m], gn[:, a:a + m], ALU.mult)
                            dve.drain()
                            last = dve.tensor_tensor(o[:, half, :], tmp[:, :], res[:, half, :], ALU.add)
                        else:
                            for a, m in pieces:
                                last = dve.tensor_copy(o[:, half, a:a + m], acc[:, half, a:a + m])
                        last.then_inc(o_done, 1)

            @block.scalar
            def _(act):
                with act.Fori(0, n // 2) as i:
                    for half in range(2):
                        t = i * 2 + half
                        act.wait_ge(o_done, t + 3)
                        act.dma_start(out[bass.ds(t * P, P), :], o[:, half, :]).then_inc(stored[half], 16)
                for half in range(2):
                    act.wait_ge(stored[half], 16 * (n // 2) + 16)


LAM_INIT = 0.8 - 0.6
DA_D = 64
QT = SEQ // P
KT1 = T1 // P


def pipelined(eng, n, first, second):
    first(0, 0)
    with eng.Fori(0, (n - 2) // 2) as i:
        for half in range(2):
            first(i * 2 + half + 1, 1 - half)
            second(i * 2 + half, half)
    first(n - 1, 1)
    second(n - 2, 0)
    second(n - 1, 1)


def diff_attention(nc, name, k, p_t, v, lam, rope_cos, rope_sin, o_da):
    H = HEADS1
    N = H * QT
    SC = DA_D ** -0.5
    LAT = T1 - CTX
    S_PIECES = [(a, min(BANK, T1 - a)) for a in range(0, T1, BANK)]
    GROUPS = [(0, 4), (4, 8), (8, 10)]
    with Phase(nc, name) as ph:
        q = ph.sb("q", [P, H, SEQ])
        kk = ph.sb("k", [P, H, T1])
        vv = ph.sb("v", [P, KT1, H * P])
        cos = ph.sb("cos", [P, SEQ])
        sin = ph.sb("sin", [P, SEQ])
        rot = ph.sb("rot", [P, SEQ])
        lv = ph.sb("lv", [P, 4, DA_D])
        lp = ph.sb("lp", [P, 2, DA_D])
        ls = ph.sb("ls", [P, 2])
        le = ph.sb("le", [P, 2])
        neglam = ph.sb("neglam", [P, 1])
        qz = ph.sb("qz", [P, 2, 2, P])
        p = ph.sb("p", [P, 2, T1])
        a = ph.sb("a", [P, 2, T1])
        a_t = ph.sb("a_t", [P, KT1, P])
        mx = ph.sb("mx", [P, 2, 2])
        nm = ph.sb("nm", [P, 2, 2])
        l = ph.sb("l", [P, 2, 2])
        rl = ph.sb("rl", [P, 2, 2])
        c = ph.sb("c", [P, 2])
        o_all = ph.sb("o_all", [P, N, P])
        S = [ph.ps("S0", [P, 3 * BANK]), ph.ps("S1", [P, 3 * BANK])]
        turned = ph.ps("turned", [P, BANK])
        O = ph.ps("O", [P, BANK])
        loaded = ph.sem("loaded")
        rot_ready = ph.sem("rot_ready")
        rope_done = ph.sem("rope_done")
        lam_sums = ph.sem("lam_sums")
        lam_exp = ph.sem("lam_exp")
        zeroed = ph.sem("zeroed")
        qz_ready = ph.sem("qz_ready")
        S_ready = [ph.sem("S0_ready"), ph.sem("S1_ready")]
        max_done = [ph.sem("max0_done"), ph.sem("max1_done")]
        exp_done = [ph.sem("exp0_done"), ph.sem("exp1_done")]
        a_done = ph.sem("a_done")
        turned_ready = ph.sem("turned_ready")
        a_t_done = ph.sem("a_t_done")
        O_ready = ph.sem("O_ready")
        O_used = ph.sem("O_used")
        stored = ph.sem("stored")
        with nc.Block() as block:

            @block.sync
            def _(sp):
                sp.dma_start(cos[:, :], rope_cos).then_inc(loaded, 16)
                sp.dma_start(sin[:, :], rope_sin).then_inc(loaded, 16)
                for i, row in enumerate(lam):
                    sp.dma_start(lv[:, i, :], on_all(row)).then_inc(loaded, 16)
                sp.dma_start(q[:, :, :], p_t[0:H * P, CTX:T1].rearrange("(h p) t -> p h t", p=P)).then_inc(loaded, 16)
                sp.dma_start(kk[:, :, :], p_t[H * P:2 * H * P, :].rearrange("(h p) t -> p h t", p=P)).then_inc(loaded, 16)
                sp.dma_start(vv[:, :, :], v.rearrange("(t p) e -> p t e", p=P)).then_inc(loaded, 16)
                sp.wait_ge(O_used, N + 1)
                o_v = o_da.rearrange("(t p) (h e) -> h p t e", p=P, e=P)
                for h in range(H):
                    sp.dma_start(o_v[h], o_all[:, h * QT:(h + 1) * QT, :]).then_inc(stored, 16)
                sp.wait_ge(stored, 16 * H)

            @block.gpsimd
            def _(pool):
                pool.memset(qz[64:128, :, 0, :], 0.0)
                pool.memset(qz[0:64, :, 1, :], 0.0).then_inc(zeroed, 1)
                pool.wait_ge(zeroed, 1)
                pool.wait_ge(rope_done, 2 * H)
                with pool.Fori(0, N // 2) as i:
                    for half in range(2):
                        pool.wait_ge(S_ready[1], i * 2 + half + 1)
                        at = bass.ds(i * (2 * P) + half * P, P)
                        q_flat = q[:, :, :].rearrange("p h t -> p (h t)")
                        pool.tensor_copy(qz[0:64, half, 0, :], q_flat[0:64, at])
                        pool.tensor_copy(qz[64:128, half, 1, :], q_flat[64:128, at]).then_inc(qz_ready, 1)

            @block.tensor
            def _(pe):
                pe.wait_ge(loaded, 16 * 9)
                for j in range(2 * H):
                    if j >= 1:
                        pe.wait_ge(rope_done, j)
                    src = q[:, j // 2, :] if j % 2 == 0 else kk[:, j // 2, CTX:T1]
                    for b in range(SEQ // BANK):
                        last = pe.matmul(S[0][:, b * BANK:(b + 1) * BANK], k.rope_swap[:, :], src[:, b * BANK:(b + 1) * BANK],
                                         start=True, stop=True)
                    last.then_inc(rot_ready, 1)
                pe.sem_inc(S_ready[1], 2)
                pe.wait_ge(rope_done, 2 * H)
                k_flat = kk[:, :, :].rearrange("p h t -> p (h t)")
                v_flat = vv[:, :, :].rearrange("p t e -> p (t e)")

                def scores(s, par):
                    pe.wait_ge(qz_ready, s + 1)
                    h = s // QT
                    for i in range(2):
                        pe.wait_ge(exp_done[i], s + 1)
                        for at, m in S_PIECES:
                            last = pe.matmul(S[i][:, at:at + m], qz[:, par, i, :], k_flat[:, bass.ds(h * T1 + at, m)],
                                             start=True, stop=True)
                        last.then_inc(S_ready[i], 1)

                def values(s, par):
                    h = s // QT
                    pe.wait_ge(a_done, s + 1)

                    def turn(g):
                        lo, hi = GROUPS[g]
                        pe.wait_ge(a_t_done, s * 3 + g + 1)
                        for b in range(lo, hi):
                            last = pe.transpose(turned[:, (b - lo) * P:(b - lo + 1) * P], a[:, par, b * P:(b + 1) * P], k.ident[:, :])
                        last.then_inc(turned_ready, 1)

                    def product(g):
                        lo, hi = GROUPS[g]
                        pe.wait_ge(a_t_done, s * 3 + g + 2)
                        for b in range(lo, hi):
                            last = pe.matmul(O[:, 0:P], a_t[:, b, :], v_flat[:, bass.ds(h * P + b * (H * P), P)],
                                             start=(b == 0), stop=(b == KT1 - 1))
                        if g == 2:
                            last.then_inc(O_ready, 1)
                    turn(0)
                    turn(1)
                    pe.wait_ge(O_used, s + 1)
                    product(0)
                    turn(2)
                    product(1)
                    product(2)
                pipelined(pe, N, scores, values)

            @block.vector
            def _(dve):
                dve.wait_ge(loaded, 16 * 9)
                for i in range(2):
                    dve.tensor_tensor(lp[:, i, :], lv[:, 2 * i, :], lv[:, 2 * i + 1, :], ALU.mult)
                dve.drain()
                for i in range(2):
                    last = dve.reduce_sum(ls[:, i:i + 1], lp[:, i, :], axis=AX.X)
                last.then_inc(lam_sums, 1)
                for j in range(2 * H):
                    src = q[:, j // 2, :] if j % 2 == 0 else kk[:, j // 2, CTX:T1]
                    dve.wait_ge(rot_ready, j + 1)
                    dve.drain()
                    for b in range(SEQ // BANK):
                        cc = slice(b * BANK, (b + 1) * BANK)
                        dve.tensor_tensor(rot[:, cc], S[0][:, cc], sin[:, cc], ALU.mult)
                    dve.tensor_tensor(src, src, cos[:, :], ALU.mult)
                    dve.drain()
                    dve.tensor_tensor(src, src, rot[:, :], ALU.add).then_inc(rope_done, 1)
                dve.wait_ge(lam_exp, 1)
                dve.scalar_tensor_tensor(neglam[:, :], le[:, 1:2], -LAM_INIT, le[:, 0:1], ALU.add, ALU.subtract)
                dve.drain()
                dve.sem_inc(O_used, 1)

                def maxima(s, par):
                    for i in range(2):
                        dve.wait_ge(S_ready[i], s + 1 + 2 * i)
                        dve.reduce_max(mx[:, par, i:i + 1], S[i][:, 0:T1], axis=AX.X)
                        dve.drain()
                        dve.tensor_scalar(nm[:, par, i:i + 1], mx[:, par, i:i + 1], -SC, None, ALU.mult).then_inc(max_done[i], 1)

                def combine(s, par):
                    dve.wait_ge(exp_done[0], s + 2)
                    dve.wait_ge(exp_done[1], s + 2)
                    dve.reciprocal(rl[:, par, :], l[:, par, :])
                    dve.drain()
                    dve.scalar_tensor_tensor(c[:, par:par + 1], l[:, par, 0:1], neglam[:, :], rl[:, par, 1:2], ALU.mult, ALU.mult)
                    dve.drain()
                    dve.scalar_tensor_tensor(a[:, par, :], p[:, 1, :], c[:, par:par + 1], p[:, 0, :], ALU.mult, ALU.add).then_inc(a_done, 1)

                def first(s, par):
                    maxima(s, par)
                    combine(s, par)

                def second(s, par):
                    dve.wait_ge(O_ready, s + 1)
                    dve.tensor_scalar(o_all[:, :, :].rearrange("p n e -> p (n e)")[:, bass.ds(s * P, P)], O[:, 0:P],
                                      rl[:, par, 0:1], None, ALU.mult).then_inc(O_used, 1)
                pipelined(dve, N, first, second)

            @block.scalar
            def _(act):
                act.wait_ge(lam_sums, 1)
                act.activation(le[:, :], ls[:, :], ACT.Exp).then_inc(lam_exp, 1)
                act.sem_inc(exp_done[0], 1)
                act.sem_inc(exp_done[1], 1)
                act.sem_inc(a_t_done, 1)

                def exp(s, par, i):
                    act.wait_ge(max_done[i], s + 1)
                    if i == 0:
                        act.wait_ge(a_done, s) if not (isinstance(s, int) and s == 0) else None
                    act.activation(p[:, i, :], S[i][:, 0:T1], ACT.Exp, bias=nm[:, par, i:i + 1], scale=SC,
                                   accum_out=l[:, par, i:i + 1]).then_inc(exp_done[i], 1)

                def copies(s):
                    for g, (lo, hi) in enumerate(GROUPS):
                        act.wait_ge(turned_ready, s * 3 + g + 1)
                        if g == 0 and not (isinstance(s, int) and s == 0):
                            act.wait_ge(O_ready, s)
                        act.copy(a_t[:, lo:hi, :], turned[:, 0:(hi - lo) * P].rearrange("p (b q) -> p b q", q=P)).then_inc(a_t_done, 1)
                exp(0, 0, 0)
                exp(0, 0, 1)

                def step(s, par):
                    exp(s + 1, 1 - par, 0)
                    copies(s)
                    exp(s + 1, 1 - par, 1)
                step(0, 0)
                with act.Fori(0, (N - 2) // 2) as i:
                    step(i * 2 + 1, 1)
                    step(i * 2 + 2, 0)
                copies(N - 1)


H2 = 4
NCB = 12
GQ = H2 * P


def short_conv_l2(nc, name, k, x_t, conv_w, out_t):
    PADC = CTX + 2
    LEN = PADC + SEQ + 2
    PIECES = [(a, min(BANK, T1 - a)) for a in range(0, T1, BANK)]
    NORM = 2 * H2
    with Phase(nc, name) as ph:
        w = ph.sb("w", [P, 3, NCB])
        x = ph.sb("x", [P, 2, LEN])
        y = ph.sb("y", [P, 2, LEN])
        act_all = ph.sb("act_all", [P, NCB, T1])
        sq = ph.sb("sq", [P, 2, T1])
        root = ph.sb("root", [P, 2, T1])
        eps = ph.sb("eps", [P, 1])
        sums = ph.ps("sums", [P, 2, 4 * BANK])
        w_in = ph.sem("w_in")
        x_in = [ph.sem("x_in0"), ph.sem("x_in1")]
        padded = ph.sem("padded")
        y_done = ph.sem("y_done")
        silu_done = ph.sem("silu_done")
        sq_done = ph.sem("sq_done")
        sums_ready = ph.sem("sums_ready")
        root_done = ph.sem("root_done")
        unit_done = ph.sem("unit_done")
        stored = ph.sem("stored")
        with nc.Block() as block:

            @block.sync
            def _(sp):
                for i in range(3):
                    sp.dma_start(w[:, i, :], columns(conv_w[i]), allow_slow_non_contiguous=True).then_inc(w_in, 16)
                sp.wait_ge(padded, 1)
                with sp.Fori(0, NCB // 2) as i:
                    for half in range(2):
                        j = i * 2 + half
                        sp.wait_ge(y_done, j + 1)
                        rows = x_t[bass.ds(j * P, P), :]
                        sp.dma_start(x[:, half, 1:1 + CTX], rows[:, 0:CTX]).then_inc(x_in[half], 16)
                        sp.dma_start(x[:, half, PADC + 1:PADC + 1 + SEQ], rows[:, CTX:T1]).then_inc(x_in[half], 16)
                with sp.Fori(0, NORM) as j:
                    sp.wait_ge(unit_done, j + 3)
                    sp.dma_start(out_t[bass.ds(j * P, P), :], act_all[:, bass.ds(j, 1), :].rearrange("p a t -> p (a t)")).then_inc(stored, 16)
                sp.dma_start(out_t[NORM * P:NCB * P, :].rearrange("(c p) t -> p c t", p=P), act_all[:, NORM:NCB, :]).then_inc(stored, 16)
                sp.wait_ge(stored, 16 * (NORM + 1))

            @block.vector
            def _(dve):
                for half in range(2):
                    dve.memset(x[:, half, :], 0.0)
                dve.memset(eps[:, :], EPS)
                dve.drain().then_inc(padded, 1)
                dve.sem_inc(y_done, 2)
                dve.wait_ge(w_in, 48)
                with dve.Fori(0, NCB // 2) as i:
                    for half in range(2):
                        j = i * 2 + half
                        n = LEN - 2
                        tap = [w[:, m, bass.ds(j, 1)] for m in range(3)]
                        out = y[:, half, 1:1 + n]
                        dve.wait_ge(x_in[half], i * 32 + 32)
                        dve.wait_ge(silu_done, j + 1)
                        dve.tensor_scalar(out, x[:, half, 0:n], tap[0], None, ALU.mult)
                        dve.drain()
                        dve.scalar_tensor_tensor(out, x[:, half, 1:1 + n], tap[1], out, ALU.mult, ALU.add)
                        dve.drain()
                        dve.scalar_tensor_tensor(out, x[:, half, 2:2 + n], tap[2], out, ALU.mult, ALU.add).then_inc(y_done, 1)
                dve.sem_inc(unit_done, 2)
                for lo, scale in ((0, float(P) ** -0.5), (H2, 1.0)):
                    with dve.Fori(0, H2 // 2) as i:
                        for half in range(2):
                            j = i * 2 + half + lo
                            dve.wait_ge(root_done, j + 3)
                            dve.reciprocal(root[:, half, :], root[:, half, :])
                            dve.drain()
                            blk = act_all[:, bass.ds(j, 1), :].rearrange("p a t -> p (a t)")
                            dve.scalar_tensor_tensor(blk, blk, scale, root[:, half, :], ALU.mult, ALU.mult).then_inc(unit_done, 1)

            @block.scalar
            def _(act):
                act.sem_inc(silu_done, 2)
                with act.Fori(0, NCB // 2) as i:
                    for half in range(2):
                        j = i * 2 + half
                        act.wait_ge(y_done, j + 3)
                        blk = act_all[:, bass.ds(j, 1), :].rearrange("p a t -> p (a t)")
                        act.activation(blk[:, 0:CTX], y[:, half, 1:1 + CTX], ACT.Silu)
                        act.activation(blk[:, CTX:T1], y[:, half, PADC + 1:PADC + 1 + SEQ], ACT.Silu).then_inc(silu_done, 1)
                with act.Fori(0, NORM // 2) as i:
                    for half in range(2):
                        j = i * 2 + half
                        act.wait_ge(sums_ready, j + 1)
                        act.wait_ge(unit_done, j + 1)
                        act.activation(root[:, half, :], sums[:, half, 0:T1], ACT.Sqrt, bias=eps[:, 0:1]).then_inc(root_done, 1)

            @block.gpsimd
            def _(pool):
                with pool.Fori(0, NORM // 2) as i:
                    for half in range(2):
                        j = i * 2 + half
                        blk = act_all[:, bass.ds(j, 1), :].rearrange("p a t -> p (a t)")
                        pool.wait_ge(silu_done, j + 3)
                        pool.wait_ge(root_done, j + 1)
                        pool.tensor_tensor(sq[:, half, :], blk, blk, ALU.mult).then_inc(sq_done, 1)

            @block.tensor
            def _(pe):
                pe.sem_inc(root_done, 2)
                with pe.Fori(0, NORM // 2) as i:
                    for half in range(2):
                        j = i * 2 + half
                        pe.wait_ge(sq_done, j + 1)
                        pe.wait_ge(unit_done, j + 1)
                        for a, m in PIECES:
                            last = pe.matmul(sums[:, half, a:a + m], k.ones[:, :], sq[:, half, a:a + m], start=True, stop=True)
                        last.then_inc(sums_ready, 1)



def delta_rule(nc, name, k, g_t, gv, a_log, dt_bias, masks, o_dir):
    NT = T1 // P
    NC = CTX // P
    HW = H2 * P
    DH = 2 * H2
    LV = 7
    with Phase(nc, name) as ph:
        mask = ph.sb("mask", [P, 2, LV * P])
        raw = ph.sb("raw", [P, NT, 2 * DH])
        par = ph.sb("par", [P, 2, DH])
        ea = ph.sb("ea", [P, DH])
        gg = ph.sb("g", [P, NT, DH])
        beta = ph.sb("beta", [P, NT, DH])
        t1 = ph.sb("t1", [P, NT, DH])
        t2 = ph.sb("t2", [P, NT, DH])
        t3 = ph.sb("t3", [P, NT, DH])
        G = ph.sb("G", [P, NT, DH])
        L = ph.sb("L", [P, NT, DH])
        beG = ph.sb("beG", [P, NT, DH])
        kdec = ph.sb("kdec", [P, NT, DH])
        eL = ph.sb("eL", [P, NT, DH])
        B = [[ph.ps(f"b{d}{i}", [P, BANK]) for i in range(4)] for d in range(2)]
        W = []
        for d in range(2):
            W.append({n: ph.sb(f"{n}{d}", [P, HW]) for n in
                      ("gb", "bb", "D", "dec", "eGr", "dm", "Nt", "AQ", "qd", "T", "Tt", "U", "kt", "kbg", "kd", "vt",
                       "vb", "Wt", "u", "o", "S")})
            W[d]["x"] = ph.sb(f"x{d}", [P, NCB, P])
            W[d]["Em"] = ph.sb(f"Em{d}", [P, LV, HW])
        ins_in = ph.sem("ins_in")
        zeroed = ph.sem("zeroed")
        soft = ph.sem("soft")
        gates = ph.sem("gates")
        sums = ph.sem("sums")
        exps = ph.sem("exps")
        vecs = ph.sem("vecs")

        def both(n):
            return [ph.sem(f"{n}{d}") for d in range(2)]
        x_in, bcast, rows, gram, eG, dec = (both(n) for n in ("x_in", "bcast", "rows", "gram", "eG", "dec"))
        D_done, made, kt_ready, kt_copied, vt_ready, vt_copied = (
            both(n) for n in ("D_done", "made", "kt_ready", "kt_copied", "vt_ready", "vt_copied"))
        scaled, em, T_ready, T_copied, U_ready, U_copied = (
            both(n) for n in ("scaled", "em", "T_ready", "T_copied", "U_ready", "U_copied"))
        TET_ready, Tt_done, W_ready, W_copied, u_ready, u_copied = (
            both(n) for n in ("TET_ready", "Tt_done", "W_ready", "W_copied", "u_ready", "u_copied"))
        out_ready, o_copied, S_done, stored = (both(n) for n in ("out_ready", "o_copied", "S_done", "stored"))
        g_v = g_t.rearrange("(c p) t -> p c t", p=P)

        def each_chunk(eng, body):
            for lo, cnt in ((0, NC), (NC, NT - NC)):
                with eng.Fori(0, cnt) as s:
                    body(s + lo, (s + lo, (2 * lo + cnt - 1) - (s + lo)))

        def head(ap, h):
            return ap[:, h * P:(h + 1) * P]

        def heads(ap):
            return ap[:, :].rearrange("p (h m) -> p h m", m=P)

        def of_chunk(ap, t, d):
            return ap[:, bass.ds(t, 1), d * H2:(d + 1) * H2].rearrange("p a h -> p (a h)")
        with nc.Block() as block:

            @block.sync
            def _(sp):
                for d in range(2):
                    sp.dma_start(mask[:, d, :], masks[d]).then_inc(ins_in, 16)
                sp.dma_start(raw[:, :, :], gv.rearrange("(t p) c -> p t c", p=P)).then_inc(ins_in, 16)
                sp.dma_start(par[:, 0, :], on_all(a_log)).then_inc(ins_in, 16)
                sp.dma_start(par[:, 1, :], on_all(dt_bias)).then_inc(ins_in, 16)

                def body(n, tile):
                    for d in range(2):
                        sp.wait_ge(vt_ready[d], n + 1)
                        sp.wait_ge(made[d], n + 1)
                        sp.sem_inc(ph.passed, 1)
                        sp.dma_start(W[d]["x"][:, :, :], g_v[:, :, bass.ds(tile[d] * P, P)]).then_inc(x_in[d], 16)
                each_chunk(sp, body)

            @block.gpsimd
            def _(pool):
                for d in range(2):
                    last = pool.memset(W[d]["S"][:, :], 0.0)
                last.then_inc(zeroed, 1)
                pool.wait_ge(vecs, 1)

                def scale(d, dst, src, by, t):
                    return pool.tensor_tensor(heads(W[d][dst]), heads(W[d][src]),
                                              of_chunk(by, t, d).rearrange("p (h m) -> p h m", m=1).to_broadcast([P, H2, P]), ALU.mult)

                def body(n, tile):
                    for d in range(2):
                        pool.wait_ge(rows[d], n + 1)
                        pool.sem_inc(ph.passed, 1)
                        for dst, src in (("gb", gg), ("bb", beta)):
                            last = pool.tensor_copy(heads(W[d][dst]), of_chunk(src, tile[d], d).rearrange("p (h m) -> p h m", m=1).to_broadcast([P, H2, P]))
                        last.then_inc(bcast[d], 1)
                    for d in range(2):
                        pool.wait_ge(out_ready[d], n + 1)
                        pool.wait_ge(kt_copied[d], n + 1)
                        pool.sem_inc(ph.passed, 1)
                        scale(d, "kbg", "kt", beG, tile[d])
                        scale(d, "kd", "kt", kdec, tile[d])
                        pool.wait_ge(vt_copied[d], n + 1)
                        pool.sem_inc(ph.passed, 1)
                        scale(d, "vb", "vt", beta, tile[d]).then_inc(scaled[d], 1)
                each_chunk(pool, body)

            @block.tensor
            def _(pe):
                pe.wait_ge(gates, 1)
                for d in range(2):
                    pe.matmul(B[d][0][:, 0:NT * H2].rearrange("p (t h) -> p t h", h=H2), k.upto[d], gg[:, :, d * H2:(d + 1) * H2],
                              start=True, stop=True)
                pe.matmul(B[0][1][:, 0:NT * DH], k.ones[:, :], gg[:, :, :].rearrange("p t c -> p (t c)"), start=True, stop=True).then_inc(sums, 1)
                pe.wait_ge(vecs, 1)
                pe.wait_ge(zeroed, 1)
                for d in range(2):
                    for s in (rows, out_ready, vt_ready):
                        pe.sem_inc(s[d], 1)

                def product(bank, lhs, rhs, d, done):
                    for h in range(H2):
                        last = pe.matmul(head(B[d][bank], h), lhs(h), rhs(h), start=True, stop=True)
                    last.then_inc(done, 1)

                def turn(bank, src, d, done):
                    for h in range(H2):
                        last = pe.transpose(head(B[d][bank], h), src(h), k.ident[:, :])
                    last.then_inc(done, 1)

                def body(n, tile):
                    def t(d, name):
                        return lambda h: head(W[d][name], h)

                    def x(d, part):
                        return lambda h: W[d]["x"][:, part * H2 + h, :]
                    for d in range(2):
                        pe.wait_ge(bcast[d], n + 1)
                        pe.wait_ge(o_copied[d], n + 1)
                        for h in range(H2):
                            pe.matmul(head(B[d][0], h), head(W[d]["gb"], h), k.upto[d], start=True, stop=True)
                        product(1, t(d, "bb"), lambda h: k.ident[:, :], d, rows[d])
                    for d in range(2):
                        pe.wait_ge(x_in[d], n * 16 + 16)
                        pe.wait_ge(S_done[d], n + 1)
                        for h in range(H2):
                            pe.matmul(head(B[d][2], h), x(d, 1)(h), x(d, 1)(h), start=True, stop=True)
                        product(3, x(d, 1), x(d, 0), d, gram[d])
                    for d in range(2):
                        pe.wait_ge(eG[d], n + 1)
                        pe.wait_ge(D_done[d], n + 1)
                        turn(0, x(d, 1), d, kt_ready[d])
                    for d in range(2):
                        pe.wait_ge(made[d], n + 2)
                        turn(3, x(d, 2), d, vt_ready[d])
                    for d in range(2):
                        pe.wait_ge(Tt_done[d], n * LV + 1)
                        turn(2, t(d, "Tt"), d, T_ready[d])
                    for lv in range(1, LV):
                        for d in range(2):
                            pe.wait_ge(em[d], n * LV + lv + 1)
                            pe.wait_ge(T_copied[d], n * (LV - 1) + lv)
                            product(1, lambda h: W[d]["Em"][:, lv, h * P:(h + 1) * P], t(d, "T"), d, U_ready[d])
                        for d in range(2):
                            pe.wait_ge(U_copied[d], n * (LV - 1) + lv)
                            product(2, t(d, "U"), t(d, "Tt"), d, TET_ready[d])
                        if lv < LV - 1:
                            for d in range(2):
                                pe.wait_ge(Tt_done[d], n * LV + lv + 1)
                                pe.wait_ge(kt_copied[d], n + 1)
                                turn(0, t(d, "Tt"), d, T_ready[d])
                    for d in range(2):
                        pe.wait_ge(Tt_done[d], n * LV + LV)
                        pe.wait_ge(scaled[d], n + 1)
                        product(1, t(d, "kbg"), t(d, "Tt"), d, W_ready[d])
                    for d in range(2):
                        pe.wait_ge(W_copied[d], n + 1)
                        for h in range(H2):
                            pe.matmul(head(B[d][2], h), head(W[d]["Tt"], h), head(W[d]["vb"], h), start=True, stop=False)
                            last = pe.matmul(head(B[d][2], h), head(W[d]["Wt"], h), head(W[d]["S"], h), start=False, stop=True)
                        last.then_inc(u_ready[d], 1)
                    for d in range(2):
                        pe.wait_ge(u_copied[d], n + 1)
                        pe.wait_ge(T_copied[d], n * (LV - 1) + LV - 1)
                        for h in range(H2):
                            pe.matmul(head(B[d][3], h), head(W[d]["kd"], h), head(W[d]["u"], h), start=True, stop=True)
                        for h in range(H2):
                            pe.matmul(head(B[d][0], h), head(W[d]["qd"], h), head(W[d]["S"], h), start=True, stop=False)
                            last = pe.matmul(head(B[d][0], h), head(W[d]["AQ"], h), head(W[d]["u"], h), start=False, stop=True)
                        last.then_inc(out_ready[d], 1)
                each_chunk(pe, body)

            @block.vector
            def _(dve):
                dve.wait_ge(ins_in, 16 * 5)
                per_chunk = lambda a: a.rearrange("p (t c) -> p t c", t=1).to_broadcast([P, NT, DH])
                dve.tensor_tensor(t1[:, :, :], raw[:, :, 0:DH], per_chunk(par[:, 1, :]), ALU.add)
                dve.drain()
                dve.tensor_scalar(t2[:, :, :], t1[:, :, :], -1.0, None, ALU.mult)
                dve.drain()
                dve.tensor_tensor(t2[:, :, :], t2[:, :, :], t1[:, :, :], ALU.min).then_inc(soft, 1)
                dve.wait_ge(soft, 2)
                dve.tensor_scalar(t1[:, :, :], t1[:, :, :], 0.0, None, ALU.max)
                dve.drain()
                dve.tensor_tensor(t1[:, :, :], t1[:, :, :], t2[:, :, :], ALU.add)
                dve.tensor_scalar(beta[:, :, :], t3[:, :, :], 1.0, None, ALU.add)
                dve.drain()
                dve.reciprocal(beta[:, :, :], beta[:, :, :])
                dve.scalar_tensor_tensor(gg[:, :, :], t1[:, :, :], -1.0, per_chunk(ea[:, :]), ALU.mult, ALU.mult)
                dve.drain().then_inc(gates, 1)
                dve.wait_ge(sums, 1)
                for d in range(2):
                    dve.tensor_copy(G[:, :, d * H2:(d + 1) * H2], B[d][0][:, 0:NT * H2].rearrange("p (t h) -> p t h", h=H2))
                dve.tensor_copy(L[:, :, :], B[0][1][:, 0:NT * DH].rearrange("p (t c) -> p t c", c=DH))
                dve.drain()
                dve.tensor_tensor(kdec[:, :, :], L[:, :, :], G[:, :, :], ALU.subtract)
                dve.drain().then_inc(exps, 1)
                dve.wait_ge(exps, 2)
                dve.tensor_tensor(beG[:, :, :], beG[:, :, :], beta[:, :, :], ALU.mult)
                dve.drain().then_inc(vecs, 1)
                for d in range(2):
                    for s in (made, S_done):
                        dve.sem_inc(s[d], 1)

                def body(n, tile):
                    for d in range(2):
                        w, b = W[d], B[d]
                        dve.wait_ge(rows[d], n + 2)
                        dve.sem_inc(ph.passed, 1)
                        for h in range(H2):
                            last = dve.tensor_scalar(head(w["D"], h), head(b[0], h), of_chunk(G, tile[d], d)[:, h:h + 1], 0.0,
                                                     ALU.subtract, ALU.min)
                        last.then_inc(D_done[d], 1)
                    for d in range(2):
                        w, b = W[d], B[d]
                        m3 = mask[:, d, :].rearrange("p (l m) -> p l m", m=P)
                        dve.wait_ge(dec[d], n + 1)
                        dve.wait_ge(gram[d], n + 1)
                        dve.tensor_tensor(w["dm"][:, :], w["dec"][:, :], b[1][:, :], ALU.mult)
                        dve.tensor_tensor(w["AQ"][:, :], b[3][:, :], w["dec"][:, :], ALU.mult)
                        dve.tensor_tensor(heads(w["qd"]), w["x"][:, 0:H2, :], heads(w["eGr"]), ALU.mult)
                        dve.drain()
                        dve.tensor_tensor(w["Nt"][:, :], b[2][:, :], w["dm"][:, :], ALU.mult)
                        dve.tensor_tensor(heads(w["AQ"]), heads(w["AQ"]), k.upto[d].rearrange("p (h m) -> p h m", h=1).to_broadcast([P, H2, P]), ALU.mult)
                        dve.drain().then_inc(made[d], 1)
                        for lv in range(LV):
                            dve.tensor_tensor(w["Em"][:, lv, :].rearrange("p (h m) -> p h m", m=P), heads(w["Nt"]),
                                              m3[:, lv:lv + 1, :].to_broadcast([P, H2, P]), ALU.mult).then_inc(em[d], 1)
                            if lv == 0:
                                dve.drain()
                                dve.tensor_tensor(heads(w["Tt"]), k.ident[:, :].rearrange("p (h m) -> p h m", h=1).to_broadcast([P, H2, P]),
                                                  w["Em"][:, 0, :].rearrange("p (h m) -> p h m", m=P), ALU.subtract).then_inc(Tt_done[d], 1)
                    for lv in range(1, LV):
                        for d in range(2):
                            dve.wait_ge(TET_ready[d], n * (LV - 1) + lv)
                            dve.tensor_tensor(W[d]["Tt"][:, :], W[d]["Tt"][:, :], B[d][2][:, :], ALU.subtract).then_inc(Tt_done[d], 1)
                    for d in range(2):
                        dve.wait_ge(u_ready[d], n + 1)
                        dve.tensor_copy(W[d]["u"][:, :], B[d][2][:, :]).then_inc(u_copied[d], 1)
                    for d in range(2):
                        dve.wait_ge(out_ready[d], n + 2)
                        for h in range(H2):
                            last = dve.scalar_tensor_tensor(head(W[d]["S"], h), head(W[d]["S"], h), of_chunk(eL, tile[d], d)[:, h:h + 1],
                                                            head(B[d][3], h), ALU.mult, ALU.add)
                        last.then_inc(S_done[d], 1)
                each_chunk(dve, body)

            @block.scalar
            def _(act):
                act.wait_ge(ins_in, 16 * 5)
                act.wait_ge(soft, 1)
                act.activation(t2[:, :, :], t2[:, :, :], ACT.Exp)
                act.activation(t3[:, :, :], raw[:, :, DH:2 * DH], ACT.Exp, scale=-1.0)
                act.activation(ea[:, :], par[:, 0, :], ACT.Exp)
                act.drain()
                act.activation(t2[:, :, :], t2[:, :, :], ACT.Ln, bias=1.0)
                act.drain().then_inc(soft, 1)
                act.wait_ge(exps, 1)
                act.activation(beG[:, :, :], G[:, :, :], ACT.Exp)
                act.activation(kdec[:, :, :], kdec[:, :, :], ACT.Exp)
                act.activation(eL[:, :, :], L[:, :, :], ACT.Exp)
                act.drain().then_inc(exps, 1)
                for d in range(2):
                    act.sem_inc(o_copied[d], 1)
                    act.sem_inc(stored[d], 16)

                def body(n, tile):
                    for d in range(2):
                        w, b = W[d], B[d]
                        act.wait_ge(D_done[d], n + 1)
                        act.wait_ge(made[d], n + 1)
                        act.activation(w["eGr"][:, :], b[0][:, :], ACT.Exp).then_inc(eG[d], 1)
                        act.activation(w["dec"][:, :], w["D"][:, :], ACT.Exp).then_inc(dec[d], 1)
                    for d in range(2):
                        act.wait_ge(kt_ready[d], n + 1)
                        act.copy(W[d]["kt"][:, :], B[d][0][:, :]).then_inc(kt_copied[d], 1)
                    for d in range(2):
                        act.wait_ge(vt_ready[d], n + 2)
                        act.copy(W[d]["vt"][:, :], B[d][3][:, :]).then_inc(vt_copied[d], 1)
                    for d in range(2):
                        act.wait_ge(T_ready[d], n * (LV - 1) + 1)
                        act.copy(W[d]["T"][:, :], B[d][2][:, :]).then_inc(T_copied[d], 1)
                    for lv in range(1, LV):
                        for d in range(2):
                            act.wait_ge(U_ready[d], n * (LV - 1) + lv)
                            act.copy(W[d]["U"][:, :], B[d][1][:, :]).then_inc(U_copied[d], 1)
                        if lv < LV - 1:
                            for d in range(2):
                                act.wait_ge(T_ready[d], n * (LV - 1) + lv + 1)
                                act.copy(W[d]["T"][:, :], B[d][0][:, :]).then_inc(T_copied[d], 1)
                    for d in range(2):
                        act.wait_ge(W_ready[d], n + 1)
                        act.mul(W[d]["Wt"][:, :], B[d][1][:, :], -1.0).then_inc(W_copied[d], 1)
                    for d in range(2):
                        act.wait_ge(out_ready[d], n + 2)
                        act.wait_ge(stored[d], n * 16 + 16)
                        act.copy(W[d]["o"][:, :], B[d][0][:, :]).then_inc(o_copied[d], 1)
                        act.wait_ge(o_copied[d], n + 2)
                        act.dma_start(o_dir[d][bass.ds(tile[d] * P, P), :], W[d]["o"][:, :]).then_inc(stored[d], 16)
                each_chunk(act, body)
                for d in range(2):
                    act.wait_ge(stored[d], 16 * NT + 16)


N_EXP1 = 16
CAP1 = 2 * SEQ // N_EXP1
NT2 = SEQ // P


def mix_norm(nc, name, k, o_da, o_dir, gate, subln_g, gdn_g, mix_t):
    H = HEADS1 + H2
    HW = H * P
    mix_v = mix_t.rearrange("(h p) t -> p h t", p=P)
    with Phase(nc, name) as ph:
        y = ph.sb("y", [P, 2, H, P])
        back = ph.sb("back", [P, 2, H2 * P])
        gt = ph.sb("gt", [P, 2, H2 * P])
        sg = ph.sb("sg", [P, 2, H2 * P])
        sq = ph.sb("sq", [P, H, P])
        ss = ph.sb("ss", [P, 2, H])
        ms = ph.sb("ms", [P, 2, H])
        rstd = ph.sb("rstd", [P, 2, H])
        g = ph.sb("g", [P, 2, P])
        ht = ph.sb("ht", [P, 2, H, P])
        turned = ph.ps("turned", [P, 2, HW])
        g_in = ph.sem("g_in")
        x_in = [ph.sem("x_in0"), ph.sem("x_in1")]
        silu_done = ph.sem("silu_done")
        ss_done = ph.sem("ss_done")
        ms_done = ph.sem("ms_done")
        rstd_done = ph.sem("rstd_done")
        y_done = ph.sem("y_done")
        turned_ready = ph.sem("turned_ready")
        ht_dve = ph.sem("ht_dve")
        ht_act = ph.sem("ht_act")
        stored = [ph.sem("stored0"), ph.sem("stored1")]
        with nc.Block() as block:

            @block.sync
            def _(sp):
                sp.dma_start(g[:, 0, :], on_all(subln_g)).then_inc(g_in, 16)
                sp.dma_start(g[:, 1, :], on_all(gdn_g)).then_inc(g_in, 16)
                with sp.Fori(0, NT2 // 2) as i:
                    for half in range(2):
                        t = i * 2 + half
                        rows = bass.ds(t * P, P)
                        lat = bass.ds(t * P + CTX, P)
                        sp.wait_ge(turned_ready, t + 1)
                        sp.dma_start(y[:, half, 0:HEADS1, :], o_da[rows, :].rearrange("p (h e) -> p h e", e=P)).then_inc(x_in[half], 16)
                        sp.dma_start(y[:, half, HEADS1:H, :], o_dir[0][lat, :].rearrange("p (h e) -> p h e", e=P)).then_inc(x_in[half], 16)
                        sp.dma_start(back[:, half, :], o_dir[1][lat, :]).then_inc(x_in[half], 16)
                        sp.dma_start(gt[:, half, :], gate[lat, :]).then_inc(x_in[half], 16)

            @block.gpsimd
            def _(pool):
                with pool.Fori(0, NT2 // 2) as i:
                    for half in range(2):
                        t = i * 2 + half
                        pool.wait_ge(ss_done, t + 1)
                        pool.sem_inc(ph.passed, 1)
                        pool.tensor_scalar(ms[:, half, :], ss[:, half, :], 1.0 / P, EPS, ALU.mult, ALU.add).then_inc(ms_done, 1)
                        pool.wait_ge(ms_done, t + 1)
                        pool.tensor_tensor(rstd[:, half, :], ms[:, half, :], k.minus_half[:, :].to_broadcast([P, H]), ALU.pow).then_inc(rstd_done, 1)

            @block.vector
            def _(dve):
                dve.sem_inc(ht_dve, 2)
                for half in range(2):
                    dve.sem_inc(stored[half], 16)
                dve.wait_ge(g_in, 32)
                dve.tensor_scalar(g[:, 0, :], g[:, 0, :], 1.0 - LAM_INIT, None, ALU.mult)
                dve.drain()
                with dve.Fori(0, NT2 // 2) as i:
                    for half in range(2):
                        t = i * 2 + half
                        delta = y[:, half, HEADS1:H, :]
                        dve.wait_ge(x_in[half], i * 64 + 64)
                        dve.tensor_tensor(delta, delta, back[:, half, :].rearrange("p (h e) -> p h e", e=P), ALU.add)
                        dve.drain()
                        dve.tensor_tensor(sq[:, :, :], y[:, half], y[:, half], ALU.mult)
                        dve.drain()
                        dve.reduce_sum(ss[:, half, :], sq[:, :, :], axis=AX.X).then_inc(ss_done, 1)
                        dve.wait_ge(rstd_done, t + 1)
                        dve.tensor_tensor(y[:, half], y[:, half], rstd[:, half, :].rearrange("p (h e) -> p h e", e=1).to_broadcast([P, H, P]), ALU.mult)
                        dve.drain()
                        for part in range(2):
                            yy = y[:, half, part * HEADS1:(part + 1) * HEADS1, :]
                            last = dve.tensor_tensor(yy, yy, g[:, part:part + 1, :].to_broadcast([P, HEADS1, P]), ALU.mult)
                        dve.drain()
                        dve.wait_ge(silu_done, t + 1)
                        dve.tensor_tensor(delta, delta, sg[:, half, :].rearrange("p (h e) -> p h e", e=P), ALU.mult)
                        dve.drain().then_inc(y_done, 1)
                        dve.wait_ge(turned_ready, t + 3)
                        dve.wait_ge(stored[half], i * 16 + 16)
                        dve.tensor_copy(ht[:, half, 0:4, :], turned[:, half, 0:4 * P].rearrange("p (h e) -> p h e", e=P)).then_inc(ht_dve, 1)

            @block.scalar
            def _(act):
                act.sem_inc(ht_act, 2)
                with act.Fori(0, NT2 // 2) as i:
                    for half in range(2):
                        t = i * 2 + half
                        act.wait_ge(x_in[half], i * 64 + 64)
                        act.wait_ge(turned_ready, t + 1)
                        act.activation(sg[:, half, :], gt[:, half, :], ACT.Silu).then_inc(silu_done, 1)
                        act.wait_ge(turned_ready, t + 3)
                        act.wait_ge(stored[half], i * 16 + 16)
                        act.copy(ht[:, half, 4:8, :], turned[:, half, 4 * P:8 * P].rearrange("p (h e) -> p h e", e=P)).then_inc(ht_act, 1)
                        act.wait_ge(ht_act, t + 3)
                        act.wait_ge(ht_dve, t + 3)
                        act.dma_start(mix_v[:, :, bass.ds(t * P, P)], ht[:, half]).then_inc(stored[half], 16)
                for half in range(2):
                    act.wait_ge(stored[half], 16 * (NT2 // 2) + 16)

            @block.tensor
            def _(pe):
                pe.sem_inc(turned_ready, 2)
                with pe.Fori(0, NT2 // 2) as i:
                    for half in range(2):
                        t = i * 2 + half
                        pe.wait_ge(y_done, t + 1)
                        pe.wait_ge(ht_dve, t + 1)
                        pe.wait_ge(ht_act, t + 1)
                        for h in range(H):
                            last = pe.transpose(turned[:, half, h * P:(h + 1) * P], y[:, half, h, :], k.ident[:, :])
                        last.then_inc(turned_ready, 1)


def expert_choice(nc, name, k, h_t, w_router, idx_out, gate_out):
    ROUNDS = CAP1 // 8
    with Phase(nc, name) as ph:
        h = ph.sb("h", [P, KD, SEQ])
        w = ph.sb("w", [P, KD, N_EXP1])
        e = ph.sb("e", [P, NT2, N_EXP1])
        m = ph.sb("m", [P, NT2])
        s = ph.sb("s", [P, NT2])
        aff = ph.sb("aff", [N_EXP1, SEQ])
        top = ph.sb("top", [N_EXP1, CAP1])
        idx = ph.sb("idx", [N_EXP1, CAP1], U32)
        logits = ph.ps("logits", [P, BANK])
        aff_t = ph.ps("aff_t", [N_EXP1, 2 * BANK])
        loaded = ph.sem("loaded")
        logits_ready = ph.sem("logits_ready")
        centred = ph.sem("centred")
        exp_done = ph.sem("exp_done")
        soft_done = ph.sem("soft_done")
        aff_ready = ph.sem("aff_ready")
        chosen = ph.sem("chosen")
        stored = ph.sem("stored")
        with nc.Block() as block:

            @block.sync
            def _(sp):
                sp.dma_start(w[:, :, :], w_router.rearrange("(k p) e -> p k e", p=P)).then_inc(loaded, 16)
                for c in range(KD):
                    sp.dma_start(h[:, c, :], h_t[c * P:(c + 1) * P, :]).then_inc(loaded, 16)
                sp.wait_ge(chosen, 1)
                sp.dma_start(idx_out, idx[:, :]).then_inc(stored, 16)
                sp.dma_start(gate_out, top[:, :]).then_inc(stored, 16)
                sp.wait_ge(stored, 32)

            @block.tensor
            def _(pe):
                pe.wait_ge(loaded, 16 * (KD + 1))
                for t in range(NT2):
                    for c in range(KD):
                        last = pe.matmul(logits[:, t * N_EXP1:(t + 1) * N_EXP1], h[:, c, t * P:(t + 1) * P], w[:, c, :],
                                         start=(c == 0), stop=(c == KD - 1))
                last.then_inc(logits_ready, 1)
                pe.wait_ge(soft_done, 1)
                for t in range(NT2):
                    last = pe.transpose(aff_t[:, t * P:(t + 1) * P], e[:, t, :], k.ident[:, :])
                last.then_inc(aff_ready, 1)

            @block.scalar
            def _(act):
                act.wait_ge(centred, 1)
                act.activation(e[:, :, :], e[:, :, :], ACT.Exp).then_inc(exp_done, 1)

            @block.vector
            def _(dve):
                lg = logits[:, 0:NT2 * N_EXP1].rearrange("p (t e) -> p t e", e=N_EXP1)
                wide = lambda a: a[:, :].rearrange("p (t e) -> p t e", e=1).to_broadcast([P, NT2, N_EXP1])
                dve.wait_ge(logits_ready, 1)
                dve.reduce_max(m[:, :], lg, axis=AX.X)
                dve.drain()
                dve.tensor_tensor(e[:, :, :], lg, wide(m), ALU.subtract).then_inc(centred, 1)
                dve.wait_ge(exp_done, 1)
                dve.reduce_sum(s[:, :], e[:, :, :], axis=AX.X)
                dve.drain()
                dve.reciprocal(s[:, :], s[:, :])
                dve.drain()
                dve.tensor_tensor(e[:, :, :], e[:, :, :], wide(s), ALU.mult).then_inc(soft_done, 1)
                dve.wait_ge(aff_ready, 1)
                for b in range(2):
                    dve.tensor_copy(aff[:, b * BANK:(b + 1) * BANK], aff_t[:, b * BANK:(b + 1) * BANK])
                dve.drain()
                for r in range(ROUNDS):
                    at = slice(8 * r, 8 * r + 8)
                    dve.max(top[:, at], aff[:, :])
                    dve.drain()
                    dve.max_index(idx[:, at], top[:, at], aff[:, :])
                    dve.drain()
                    dve.match_replace(aff[:, :], top[:, at], aff[:, :], -1.0)
                    dve.drain()
                dve.sem_inc(chosen, 1)


def experts(nc, name, k, blocks, tok_of, x_n, g, shift, scale, w_gate, w_up, w_down, expert_of=None, first=0,
            used=None, gates=None, acc=None, rows_out=None):
    FF = w_gate.shape[2]
    FH = FF // BANK
    KF = FF // P
    WC = KD * BANK
    NW = 2 * FH + (KF * D) // WC
    DH_ = (KF * D) // WC
    DC = D // DH_
    wg_v = w_gate.rearrange("e (k p) f -> e p k f", p=P)
    wu_v = w_up.rearrange("e (k p) f -> e p k f", p=P)
    wd_v = w_down.rearrange("e (k p) n -> e p k n", p=P)
    with Phase(nc, name) as ph:
        gain = ph.sb("gain", [P, KD])
        sh = ph.sb("sh", [P, KD])
        sc = ph.sb("sc", [P, KD])
        w = [ph.sb(f"w{i}", [P, WC]) for i in range(NW)]
        ib = ph.sb("idx", [P, 2], U32)
        gb = ph.sb("gates", [P, 2])
        xe = ph.sb("xe", [P, 2, D])
        xt = ph.sb("xt", [P, KD, P])
        sg = ph.sb("sg", [P, BANK])
        hid = ph.sb("hid", [P, FF])
        hid_t = ph.sb("hid_t", [P, KF, P])
        y = ph.sb("y", [P, 2, D])
        tab = ph.sb("tab", [1, 64], I32)
        up_ps = [ph.ps(f"up{i}", [P, 2, BANK]) for i in range(FH)]
        t_hid = ph.ps("t_hid", [P, BANK])
        t_x = ph.ps("t_x", [P, BANK])
        y_ps = ph.ps("y_ps", [P, D])
        vecs_in = ph.sem("vecs_in")
        tab_in = ph.sem("tab_in")
        gain_done = ph.sem("gain_done")
        w_in = [ph.sem(f"w_in{i}") for i in range(NW)]
        w_used = [ph.sem(f"w_used{i}") for i in range(NW)]
        idx_in = [ph.sem("idx_in0"), ph.sem("idx_in1")]
        xe_in = [ph.sem("xe_in0"), ph.sem("xe_in1")]
        x_turned = ph.sem("x_turned")
        xt_done = ph.sem("xt_done")
        silu_done = ph.sem("silu_done")
        hid_done = ph.sem("hid_done")
        hid_turned = ph.sem("hid_turned")
        hid_t_done = ph.sem("hid_t_done")
        y_ready = w_used[NW - 1]
        y_act = ph.sem("y_act")
        y_dve = ph.sem("y_dve")
        stored = ph.sem("stored")
        y_free = ph.sem("y_free")

        def over_blocks(eng, body):
            count = None
            if used is not None:
                eng.wait_ge(tab_in, 16 if expert_of is None else 32)
                count = eng.value_load(tab[0:1, 62:63], min_val=0, max_val=blocks)
            with eng.Fori(0, blocks // 2) as i:
                for par in range(2):
                    b = i * 2 + par
                    if used is None:
                        body(b, i, par)
                    else:
                        with eng.If(b < count):
                            body(b, i, par)

        def over_blocks_ahead(eng, n, ahead, body):
            ahead(0, 0, 0)
            with eng.Fori(0, (n - 2) // 2) as i:
                ahead(i * 2 + 1, i, 1)
                body(i * 2, i, 0)
                ahead(i * 2 + 2, i + 1, 0)
                body(i * 2 + 1, i, 1)
            ahead(n - 1, n // 2 - 1, 1)
            body(n - 2, n // 2 - 1, 0)
            body(n - 1, n // 2 - 1, 1)
        with nc.Block() as block:

            @block.sync
            def _(sp):
                for dst, row in ((gain, g), (sh, shift), (sc, scale)):
                    sp.dma_start(dst[:, :], columns(row), allow_slow_non_contiguous=True).then_inc(vecs_in, 16)

                def body(b, i, par):
                    if expert_of is not None:
                        e = sp.value_load(tab[0:1, bass.ds(b, 1)], min_val=0, max_val=w_gate.shape[0] - 1)
                    else:
                        e = b
                    at = bass.ds(e, 1)

                    def fill(j, src, dst):
                        sp.wait_ge(w_used[j], b + 1)
                        sp.sem_inc(ph.passed, 1)
                        sp.dma_start(dst, src).then_inc(w_in[j], 16)
                    sp.wait_ge(x_turned, 2 * b + 2)
                    sp.sem_inc(ph.passed, 1)
                    sp.wait_ge(y_free, b + 1)
                    sp.sem_inc(ph.passed, 1)
                    if gates is not None:
                        sp.dma_start(gb[:, par:par + 1], gates[bass.ds(b, 1), :].rearrange("a p -> p a"), allow_slow_non_contiguous=True).then_inc(idx_in[par], 16)
                    sp.dma_start(ib[:, par:par + 1], tok_of[bass.ds(b, 1), :].rearrange("a p -> p a"), allow_slow_non_contiguous=True).then_inc(idx_in[par], 16)
                    for f in range(FH):
                        fc = slice(f * BANK, (f + 1) * BANK)
                        for j, src in ((2 * f, wg_v), (2 * f + 1, wu_v)):
                            fill(j, src[at, :, :, fc].rearrange("a p k f -> p (a k) f"), w[j][:, :].rearrange("p (k f) -> p k f", f=BANK))
                    for c in range(DH_):
                        fill(2 * FH + c, wd_v[at, :, :, c * DC:(c + 1) * DC].rearrange("a p k n -> p (a k) n"),
                             w[2 * FH + c][:, :].rearrange("p (k n) -> p k n", n=DC))
                if used is not None or expert_of is not None:
                    if expert_of is not None:
                        sp.dma_start(tab[0:1, 0:blocks], expert_of).then_inc(tab_in, 16)
                        sp.wait_ge(tab_in, 16)
                    if used is not None:
                        sp.dma_start(tab[0:1, 62:63], used).then_inc(tab_in, 16)
                        sp.wait_ge(tab_in, 32)
                over_blocks(sp, body)

            @block.gpsimd
            def _(pool):
                def gather(b, i, par):
                    n_in = 32 if gates is not None else 16
                    pool.wait_ge(idx_in[par], i * n_in + n_in)
                    pool.wait_ge(x_turned, 2 * b + 2)
                    pool.sem_inc(ph.passed, 1)
                    pool.indirect_dma_start(out=xe[:, par, :], out_offset=None, in_=x_n,
                                            in_offset=bass.IndirectOffsetOnAxis(ap=ib[:, par:par + 1], axis=0)).then_inc(xe_in[par], 16)

                def store(b, i, par):
                    pool.wait_ge(y_act, b + 3)
                    pool.wait_ge(y_dve, b + 3)
                    pool.sem_inc(ph.passed, 1)
                    if acc is not None:
                        pool.indirect_dma_start(out=acc, out_offset=bass.IndirectOffsetOnAxis(ap=ib[:, par:par + 1], axis=0),
                                                in_=y[:, par, :], in_offset=None, compute_op=ALU.add).then_inc(stored, 16)
                    else:
                        pool.dma_start(rows_out[bass.ds((b + first) * P, P), :], y[:, par, :]).then_inc(stored, 16)
                    pool.wait_ge(stored, b * 16 + 16)
                    pool.sem_inc(y_free, 1)
                if used is not None:
                    def body(b, i, par):
                        gather(b, i, par)
                        store(b, i, par)
                    over_blocks(pool, body)
                else:
                    over_blocks_ahead(pool, blocks, gather, store)

            @block.tensor
            def _(pe):
                for j in range(NW):
                    pe.sem_inc(w_used[j], 1)
                pe.sem_inc(x_turned, 4)
                pe.sem_inc(hid_turned, FH)
                pe.sem_inc(y_free, 2)

                def turn_x(b, par, c):
                    pe.wait_ge(xt_done, 2 * b + c + 1)
                    for q in range(4 * c, 4 * c + 4):
                        last = pe.transpose(t_x[:, (q - 4 * c) * P:(q - 4 * c + 1) * P], xe[:, par, q * P:(q + 1) * P], k.ident[:, :])
                    last.then_inc(x_turned, 1)

                def turn_hid(b, f):
                    pe.wait_ge(hid_done, FH * b + f + 1 + FH)
                    pe.wait_ge(hid_t_done, FH * b + f + 1)
                    for q in range(4):
                        last = pe.transpose(t_hid[:, q * P:(q + 1) * P], hid[:, (4 * f + q) * P:(4 * f + q + 1) * P], k.ident[:, :])
                    last.then_inc(hid_turned, 1)

                def prepare(b, i, par):
                    pe.wait_ge(xe_in[par], i * 16 + 16)
                    turn_x(b, par, 0)
                    turn_x(b, par, 1)

                def up(b):
                    for f in range(FH):
                        pe.wait_ge(hid_done, FH * b + f + 1)
                        for j in range(2):
                            pe.wait_ge(w_in[2 * f + j], b * 16 + 16)
                            if f == 0 and j == 0:
                                pe.wait_ge(xt_done, 2 * b + 3)
                            for kk in range(KD):
                                last = pe.matmul(up_ps[f][:, j, :], xt[:, kk, :], w[2 * f + j][:, kk * BANK:(kk + 1) * BANK],
                                                 start=(kk == 0), stop=(kk == KD - 1))
                            last.then_inc(w_used[2 * f + j], 1)

                def down(b):
                    pe.wait_ge(y_act, b + 2)
                    pe.wait_ge(y_dve, b + 2)
                    pe.wait_ge(hid_t_done, FH * b + FH + 1)
                    for c in range(DH_):
                        pe.wait_ge(w_in[2 * FH + c], b * 16 + 16)
                        for a in range(0, DC, BANK):
                            for kk in range(KF):
                                last = pe.matmul(y_ps[:, c * DC + a:c * DC + a + BANK], hid_t[:, kk, :],
                                                 w[2 * FH + c][:, kk * DC + a:kk * DC + a + BANK], start=(kk == 0), stop=(kk == KF - 1))
                        last.then_inc(w_used[2 * FH + c], 1)

                if used is not None:
                    def body(b, i, par):
                        prepare(b, i, par)
                        up(b)
                        for f in range(FH):
                            turn_hid(b, f)
                        down(b)
                    over_blocks(pe, body)
                else:
                    def step(b, i, par, more=True):
                        up(b)
                        turn_hid(b, 0)
                        if more:
                            prepare(b + 1, i + par, 1 - par)
                        for f in range(1, FH):
                            turn_hid(b, f)
                        down(b)
                    prepare(0, 0, 0)
                    with pe.Fori(0, blocks // 2 - 1) as i:
                        for par in range(2):
                            step(i * 2 + par, i, par)
                    step(blocks - 2, blocks // 2 - 1, 0)
                    step(blocks - 1, blocks // 2 - 1, 1, more=False)

            @block.scalar
            def _(act):
                act.sem_inc(hid_t_done, 1)
                act.sem_inc(y_act, 2)

                def body(b, i, par):
                    for f in range(FH):
                        act.wait_ge(w_used[2 * f], b + 2)
                        act.wait_ge(hid_done, FH * b + f + FH)
                        act.activation(sg[:, :], up_ps[f][:, 0, :], ACT.Silu).then_inc(silu_done, 1)
                    act.wait_ge(y_ready, b + 1)
                    for f in range(FH):
                        act.wait_ge(hid_turned, FH * b + f + 1 + FH)
                        act.copy(hid_t[:, 4 * f:4 * f + 4, :], t_hid[:, :].rearrange("p (k t) -> p k t", t=P)).then_inc(hid_t_done, 1)
                    act.wait_ge(y_ready, b + 2)
                    act.wait_ge(y_free, b + 1)
                    scale_ = gb[:, par:par + 1] if gates is not None else 1.0
                    act.activation(y[:, par, 0:BANK], y_ps[:, 0:BANK], ACT.Copy, scale=scale_).then_inc(y_act, 1)
                over_blocks(act, body)

            @block.vector
            def _(dve):
                dve.wait_ge(vecs_in, 48)
                dve.scalar_tensor_tensor(gain[:, :], sc[:, :], 1.0, gain[:, :], ALU.add, ALU.mult)
                dve.drain()
                dve.sem_inc(xt_done, 1)
                dve.sem_inc(hid_done, FH)
                dve.sem_inc(y_dve, 2)

                def modulate(b, i, par):
                    dve.wait_ge(w_used[2 * FH - 1], b + 1)
                    for c in range(2):
                        dve.wait_ge(x_turned, 2 * b + c + 5)
                        for q in range(4):
                            kk = 4 * c + q
                            last = dve.tensor_scalar(xt[:, kk, :], t_x[:, q * P:(q + 1) * P], gain[:, kk:kk + 1], sh[:, kk:kk + 1], ALU.mult, ALU.add)
                        last.then_inc(xt_done, 1)

                def products(b):
                    for f in range(FH):
                        dve.wait_ge(silu_done, FH * b + f + 1)
                        dve.wait_ge(w_used[2 * f + 1], b + 2)
                        dve.wait_ge(hid_turned, FH * b + f + 1)
                        dve.tensor_tensor(hid[:, f * BANK:(f + 1) * BANK], up_ps[f][:, 1, :], sg[:, :], ALU.mult).then_inc(hid_done, 1)

                def result(b, i, par):
                    dve.wait_ge(y_ready, b + 2)
                    dve.wait_ge(y_free, b + 1)
                    out = y[:, par, BANK:D]
                    if gates is not None:
                        dve.tensor_scalar(out, y_ps[:, BANK:D], gb[:, par:par + 1], None, ALU.mult).then_inc(y_dve, 1)
                    else:
                        dve.tensor_copy(out, y_ps[:, BANK:D]).then_inc(y_dve, 1)
                if used is not None:
                    def body(b, i, par):
                        modulate(b, i, par)
                        products(b)
                        result(b, i, par)
                    over_blocks(dve, body)
                else:
                    def step(b, i, par, more=True):
                        products(b)
                        if more:
                            modulate(b + 1, i + par, 1 - par)
                        result(b, i, par)
                    modulate(0, 0, 0)
                    with dve.Fori(0, blocks // 2 - 1) as i:
                        for par in range(2):
                            step(i * 2 + par, i, par)
                    step(blocks - 2, blocks // 2 - 1, 0)
                    step(blocks - 1, blocks // 2 - 1, 1, more=False)


def finish(nc, name, k, x1, gain, g, out, acc=None, rows=None, dest=None, gates=None):
    with Phase(nc, name) as ph:
        gn = ph.sb("gain", [P, D])
        gg = ph.sb("g", [P, D])
        x = ph.sb("x", [P, 2, D])
        m = ph.sb("m", [P, 2, D])
        m2 = ph.sb("m2", [P, 2, D])
        sq = ph.sb("sq", [P, D])
        ss = ph.sb("ss", [P, 2])
        ms = ph.sb("ms", [P, 2])
        rstd = ph.sb("rstd", [P, 2])
        o = ph.sb("o", [P, 2, D])
        dst = ph.sb("dest", [P, 2 * NT2], U32)
        gt = ph.sb("gates", [P, 2 * NT2])
        ib = ph.sb("ib", [P, 4], U32)
        rows_in = ph.sem("rows_in")
        x_in = [ph.sem("x_in0"), ph.sem("x_in1")]
        m_in = [ph.sem("m_in0"), ph.sem("m_in1")]
        ib_done = ph.sem("ib_done")
        x_done = ph.sem("x_done")
        sq_done = ph.sem("sq_done")
        ms_done = ph.sem("ms_done")
        rstd_done = ph.sem("rstd_done")
        o_done = ph.sem("o_done")
        stored = [ph.sem("stored0"), ph.sem("stored1")]
        M_IN = 16 if acc is not None else 32
        with nc.Block() as block:

            @block.sync
            def _(sp):
                sp.dma_start(gn[:, :], on_all(gain)).then_inc(rows_in, 16)
                sp.dma_start(gg[:, :], on_all(g)).then_inc(rows_in, 16)
                if acc is None:
                    sp.dma_start(dst[:, :], dest).then_inc(rows_in, 16)
                    sp.dma_start(gt[:, :], gates).then_inc(rows_in, 16)
                with sp.Fori(0, NT2 // 2) as i:
                    for half in range(2):
                        t = i * 2 + half
                        sp.wait_ge(o_done, t + 1)
                        sp.dma_start(x[:, half, :], x1[bass.ds(t * P, P), :]).then_inc(x_in[half], 16)
                        if acc is not None:
                            sp.dma_start(m[:, half, :], acc[bass.ds(t * P, P), :]).then_inc(m_in[half], 16)

            @block.gpsimd
            def _(pool):
                if acc is None:
                    pool.wait_ge(rows_in, 64)

                def gather(t, half):
                    pool.wait_ge(o_done, t + 1)
                    for c in range(2):
                        last = pool.tensor_copy(ib[:, 2 * half + c:2 * half + c + 1], dst[:, bass.ds(t * 2 + c, 1)])
                    last.then_inc(ib_done, 1)
                    pool.wait_ge(ib_done, t + 1)
                    pool.sem_inc(ph.passed, 1)
                    for c, buf in enumerate((m, m2)):
                        pool.indirect_dma_start(out=buf[:, half, :], out_offset=None, in_=rows,
                                                in_offset=bass.IndirectOffsetOnAxis(ap=ib[:, 2 * half + c:2 * half + c + 1], axis=0)).then_inc(m_in[half], 16)
                with pool.Fori(0, NT2 // 2) as i:
                    if acc is None:
                        for half in range(2):
                            gather(i * 2 + half, half)
                    for half in range(2):
                        t = i * 2 + half
                        pool.wait_ge(sq_done, t + 1)
                        pool.sem_inc(ph.passed, 1)
                        pool.tensor_scalar(ms[:, half:half + 1], ss[:, half:half + 1], 1.0 / D, EPS, ALU.mult, ALU.add).then_inc(ms_done, 1)
                        pool.wait_ge(ms_done, t + 1)
                        pool.tensor_tensor(rstd[:, half:half + 1], ms[:, half:half + 1], k.minus_half[:, :], ALU.pow).then_inc(rstd_done, 1)

            @block.scalar
            def _(act):
                with act.Fori(0, NT2 // 2) as i:
                    for half in range(2):
                        t = i * 2 + half
                        act.wait_ge(x_done, t + 1)
                        act.wait_ge(o_done, t + 1)
                        act.activation(sq[:, :], x[:, half, :], ACT.Square, accum_out=ss[:, half:half + 1]).then_inc(sq_done, 1)
                        act.wait_ge(o_done, t + 3)
                        act.dma_start(out[bass.ds(t * P, P), :], o[:, half, :]).then_inc(stored[half], 16)
                for half in range(2):
                    act.wait_ge(stored[half], 16 * (NT2 // 2) + 16)

            @block.vector
            def _(dve):
                dve.sem_inc(o_done, 2)
                for half in range(2):
                    dve.sem_inc(stored[half], 16)
                dve.wait_ge(rows_in, 32 if acc is not None else 64)
                with dve.Fori(0, NT2 // 2) as i:
                    for half in range(2):
                        t = i * 2 + half
                        dve.wait_ge(x_in[half], i * 16 + 16)
                        dve.wait_ge(m_in[half], i * M_IN + M_IN)
                        if acc is None:
                            dve.tensor_scalar(m[:, half, :], m[:, half, :], gt[:, bass.ds(t * 2, 1)], None, ALU.mult)
                            dve.drain()
                            dve.scalar_tensor_tensor(m[:, half, :], m2[:, half, :], gt[:, bass.ds(t * 2 + 1, 1)], m[:, half, :], ALU.mult, ALU.add)
                            dve.drain()
                        dve.tensor_tensor(m[:, half, :], m[:, half, :], gn[:, :], ALU.mult)
                        dve.drain()
                        dve.tensor_tensor(x[:, half, :], x[:, half, :], m[:, half, :], ALU.add).then_inc(x_done, 1)
                        dve.wait_ge(rstd_done, t + 1)
                        dve.wait_ge(stored[half], i * 16 + 16)
                        dve.scalar_tensor_tensor(o[:, half, :], x[:, half, :], rstd[:, half:half + 1], gg[:, :], ALU.mult, ALU.mult).then_inc(o_done, 1)


D_RNN = 1280
RB = D_RNN // P
LRU_C = 8.0
HEADS2 = 8
KV_RANK = 256
IDX_H = 8
IDX_D = 64
TOPK = 256
IDX_SCALE = IDX_D ** -0.5 * IDX_H ** -0.5
ATT_SCALE = float(P) ** -0.5
STRUCK = -3.0e38


def rg_lru(nc, name, k, x_t, gr_t, conv_w, conv_b, w_a, b_a, w_x, b_x, lam, y_t):
    TAPS = conv_w.shape[0]
    PAD = TAPS - 1
    with Phase(nc, name) as ph:
        cw = ph.sb("cw", [P, TAPS, RB])
        vec = {n: ph.sb(n, [P, RB]) for n in ("cb", "ba", "bx", "lam", "e", "hs")}
        x = ph.sb("x", [P, 2, PAD + SEQ])
        xc = ph.sb("xc", [P, 2, SEQ])
        wa = ph.sb("wa", [P, 2, P])
        wx = ph.sb("wx", [P, 2, P])
        tr = ph.sb("tr", [P, 2, SEQ])
        gel = ph.sb("gelu", [P, RB, SEQ])
        a = ph.sb("a", [P, RB, SEQ])
        th = ph.sb("th", [P, RB, SEQ])
        ix = ph.sb("ix", [P, RB, SEQ])
        r_ps = ph.ps("r", [P, 2, SEQ])
        i_ps = ph.ps("i", [P, 2, SEQ])
        vecs_in = ph.sem("vecs_in")
        gr_in = ph.sem("gr_in")
        padded = ph.sem("padded")
        soft = ph.sem("soft")
        x_in = [ph.sem("x_in0"), ph.sem("x_in1")]
        conv_done = ph.sem("conv_done")
        gates_ready = ph.sem("gates_ready")
        tanh_done = ph.sem("tanh_done")
        s_done = ph.sem("s_done")
        ix_done = ph.sem("ix_done")
        a_done = ph.sem("a_done")
        root_done = ph.sem("root_done")
        y_done = ph.sem("y_done")
        stored = ph.sem("stored")

        def blk(ap, j):
            return ap[:, bass.ds(j, 1), :].rearrange("p a t -> p (a t)")
        with nc.Block() as block:

            @block.sync
            def _(sp):
                for i in range(TAPS):
                    sp.dma_start(cw[:, i, :], columns(conv_w[i]), allow_slow_non_contiguous=True).then_inc(vecs_in, 16)
                for n, row in (("cb", conv_b), ("ba", b_a), ("bx", b_x), ("lam", lam)):
                    sp.dma_start(vec[n][:, :], columns(row), allow_slow_non_contiguous=True).then_inc(vecs_in, 16)
                sp.dma_start(gel[:, :, :], gr_t.rearrange("(c p) t -> p c t", p=P)).then_inc(gr_in, 16)
                sp.wait_ge(padded, 1)
                with sp.Fori(0, RB // 2) as i:
                    for par in range(2):
                        j = i * 2 + par
                        sp.wait_ge(ix_done, j + 1)
                        sp.dma_start(x[:, par, PAD:PAD + SEQ], x_t[bass.ds(j * P, P), :]).then_inc(x_in[par], 16)
                        sp.dma_start(wa[:, par, :], w_a[bass.ds(j, 1)].rearrange("a c d -> c (a d)")).then_inc(x_in[par], 16)
                        sp.dma_start(wx[:, par, :], w_x[bass.ds(j, 1)].rearrange("a c d -> c (a d)")).then_inc(x_in[par], 16)
                with sp.Fori(0, RB) as j:
                    sp.wait_ge(y_done, j + 1)
                    sp.dma_start(y_t[bass.ds(j * P, P), :], blk(ix, j)).then_inc(stored, 16)
                sp.wait_ge(stored, 16 * RB)

            @block.vector
            def _(dve):
                for par in range(2):
                    dve.memset(x[:, par, 0:PAD], 0.0)
                dve.drain().then_inc(padded, 1)
                dve.sem_inc(ix_done, 2)
                dve.wait_ge(vecs_in, 16 * (TAPS + 4))
                dve.tensor_scalar(vec["e"][:, :], vec["lam"][:, :], -1.0, None, ALU.mult)
                dve.tensor_scalar(vec["ba"][:, :], vec["ba"][:, :], 0.5, None, ALU.mult)
                dve.tensor_scalar(vec["bx"][:, :], vec["bx"][:, :], 0.5, None, ALU.mult)
                dve.drain()
                dve.tensor_scalar(vec["hs"][:, :], vec["e"][:, :], 0.0, None, ALU.max)
                dve.tensor_tensor(vec["e"][:, :], vec["e"][:, :], vec["lam"][:, :], ALU.min)
                dve.drain().then_inc(soft, 1)
                dve.wait_ge(soft, 2)
                dve.tensor_tensor(vec["hs"][:, :], vec["hs"][:, :], vec["e"][:, :], ALU.add)
                dve.drain()
                dve.tensor_scalar(vec["hs"][:, :], vec["hs"][:, :], LRU_C / 2, None, ALU.mult)
                dve.drain()
                with dve.Fori(0, RB // 2) as i:
                    for par in range(2):
                        j = i * 2 + par
                        tap = [cw[:, m, bass.ds(j, 1)] for m in range(TAPS)]
                        hs = vec["hs"][:, bass.ds(j, 1)]
                        dve.wait_ge(x_in[par], i * 48 + 48)
                        dve.tensor_scalar(xc[:, par, :], x[:, par, 0:SEQ], tap[0], vec["cb"][:, bass.ds(j, 1)], ALU.mult, ALU.add)
                        dve.drain()
                        for m in range(1, TAPS):
                            dve.scalar_tensor_tensor(xc[:, par, :], x[:, par, m:m + SEQ], tap[m], xc[:, par, :], ALU.mult, ALU.add)
                            dve.drain()
                        dve.sem_inc(conv_done, 1)
                        dve.wait_ge(tanh_done, j + 1)
                        dve.tensor_scalar(blk(th, j), tr[:, par, :], hs, hs, ALU.mult, ALU.add).then_inc(s_done, 1)
                        dve.scalar_tensor_tensor(blk(ix, j), blk(ix, j), 1.0, xc[:, par, :], ALU.add, ALU.mult).then_inc(ix_done, 1)
                with dve.Fori(0, RB) as j:
                    dve.wait_ge(root_done, j + 1)
                    dve.scalar_tensor_tensor(blk(th, j), blk(a, j), 1.0, blk(th, j), ALU.add, ALU.mult)
                    dve.drain()
                    dve.scalar_tensor_tensor(blk(ix, j), blk(ix, j), 0.5, blk(th, j), ALU.mult, ALU.mult)
                    dve.drain()
                    dve.tensor_tensor_scan(blk(th, j), blk(a, j), blk(ix, j), 0.0, ALU.mult, ALU.add)
                    dve.drain()
                    dve.tensor_tensor(blk(ix, j), blk(th, j), blk(gel, j), ALU.mult).then_inc(y_done, 1)

            @block.tensor
            def _(pe):
                with pe.Fori(0, RB // 2) as i:
                    for par in range(2):
                        j = i * 2 + par
                        pe.wait_ge(conv_done, j + 1)
                        pe.wait_ge(ix_done, j + 1)
                        for ps, wt in ((r_ps, wa), (i_ps, wx)):
                            for b in range(0, SEQ, BANK):
                                last = pe.matmul(ps[:, par, b:b + BANK], wt[:, par, :], xc[:, par, b:b + BANK], start=True, stop=True)
                        last.then_inc(gates_ready, 1)

            @block.scalar
            def _(act):
                act.wait_ge(gr_in, 16)
                act.activation(gel[:, :, :], gel[:, :, :], ACT.Gelu_apprx_tanh)
                act.wait_ge(soft, 1)
                act.activation(vec["e"][:, :], vec["e"][:, :], ACT.Exp)
                act.drain()
                act.activation(vec["e"][:, :], vec["e"][:, :], ACT.Ln, bias=1.0)
                act.drain().then_inc(soft, 1)
                with act.Fori(0, RB // 2) as i:
                    for par in range(2):
                        j = i * 2 + par
                        act.wait_ge(gates_ready, j + 1)
                        act.activation(tr[:, par, :], r_ps[:, par, :], ACT.Tanh, bias=vec["ba"][:, bass.ds(j, 1)], scale=0.5)
                        act.activation(blk(ix, j), i_ps[:, par, :], ACT.Tanh, bias=vec["bx"][:, bass.ds(j, 1)], scale=0.5).then_inc(tanh_done, 1)
                        act.wait_ge(s_done, j + 1)
                        act.activation(blk(a, j), blk(th, j), ACT.Exp, scale=-1.0)
                        act.drain()
                        act.activation(blk(th, j), blk(th, j), ACT.Tanh, scale=0.5).then_inc(a_done, 1)
                act.wait_ge(a_done, RB)
                with act.Fori(0, RB) as j:
                    act.activation(blk(th, j), blk(th, j), ACT.Sqrt).then_inc(root_done, 1)


def kv_norm(nc, name, k, c_t, g, out_t):
    R = KV_RANK // P
    with Phase(nc, name) as ph:
        c = ph.sb("c", [P, R, SEQ])
        sq = ph.sb("sq", [P, R, SEQ])
        root = ph.sb("root", [P, SEQ])
        gg = ph.sb("g", [P, R])
        eps = ph.sb("eps", [P, 1])
        sums = ph.ps("sums", [P, SEQ])
        loaded = ph.sem("loaded")
        sq_done = ph.sem("sq_done")
        sums_ready = ph.sem("sums_ready")
        root_done = ph.sem("root_done")
        done = ph.sem("done")
        stored = ph.sem("stored")
        with nc.Block() as block:

            @block.sync
            def _(sp):
                sp.dma_start(c[:, :, :], c_t.rearrange("(r p) t -> p r t", p=P)).then_inc(loaded, 16)
                sp.dma_start(gg[:, :], columns(g), allow_slow_non_contiguous=True).then_inc(loaded, 16)
                sp.wait_ge(done, 1)
                sp.dma_start(out_t.rearrange("(r p) t -> p r t", p=P), c[:, :, :]).then_inc(stored, 16)
                sp.wait_ge(stored, 16)

            @block.vector
            def _(dve):
                dve.memset(eps[:, :], EPS)
                dve.wait_ge(loaded, 32)
                dve.tensor_tensor(sq[:, :, :], c[:, :, :], c[:, :, :], ALU.mult)
                dve.drain().then_inc(sq_done, 1)
                dve.wait_ge(root_done, 1)
                dve.reciprocal(root[:, :], root[:, :])
                dve.drain()
                for r in range(R):
                    dve.scalar_tensor_tensor(c[:, r, :], c[:, r, :], gg[:, r:r + 1], root[:, :], ALU.mult, ALU.mult)
                dve.drain().then_inc(done, 1)

            @block.tensor
            def _(pe):
                pe.wait_ge(sq_done, 1)
                for b in range(0, SEQ, BANK):
                    for r in range(R):
                        last = pe.matmul(sums[:, b:b + BANK], k.ones[:, :], sq[:, r, b:b + BANK], start=(r == 0), stop=(r == R - 1))
                last.then_inc(sums_ready, 1)

            @block.scalar
            def _(act):
                act.wait_ge(sums_ready, 1)
                act.activation(root[:, :], sums[:, :], ACT.Sqrt, bias=eps[:, 0:1], scale=1.0 / KV_RANK).then_inc(root_done, 1)


def index_select(nc, name, k, qi_t, kw, dist, causal, dm_out):
    first_sel = TOPK // P
    with Phase(nc, name) as ph:
        kwt = ph.sb("kw", [P, NT2, IDX_D + IDX_H])
        kk2 = ph.sb("kk2", [P, NT2, 2, IDX_D])
        wi = ph.sb("wi", [P, NT2, IDX_H])
        ki = ph.sb("ki", [P, SEQ])
        qi = ph.sb("qi", [P, 2, IDX_H // 2, P])
        dn = ph.sb("dn", [P, SEQ])
        cm = ph.sb("cm", [P, P])
        rel = ph.sb("rel", [P, 2, SEQ])
        score = ph.sb("score", [P, SEQ])
        top = ph.sb("top", [P, 8])
        dm = ph.sb("dm", [P, 2, SEQ])
        S = ph.ps("S", [P, 2, SEQ])
        loaded = ph.sem("loaded")
        q_in = [ph.sem("q_in0"), ph.sem("q_in1")]
        kk2_done = ph.sem("kk2_done")
        ki_turned = ph.sem("ki_turned")
        ki_done = ph.sem("ki_done")
        S_ready = ph.sem("S_ready")
        rel_done = ph.sem("rel_done")
        score_done = ph.sem("score_done")
        dm_done = ph.sem("dm_done")
        stored = [ph.sem("stored0"), ph.sem("stored1")]
        tiles = list(range(first_sel, NT2))
        with nc.Block() as block:

            @block.sync
            def _(sp):
                sp.dma_start(kwt[:, :, :], kw.rearrange("(t p) c -> p t c", p=P)).then_inc(loaded, 16)
                sp.dma_start(dn[:, :], dist).then_inc(loaded, 16)
                sp.dma_start(cm[:, :], causal).then_inc(loaded, 16)

                def load(t):
                    i = t - first_sel
                    sp.dma_start(qi[:, i % 2], qi_t[:, t * P:(t + 1) * P].rearrange("(c p) t -> p c t", p=P)).then_inc(q_in[i % 2], 16)
                for t in tiles[:2]:
                    load(t)
                for t in range(NT2):
                    sp.wait_ge(dm_done, t + 1)
                    W = (t + 1) * P
                    sp.dma_start(dm_out[t * P:(t + 1) * P, 0:W], dm[:, t % 2, 0:W]).then_inc(stored[t % 2], 16)
                    if first_sel <= t < NT2 - 2:
                        load(t + 2)
                for par in range(2):
                    sp.wait_ge(stored[par], 16 * NT2 // 2)

            @block.tensor
            def _(pe):
                pe.wait_ge(kk2_done, 1)
                for t in range(NT2):
                    last = pe.transpose(S[:, 0, t * P:(t + 1) * P], kk2[:, t].rearrange("p a c -> p (a c)"), k.ident[:, :])
                last.then_inc(ki_turned, 1)
                pe.wait_ge(ki_done, 1)
                n = 0
                for i, t in enumerate(tiles):
                    pe.wait_ge(q_in[i % 2], 16 * (i // 2 + 1))
                    W = (t + 1) * P
                    for h in range(IDX_H):
                        rows = slice(IDX_D * (h % 2), IDX_D * (h % 2) + IDX_D)
                        if n >= 2:
                            pe.wait_ge(rel_done, n - 1)
                        for b in range(0, W, BANK):
                            e = min(W, b + BANK)
                            last = pe.matmul(S[:, n % 2, b:e], qi[rows, i % 2, h // 2, :], ki[rows, b:e], start=True, stop=True)
                        last.then_inc(S_ready, 1)
                        n += 1

            @block.scalar
            def _(act):
                act.wait_ge(ki_turned, 1)
                act.copy(ki[:, :], S[:, 0, :]).then_inc(ki_done, 1)
                n = 0
                for i, t in enumerate(tiles):
                    W = (t + 1) * P
                    for h in range(IDX_H):
                        act.wait_ge(S_ready, n + 1)
                        if n >= 2:
                            act.wait_ge(score_done, n - 1)
                        act.activation(rel[:, n % 2, 0:W], S[:, n % 2, 0:W], ACT.Relu).then_inc(rel_done, 1)
                        n += 1

            @block.vector
            def _(dve):
                dve.wait_ge(loaded, 48)
                for c in range(2):
                    dve.tensor_copy(kk2[:, :, c, :], kwt[:, :, 0:IDX_D])
                dve.drain().then_inc(kk2_done, 1)
                dve.tensor_scalar(wi[:, :, :], kwt[:, :, IDX_D:], IDX_SCALE, None, ALU.mult)
                dve.drain()
                n = 0
                for t in range(NT2):
                    W = (t + 1) * P
                    diag = slice(t * P, W)
                    sel = score[:, 0:W]
                    if t >= first_sel:
                        for h in range(IDX_H):
                            dve.wait_ge(rel_done, n + 1)
                            if h == 0:
                                dve.tensor_scalar(sel, rel[:, n % 2, 0:W], wi[:, t, 0:1], None, ALU.mult)
                            else:
                                dve.scalar_tensor_tensor(sel, rel[:, n % 2, 0:W], wi[:, t, h:h + 1], sel, ALU.mult, ALU.add)
                            dve.drain().then_inc(score_done, 1)
                            n += 1
                        dve.tensor_tensor(score[:, diag], score[:, diag], cm[:, :], ALU.add)
                        dve.drain()
                        with dve.Fori(0, TOPK // 8):
                            dve.max(top[:, :], sel)
                            dve.drain()
                            dve.match_replace(sel, top[:, :], sel, STRUCK)
                            dve.drain()
                        dve.tensor_scalar(sel, sel, STRUCK, NEG, ALU.not_equal, ALU.mult)
                        dve.drain()
                    if t >= 2:
                        dve.wait_ge(stored[t % 2], 16 * (t // 2))
                    out = dm[:, t % 2, 0:W]
                    if t >= first_sel:
                        dve.scalar_tensor_tensor(out, dn[:, 0:W], -float(t * P), sel, ALU.add, ALU.add)
                    else:
                        dve.tensor_scalar(out, dn[:, 0:W], -float(t * P), None, ALU.add)
                        dve.drain()
                        dve.tensor_tensor(dm[:, t % 2, diag], dm[:, t % 2, diag], cm[:, :], ALU.add)
                    dve.drain().then_inc(dm_done, 1)


def sparse_attention(nc, name, k, q_t, k_t, v, dm, slopes, att_t):
    H = HEADS2
    with Phase(nc, name) as ph:
        kk = ph.sb("k", [P, H, SEQ])
        vv = ph.sb("v", [P, NT2, H * P])
        sl = ph.sb("sl", [P, H])
        q = ph.sb("q", [P, 2, H, P])
        dmt = ph.sb("dm", [P, 2, SEQ])
        qs = ph.sb("qs", [P, 2, P])
        cs = ph.sb("cs", [P, 2])
        bias = ph.sb("bias", [P, 2, SEQ])
        X = ph.sb("X", [P, 2, SEQ])
        p = ph.sb("p", [P, 2, SEQ])
        p_t = ph.sb("p_t", [P, NT2, P])
        mx = ph.sb("mx", [P, 2])
        nm = ph.sb("nm", [P, 2])
        l = ph.sb("l", [P, 2])
        rl = ph.sb("rl", [P, 2])
        o = ph.sb("o", [P, H, P])
        ot = ph.sb("ot", [P, 2, H, P])
        S = ph.ps("S", [P, 2, SEQ])
        T = ph.ps("T", [P, 2, BANK])
        O = ph.ps("O", [P, BANK])
        loaded = ph.sem("loaded")
        tile_in = [ph.sem("tile_in0"), ph.sem("tile_in1")]
        cs_done = ph.sem("cs_done")
        head_in = ph.sem("head_in")
        S_ready = ph.sem("S_ready")
        X_done = ph.sem("X_done")
        max_done = ph.sem("max_done")
        p_done = ph.sem("p_done")
        turned = ph.sem("turned")
        copied = ph.sem("copied")
        O_ready = ph.sem("O_ready")
        o_done = ph.sem("o_done")
        o_turned = ph.sem("o_turned")
        ot_done = ph.sem("ot_done")
        stored = [ph.sem("stored0"), ph.sem("stored1")]
        att_v = att_t.rearrange("(h p) t -> p h t", p=P)
        groups = [[(a, min(a + 4, t + 1)) for a in range(0, t + 1, 4)] for t in range(NT2)]
        before = [H * sum(len(g) for g in groups[:t]) + 2 * t for t in range(NT2 + 1)]
        with nc.Block() as block:

            @block.sync
            def _(sp):
                sp.dma_start(sl[:, :], slopes).then_inc(loaded, 16)
                sp.dma_start(kk[:, :, :], k_t.rearrange("(h p) t -> p h t", p=P)).then_inc(loaded, 16)
                sp.dma_start(vv[:, :, :], v.rearrange("(t p) e -> p t e", p=P)).then_inc(loaded, 16)

                def load(t):
                    W = (t + 1) * P
                    sp.dma_start(q[:, t % 2], q_t[:, t * P:(t + 1) * P].rearrange("(h p) t -> p h t", p=P)).then_inc(tile_in[t % 2], 16)
                    sp.dma_start(dmt[:, t % 2, 0:W], dm[t * P:(t + 1) * P, 0:W]).then_inc(tile_in[t % 2], 16)
                load(0)
                load(1)
                for t in range(NT2):
                    if t < NT2 - 2:
                        sp.wait_ge(head_in, H * (t + 1))
                        load(t + 2)
                    sp.wait_ge(ot_done, 2 * t + 2)
                    sp.dma_start(att_v[:, :, t * P:(t + 1) * P], ot[:, t % 2]).then_inc(stored[t % 2], 16)
                for par in range(2):
                    sp.wait_ge(stored[par], 16 * NT2 // 2)

            @block.gpsimd
            def _(pool):
                pool.wait_ge(loaded, 48)
                for t in range(NT2):
                    W = (t + 1) * P
                    pool.wait_ge(tile_in[t % 2], 32 * (t // 2 + 1))
                    with pool.Fori(0, H // 2) as i:
                        for par in range(2):
                            h = i * 2 + par
                            n = h + t * H
                            pool.wait_ge(X_done, n + 1)
                            pool.tensor_copy(cs[:, par:par + 1], sl[:, bass.ds(h, 1)]).then_inc(cs_done, 1)
                            pool.tensor_copy(qs[:, par, :], q[:, t % 2, :, :].rearrange("p h t -> p (h t)")[:, bass.ds(h * P, P)])
                            pool.wait_ge(cs_done, n + 1)
                            pool.sem_inc(ph.passed, 1)
                            pool.tensor_scalar(bias[:, par, 0:W], dmt[:, t % 2, 0:W], cs[:, par:par + 1], None, ALU.mult)
                            pool.drain().then_inc(head_in, 1)

            @block.tensor
            def _(pe):
                pe.wait_ge(loaded, 48)
                pe.sem_inc(X_done, 2)
                k_flat = kk[:, :, :].rearrange("p h t -> p (h t)")
                v_flat = vv[:, :, :].rearrange("p t e -> p (t e)")
                for t in range(NT2):
                    W = (t + 1) * P
                    g = groups[t]

                    def scores(h, par):
                        n = h + t * H
                        pe.wait_ge(head_in, n + 1)
                        pe.wait_ge(X_done, n + 1)
                        for b in range(0, W, BANK):
                            e = min(W, b + BANK)
                            last = pe.matmul(S[:, par, b:e], qs[:, par, :], k_flat[:, bass.ds(h * SEQ + b, e - b)], start=True, stop=True)
                        last.then_inc(S_ready, 1)

                    def values(h, par):
                        n = h + t * H
                        pe.wait_ge(p_done, n + 1)
                        for j, (lo, hi) in enumerate(g):
                            pe.wait_ge(copied, h * len(g) + (before[t] + j + 1))
                            for b in range(lo, hi):
                                last = pe.transpose(T[:, j % 2, (b - lo) * P:(b - lo + 1) * P], p[:, par, b * P:(b + 1) * P], k.ident[:, :])
                            last.then_inc(turned, 1)
                        pe.wait_ge(o_done, n + 1)
                        for j, (lo, hi) in enumerate(g):
                            pe.wait_ge(copied, h * len(g) + (before[t] + j + 3))
                            for b in range(lo, hi):
                                last = pe.matmul(O[:, 0:P], p_t[:, b, :], v_flat[:, bass.ds(h * P + b * (H * P), P)],
                                                 start=(b == 0), stop=(b == t))
                        last.then_inc(O_ready, 1)
                    pipelined(pe, H, scores, values)
                    pe.wait_ge(o_done, H * (t + 1) + 1)
                    pe.wait_ge(copied, before[t + 1])
                    for j in range(2):
                        for b in range(4):
                            last = pe.transpose(T[:, j, b * P:(b + 1) * P], o[:, 4 * j + b, :], k.ident[:, :])
                        last.then_inc(o_turned, 1)

            @block.scalar
            def _(act):
                act.sem_inc(copied, 2)
                for t in range(NT2):
                    W = (t + 1) * P
                    g = groups[t]

                    def first(h, par):
                        n = h + t * H
                        act.wait_ge(max_done, n + 1)
                        act.wait_ge(O_ready, n + 1)
                        act.activation(p[:, par, 0:W], X[:, par, 0:W], ACT.Exp, bias=nm[:, par:par + 1], scale=ATT_SCALE,
                                       accum_out=l[:, par:par + 1]).then_inc(p_done, 1)

                    def second(h, par):
                        n = h + t * H
                        act.wait_ge(O_ready, n + 2)
                        for j, (lo, hi) in enumerate(g):
                            act.wait_ge(turned, h * len(g) + (before[t] - 2 * t + j + 1))
                            act.copy(p_t[:, lo:hi, :], T[:, j % 2, 0:(hi - lo) * P].rearrange("p (b q) -> p b q", q=P)).then_inc(copied, 1)
                    pipelined(act, H, first, second)
                    for j in range(2):
                        act.wait_ge(o_turned, 2 * t + j + 1)
                        if t >= 2 and j == 0:
                            act.wait_ge(stored[t % 2], 16 * (t // 2))
                        act.copy(ot[:, t % 2, 4 * j:4 * j + 4, :], T[:, j, :].rearrange("p (h q) -> p h q", q=P)).then_inc(ot_done, 1)
                    act.wait_ge(ot_done, 2 * t + 2)
                    act.sem_inc(copied, 2)

            @block.vector
            def _(dve):
                dve.sem_inc(O_ready, 2)
                dve.sem_inc(o_done, 1)
                for t in range(NT2):
                    W = (t + 1) * P

                    def first(h, par):
                        n = h + t * H
                        dve.wait_ge(S_ready, n + 1)
                        dve.wait_ge(head_in, n + 1)
                        dve.wait_ge(O_ready, n + 1)
                        dve.sem_inc(ph.passed, 1)
                        dve.tensor_tensor_reduce(X[:, par, 0:W], S[:, par, 0:W], bias[:, par, 0:W], 1.0, NEG, ALU.add, ALU.max,
                                                 mx[:, par:par + 1]).then_inc(X_done, 1)
                        dve.drain()
                        dve.tensor_scalar(nm[:, par:par + 1], mx[:, par:par + 1], -ATT_SCALE, None, ALU.mult).then_inc(max_done, 1)

                    def second(h, par):
                        n = h + t * H
                        if t >= 1 and isinstance(h, int) and h == 0:
                            dve.wait_ge(o_turned, 2 * t)
                        dve.wait_ge(O_ready, n + 3)
                        dve.reciprocal(rl[:, par:par + 1], l[:, par:par + 1])
                        dve.drain()
                        dve.tensor_scalar(o[:, :, :].rearrange("p h e -> p (h e)")[:, bass.ds(h * P, P)], O[:, 0:P], rl[:, par:par + 1], None,
                                          ALU.mult).then_inc(o_done, 1)
                    pipelined(dve, H, first, second)


N_GROUP = 4
PER_GROUP = 8
N_EXP2 = N_GROUP * PER_GROUP
EXTRA = 2 * SEQ // P
N_BLOCKS2 = N_EXP2 + EXTRA


def route_top2(nc, name, k, h_t, w_group, w_expert, b_group, b_expert, tab, tok_of, dest_out, gate_out, extra_out, used_out):
    NL = N_GROUP + N_EXP2
    E = N_EXP2
    with Phase(nc, name) as ph:
        h = ph.sb("h", [P, KD, SEQ])
        w = ph.sb("w", [P, KD, NL])
        bias = ph.sb("bias", [P, NL])
        ct = ph.sb("ct", [P, P])
        L = ph.sb("L", [P, NT2, NL])
        ge = ph.sb("ge", [P, NT2, N_GROUP])
        gm = ph.sb("gm", [P, NT2])
        gw = ph.sb("gw", [P, NT2])
        goh = ph.sb("goh", [P, NT2, N_GROUP])
        em = ph.sb("em", [P, NT2, E])
        tmp = ph.sb("tmp", [P, NT2, E])
        e = [ph.sb(f"e{i}", [P, NT2]) for i in range(2)]
        oh = [ph.sb(f"oh{i}", [P, NT2, E]) for i in range(2)]
        both = ph.sb("both", [P, NT2, E])
        m = ph.sb("m", [P, NT2])
        d = ph.sb("d", [P, NT2])
        p1 = ph.sb("p1", [P, NT2])
        gate = ph.sb("gate", [P, NT2, 2])
        pos = ph.sb("pos", [P, NT2, E])
        posi = ph.sb("posi", [P, NT2, E], I32)
        q = ph.sb("q", [P, NT2, E])
        cnt = ph.sb("cnt", [P, E])
        cnti = ph.sb("cnti", [P, E], I32)
        xtra = ph.sb("xtra", [P, E])
        xin = ph.sb("xin", [P, E])
        zero = ph.sb("zero", [P, E])
        A = ph.sb("A", [P, E])
        destf = ph.sb("destf", [P, NT2, 2])
        dest = ph.sb("dest", [P, NT2, 2], U32)
        tok = ph.sb("tok", [P, NT2], U32)
        zrow = ph.sb("zrow", [P, N_BLOCKS2], U32)
        cmp = ph.sb("cmp", [1, EXTRA, E])
        xe = ph.sb("xe", [1, EXTRA])
        xei = ph.sb("xei", [1, EXTRA + 1], I32)
        logits = ph.ps("logits", [P, BANK])
        pos_ps = ph.ps("pos_ps", [P, BANK])
        cnt_ps = ph.ps("cnt_ps", [P, BANK])
        loaded = ph.sem("loaded")
        zeroed = ph.sem("zeroed")
        table_zero = ph.sem("table_zero")
        logits_ready = ph.sem("logits_ready")
        centred = ph.sem("centred")
        exp_done = ph.sem("exp_done")
        both_done = ph.sem("both_done")
        pos_ready = ph.sem("pos_ready")
        dest_done = ph.sem("dest_done")
        scattered = ph.sem("scattered")
        done = ph.sem("done")
        stored = ph.sem("stored")
        with nc.Block() as block:

            @block.sync
            def _(sp):
                sp.dma_start(w[:, :, 0:N_GROUP], w_group.rearrange("(k p) e -> p k e", p=P)).then_inc(loaded, 16)
                sp.dma_start(w[:, :, N_GROUP:NL], w_expert.rearrange("(k p) e -> p k e", p=P)).then_inc(loaded, 16)
                sp.dma_start(bias[:, 0:N_GROUP], on_all(b_group)).then_inc(loaded, 16)
                sp.dma_start(bias[:, N_GROUP:NL], on_all(b_expert)).then_inc(loaded, 16)
                sp.dma_start(ct[:, :], tab).then_inc(loaded, 16)
                for c in range(KD):
                    sp.dma_start(h[:, c, :], h_t[c * P:(c + 1) * P, :]).then_inc(loaded, 16)
                sp.wait_ge(zeroed, 1)
                sp.dma_start(tok_of.rearrange("(b p) a -> p (b a)", p=P), zrow[:, :], allow_slow_non_contiguous=True).then_inc(table_zero, 16)
                sp.wait_ge(done, 1)
                sp.dma_start(dest_out, dest[:, :, :].rearrange("p t c -> p (t c)")).then_inc(stored, 16)
                sp.dma_start(gate_out, gate[:, :, :].rearrange("p t c -> p (t c)")).then_inc(stored, 16)
                sp.dma_start(extra_out, xei[:, 0:EXTRA]).then_inc(stored, 16)
                sp.dma_start(used_out, xei[:, EXTRA:EXTRA + 1], allow_slow_non_contiguous=True).then_inc(stored, 16)
                sp.wait_ge(stored, 64)

            @block.tensor
            def _(pe):
                pe.wait_ge(loaded, 16 * (KD + 5))
                for t in range(NT2):
                    for c in range(KD):
                        last = pe.matmul(logits[:, t * NL:(t + 1) * NL], h[:, c, t * P:(t + 1) * P], w[:, c, :],
                                         start=(c == 0), stop=(c == KD - 1))
                last.then_inc(logits_ready, 1)
                pe.wait_ge(both_done, 1)
                for t in range(NT2):
                    for s in range(t + 1):
                        pe.matmul(pos_ps[:, t * E:(t + 1) * E], k.before[:, :] if s == t else k.ones[:, :], both[:, s, :],
                                  start=(s == 0), stop=(s == t))
                for s in range(NT2):
                    last = pe.matmul(cnt_ps[:, 0:E], k.ones[:, :], both[:, s, :], start=(s == 0), stop=(s == NT2 - 1))
                last.then_inc(pos_ready, 1)

            @block.scalar
            def _(act):
                act.wait_ge(centred, 1)
                act.activation(ge[:, :, :], ge[:, :, :], ACT.Exp)
                act.activation(d[:, :], d[:, :], ACT.Exp).then_inc(exp_done, 1)

            @block.gpsimd
            def _(pool):
                pool.memset(zrow[:, :], 0).then_inc(zeroed, 1)
                pool.wait_ge(table_zero, 16)
                pool.wait_ge(dest_done, 1)
                for t in range(NT2):
                    for c in range(2):
                        pool.indirect_dma_start(out=tok_of, out_offset=bass.IndirectOffsetOnAxis(ap=dest[:, t, c:c + 1], axis=0),
                                                in_=tok[:, t:t + 1], in_offset=None).then_inc(scattered, 16)
                pool.wait_ge(scattered, 16 * 2 * NT2)

            @block.vector
            def _(dve):
                def wide(a, n):
                    return a[:, :].rearrange("p (t e) -> p t e", e=1).to_broadcast([P, NT2, n])

                def const(lo, n, shape):
                    a = ct[:, lo:lo + n]
                    return a.rearrange("p (t e) -> p t e", t=1).to_broadcast(shape)

                def first_max(out, values, top, rank, n):
                    dve.tensor_tensor(out, values, wide(top, n), ALU.is_equal)
                    dve.drain()
                    dve.tensor_tensor(out, out, rank, ALU.mult)
                    dve.drain()
                    dve.reduce_max(m[:, :], out, axis=AX.X)
                    dve.drain()
                    dve.tensor_tensor(out, out, wide(m, n), ALU.is_equal)
                    dve.drain()
                dve.memset(zero[:, :], 0.0)
                dve.wait_ge(loaded, 16 * (KD + 5))
                dve.wait_ge(logits_ready, 1)
                dve.tensor_tensor(L[:, :, :], logits[:, 0:NT2 * NL].rearrange("p (t e) -> p t e", e=NL),
                                  bias[:, :].rearrange("p (t e) -> p t e", t=1).to_broadcast([P, NT2, NL]), ALU.add)
                dve.tensor_copy(tok[:, :], ct[:, 100:100 + NT2])
                dve.drain()
                gl = L[:, :, 0:N_GROUP]
                dve.reduce_max(gm[:, :], gl, axis=AX.X)
                dve.drain()
                dve.tensor_tensor(ge[:, :, :], gl, wide(gm, N_GROUP), ALU.subtract)
                first_max(goh[:, :, :], gl, gm, const(96, N_GROUP, [P, NT2, N_GROUP]), N_GROUP)
                for g in range(N_GROUP):
                    cols = slice(g * PER_GROUP, (g + 1) * PER_GROUP)
                    of_g = goh[:, :, g:g + 1].to_broadcast([P, NT2, PER_GROUP])
                    dve.tensor_tensor(em[:, :, cols], L[:, :, N_GROUP + g * PER_GROUP:N_GROUP + (g + 1) * PER_GROUP], of_g, ALU.mult)
                    dve.tensor_scalar(tmp[:, :, cols], of_g, -1.0, -NEG, ALU.add, ALU.mult)
                dve.drain()
                dve.tensor_tensor(em[:, :, :], em[:, :, :], tmp[:, :, :], ALU.add)
                dve.drain()
                for c in range(2):
                    dve.reduce_max(e[c][:, :], em[:, :, :], axis=AX.X)
                    dve.drain()
                    first_max(oh[c][:, :, :], em[:, :, :], e[c], const(32, E, [P, NT2, E]), E)
                    if c == 0:
                        dve.scalar_tensor_tensor(em[:, :, :], oh[0][:, :, :], 3.0 * NEG, em[:, :, :], ALU.mult, ALU.add)
                        dve.drain()
                dve.tensor_tensor(both[:, :, :], oh[0][:, :, :], oh[1][:, :, :], ALU.add)
                dve.tensor_tensor(d[:, :], e[1][:, :], e[0][:, :], ALU.subtract)
                dve.drain().then_inc(both_done, 1)
                dve.sem_inc(centred, 1)
                dve.wait_ge(exp_done, 1)
                dve.reduce_sum(gw[:, :], ge[:, :, :], axis=AX.X)
                dve.tensor_scalar(p1[:, :], d[:, :], 1.0, None, ALU.add)
                dve.drain()
                dve.reciprocal(gw[:, :], gw[:, :])
                dve.reciprocal(p1[:, :], p1[:, :])
                dve.drain()
                dve.tensor_tensor(p1[:, :], p1[:, :], gw[:, :], ALU.mult)
                dve.drain()
                dve.tensor_copy(gate[:, :, 0], p1[:, :])
                dve.tensor_tensor(gate[:, :, 1], p1[:, :], d[:, :], ALU.mult)
                dve.wait_ge(pos_ready, 1)
                pv = pos_ps[:, 0:NT2 * E].rearrange("p (t e) -> p t e", e=E)
                dve.tensor_copy(pos[:, :, :], pv)
                dve.tensor_copy(posi[:, :, :], pv)
                dve.tensor_scalar(cnt[:, :], cnt_ps[:, 0:E], -1.0, 0.0, ALU.add, ALU.max)
                dve.drain()
                dve.tensor_copy(cnti[:, :], cnt[:, :])
                dve.tensor_scalar(posi[:, :, :], posi[:, :, :], 7, None, ALU.arith_shift_right)
                dve.drain()
                dve.tensor_scalar(cnti[:, :], cnti[:, :], 7, None, ALU.arith_shift_right)
                dve.tensor_copy(q[:, :, :], posi[:, :, :])
                dve.drain()
                dve.tensor_copy(xtra[:, :], cnti[:, :])
                dve.drain()
                dve.tensor_tensor_scan(xin[:, :], xtra[:, :], zero[:, :], 0.0, ALU.add, ALU.add)
                dve.drain()
                dve.tensor_tensor(A[:, :], xin[:, :], xtra[:, :], ALU.subtract)
                dve.drain()
                dve.tensor_tensor(A[:, :], A[:, :], ct[:, 0:E], ALU.subtract)
                dve.drain()
                dve.tensor_scalar(A[:, :], A[:, :], float(E - 1), None, ALU.add)
                dve.drain()
                flat = lambda a: a.rearrange("p (t e) -> p t e", t=1).to_broadcast([P, NT2, E])
                dve.tensor_tensor(tmp[:, :, :], q[:, :, :], flat(A[:, :]), ALU.add)
                dve.drain()
                dve.scalar_tensor_tensor(tmp[:, :, :], q[:, :, :], 0.0, tmp[:, :, :], ALU.is_gt, ALU.mult)
                dve.drain()
                dve.tensor_tensor(tmp[:, :, :], tmp[:, :, :], q[:, :, :], ALU.subtract)
                dve.drain()
                dve.tensor_tensor(tmp[:, :, :], tmp[:, :, :], flat(ct[:, 0:E]), ALU.add)
                dve.drain()
                dve.scalar_tensor_tensor(pos[:, :, :], tmp[:, :, :], float(P), pos[:, :, :], ALU.mult, ALU.add)
                dve.drain()
                for c in range(2):
                    dve.tensor_tensor(tmp[:, :, :], oh[c][:, :, :], pos[:, :, :], ALU.mult)
                    dve.drain()
                    dve.reduce_sum(destf[:, :, c], tmp[:, :, :], axis=AX.X)
                    dve.drain()
                dve.tensor_copy(dest[:, :, :], destf[:, :, :])
                dve.drain().then_inc(dest_done, 1)
                dve.tensor_tensor(cmp[:, :, :], ct[0:1, 64:64 + EXTRA].rearrange("p (x e) -> p x e", e=1).to_broadcast([1, EXTRA, E]),
                                  xin[0:1, :].rearrange("p (x e) -> p x e", x=1).to_broadcast([1, EXTRA, E]), ALU.is_ge)
                dve.drain()
                dve.reduce_sum(xe[:, :], cmp[:, :, :], axis=AX.X)
                dve.drain()
                dve.tensor_scalar(xe[:, :], xe[:, :], float(E - 1), None, ALU.min)
                dve.drain()
                dve.tensor_copy(xei[:, 0:EXTRA], xe[:, :])
                dve.tensor_copy(xei[:, EXTRA:EXTRA + 1], xin[0:1, E - 1:E])
                dve.drain().then_inc(done, 1)


def constants():
    i32 = np.arange(P)
    row, col = np.meshgrid(i32, i32, indexing="ij")
    levels = []
    for lv in range(7):
        s = 2 ** lv
        levels.append((col // (2 * s) == row // (2 * s)) & (col // s == row // s + 1))
    upto = row <= col
    grid_w, axis = 64, DA_D // 2
    t = np.arange(SEQ)
    rows = (t // grid_w).astype(np.float32)
    cols = (t % grid_w).astype(np.float32)
    inv = np.power(np.float32(10000.0), -np.arange(0, axis, 2, dtype=np.float32) / np.float32(axis)).astype(np.float32)
    ang = np.stack([(rows if (p % DA_D) // axis == 0 else cols) * inv[p % (axis // 2)] for p in range(P)]).astype(np.float32)
    swap = np.zeros((P, P), np.float32)
    for p in range(P):
        lower = p % axis < axis // 2
        swap[p + axis // 2 if lower else p - axis // 2, p] = -1.0 if lower else 1.0
    slopes = 2.0 ** (-8.0 * np.arange(1, HEADS2 + 1) / HEADS2)
    tab = np.zeros((P, P), np.float32)
    tab[:, 0:32] = np.arange(32)
    tab[:, 32:64] = 32 - np.arange(32)
    tab[:, 64:96] = np.arange(32)
    tab[:, 96:100] = 4 - np.arange(4)
    tab[:, 100:100 + NT2] = np.arange(NT2)[None] * P + i32[:, None]
    out = {
        "ident": np.eye(P), "ones": np.ones((P, P)), "upto0": upto, "upto1": upto.T, "before": row < col,
        "rope_swap": swap, "rope_cos": np.cos(ang), "rope_sin": np.sin(ang),
        "levels0": np.concatenate(levels, 1), "levels1": np.concatenate([x.T for x in levels], 1),
        "causal": np.where(col <= row, 0.0, NEG), "dist": np.arange(SEQ)[None] - i32[:, None],
        "slopes": np.tile(slopes / ATT_SCALE, (P, 1)), "route_tab": tab,
    }
    return {n: np.ascontiguousarray(a, dtype=np.float32) for n, a in out.items()}


class Resident:
    pass


def load_resident(nc, stack, c):
    k = Resident()
    names = ("ident", "ones", "upto0", "upto1", "before", "rope_swap")
    t = {n: stack.enter_context(nc.sbuf_tensor(f"k_{n}", [P, P], F32)) for n in names}
    half = stack.enter_context(nc.sbuf_tensor("k_minus_half", [P, 1], F32))
    with Phase(nc, "resident") as ph:
        loaded = ph.sem("loaded")
        with nc.Block() as block:

            @block.sync
            def _(sp):
                for n in names:
                    sp.dma_start(t[n][:, :], c[n]).then_inc(loaded, 16)
                sp.wait_ge(loaded, 16 * len(names))

            @block.vector
            def _(dve):
                dve.memset(half[:, :], -0.5)
    k.ident, k.ones, k.before, k.rope_swap = t["ident"], t["ones"], t["before"], t["rope_swap"]
    k.upto = [t["upto0"][:, :], t["upto1"][:, :]]
    k.minus_half = half
    return k


def clear_rows(nc, name, out):
    n = out.shape[0] // P
    with Phase(nc, name) as ph:
        z = ph.sb("z", [P, D])
        zeroed = ph.sem("zeroed")
        stored = ph.sem("stored")
        with nc.Block() as block:

            @block.vector
            def _(dve):
                dve.memset(z[:, :], 0.0).then_inc(zeroed, 1)

            @block.sync
            def _(sp):
                sp.wait_ge(zeroed, 1)
                for t in range(n):
                    sp.dma_start(out[t * P:(t + 1) * P, :], z[:, :]).then_inc(stored, 16)
                sp.wait_ge(stored, 16 * n)


SCRATCH = {
    "mod1": ([2, NMOD], F32), "mod2": ([1, NMOD], F32),
    "h_t": ([D, T1], F32), "g_raw_t": ([3 * GQ, T1], F32), "qk_t": ([2 * HEADS1 * P, T1], F32),
    "vga": ([T1, 1040], F32), "g_t": ([3 * GQ, T1], F32), "o_da": ([SEQ, HEADS1 * P], F32),
    "o_fwd": ([T1, GQ], F32), "o_rev": ([T1, GQ], F32), "mix_t": ([D, SEQ], F32),
    "x1": ([SEQ, D], F32), "x1_n": ([SEQ, D], F32), "x1_t": ([D, SEQ], F32),
    "choice": ([N_EXP1, CAP1], U32), "affinity": ([N_EXP1, CAP1], F32), "moe1": ([SEQ, D], F32), "x2": ([SEQ, D], F32),
    "u_t": ([D, SEQ], F32), "p_t": ([4352, SEQ], F32), "merge_t": ([2048, SEQ], F32), "kw": ([SEQ, 72], F32),
    "c_t": ([KV_RANK, SEQ], F32), "k_t": ([D, SEQ], F32), "v": ([SEQ, D], F32), "dm": ([SEQ, SEQ], F32),
    "rnn_t": ([D_RNN, SEQ], F32), "att_t": ([D, SEQ], F32), "ya_t": ([D, SEQ], F32), "yab_t": ([D, SEQ], F32),
    "h1": ([SEQ, D], F32), "h1_n": ([SEQ, D], F32), "h1_t": ([D, SEQ], F32),
    "tok_of": ([N_BLOCKS2 * P, 1], U32), "dest": ([P, 2 * NT2], U32), "gate2": ([P, 2 * NT2], F32),
    "extra": ([1, EXTRA], I32), "used": ([1, 1], I32), "rows2": ([N_BLOCKS2 * P, D], F32),
}


def build(nc, a, c, s, out):
    with ExitStack() as stack:
        k = load_resident(nc, stack, c)
        mod = lambda m, i, row=0: s[m][row, i * D:(i + 1) * D]
        modulation(nc, "mod1", [a["c"][0], a["c_ctx"]], a["w_mod"][0], a["b_mod"][0], s["mod1"])
        modulation(nc, "mod2", [a["c_2"][0]], a["w_mod_2"][0], a["b_mod_2"][0], s["mod2"])
        norm_transpose(nc, "norm_ctx", k, a["ctx"][0], a["norm1_g"][0], mod("mod1", 0, 1), mod("mod1", 1, 1), s["h_t"][:, 0:CTX])
        norm_transpose(nc, "norm_lat", k, a["x"][0], a["norm1_g"][0], mod("mod1", 0), mod("mod1", 1), s["h_t"][:, CTX:T1])
        w_in = a["w_in"][0]
        gemm_t(nc, "proj_qk", s["h_t"], w_in[:, 0:1024], s["qk_t"])
        gemm_t(nc, "proj_gdn", s["h_t"], w_in[:, 1536:3072], s["g_raw_t"])
        gemm_tok(nc, "proj_v", s["h_t"], [w_in[:, 1024:1536], w_in[:, 3072:3600]], s["vga"])
        diff_attention(nc, "da", k, s["qk_t"], s["vga"][:, 0:512], [a[n][0] for n in ("lam_q1", "lam_k1", "lam_q2", "lam_k2")],
                       c["rope_cos"], c["rope_sin"], s["o_da"])
        short_conv_l2(nc, "conv", k, s["g_raw_t"], a["conv_w"][0], s["g_t"])
        delta_rule(nc, "gdn", k, s["g_t"], s["vga"][:, 1024:1040], a["a_log"][0].rearrange("d h -> (d h)"),
                   a["dt_bias"][0].rearrange("d h -> (d h)"), [c["levels0"], c["levels1"]], [s["o_fwd"], s["o_rev"]])
        mix_norm(nc, "mix", k, s["o_da"], [s["o_fwd"], s["o_rev"]], s["vga"][:, 512:1024], a["da_subln_g"][0], a["gdn_norm_g"][0], s["mix_t"])
        gemm_tok(nc, "out1", s["mix_t"], [a["w_out"][0]], s["x1"], residual=a["x"][0], gain=mod("mod1", 2))
        norm_transpose(nc, "norm_moe1", k, s["x1"], a["norm2_g"][0], mod("mod1", 3), mod("mod1", 4), s["x1_t"], s["x1_n"])
        expert_choice(nc, "choose1", k, s["x1_t"], a["w_router"][0], s["choice"], s["affinity"])
        clear_rows(nc, "clear1", s["moe1"])
        experts(nc, "exp1", k, N_EXP1, s["choice"], s["x1_n"], a["norm2_g"][0], mod("mod1", 3), mod("mod1", 4),
                a["w_gate"][0], a["w_up"][0], a["w_down"][0], gates=s["affinity"], acc=s["moe1"])
        finish(nc, "fin1", k, s["x1"], mod("mod1", 5), a["final_g"], s["x2"], acc=s["moe1"])
        norm_transpose(nc, "norm2", k, s["x2"], a["norm1_g_2"][0], mod("mod2", 0), mod("mod2", 1), s["u_t"])
        w2 = a["w_in_2"][0]
        gemm_t(nc, "proj2", s["u_t"], w2[:, 0:4352], s["p_t"])
        gemm_t(nc, "proj2_merge", s["u_t"], w2[:, 4424:6472], s["merge_t"])
        gemm_tok(nc, "proj2_kw", s["u_t"], [w2[:, 4352:4424]], s["kw"])
        rg_lru(nc, "rnn", k, s["p_t"][0:D_RNN], s["p_t"][D_RNN:2 * D_RNN], a["conv_w_2"][0], a["conv_b_2"][0], a["w_rg_a_2"][0],
               a["b_rg_a_2"][0], a["w_rg_x_2"][0], a["b_rg_x_2"][0], a["lru_lambda_2"][0], s["rnn_t"])
        gemm_t(nc, "rnn_out", s["rnn_t"], a["w_rnn_out_2"][0], s["ya_t"], gate_t=s["merge_t"][0:D])
        kv_norm(nc, "kvn", k, s["p_t"][3584:3840], a["kv_norm_g_2"][0], s["c_t"])
        gemm_t(nc, "uk", s["c_t"], a["w_uk_2"][0].rearrange("r h d -> r (h d)"), s["k_t"])
        gemm_tok(nc, "uv", s["c_t"], [a["w_uv_2"][0].rearrange("r h d -> r (h d)")], s["v"])
        index_select(nc, "index", k, s["p_t"][3840:4352], s["kw"], c["dist"], c["causal"], s["dm"])
        sparse_attention(nc, "dsa", k, s["p_t"][2560:3584], s["k_t"], s["v"], s["dm"], c["slopes"], s["att_t"])
        gemm_t(nc, "att_out", s["att_t"], a["w_att_out_2"][0], s["yab_t"], gate_t=s["merge_t"][D:2 * D], add_t=s["ya_t"])
        gemm_tok(nc, "out2", s["yab_t"], [a["w_out_2"][0]], s["h1"], residual=s["x2"], gain=mod("mod2", 2))
        norm_transpose(nc, "norm_moe2", k, s["h1"], a["norm2_g_2"][0], mod("mod2", 3), mod("mod2", 4), s["h1_t"], s["h1_n"])
        route_top2(nc, "route2", k, s["h1_t"], a["w_group_2"][0], a["w_expert_2"][0], a["b_group_2"][0], a["b_expert_2"][0],
                   c["route_tab"], s["tok_of"], s["dest"], s["gate2"], s["extra"], s["used"])
        toks = s["tok_of"].rearrange("(b p) a -> b (p a)", p=P)
        weights = [a[n][0] for n in ("moe_w1_2", "moe_w3_2", "moe_w2_2")]
        clear_rows(nc, "clear2", s["rows2"][N_EXP2 * P:])
        experts(nc, "exp2", k, N_EXP2, toks[0:N_EXP2], s["h1_n"], a["norm2_g_2"][0], mod("mod2", 3), mod("mod2", 4), *weights,
                rows_out=s["rows2"])
        experts(nc, "exp2x", k, EXTRA, toks[N_EXP2:N_BLOCKS2], s["h1_n"], a["norm2_g_2"][0], mod("mod2", 3), mod("mod2", 4), *weights,
                rows_out=s["rows2"], first=N_EXP2, expert_of=s["extra"], used=s["used"])
        finish(nc, "fin2", k, s["h1"], mod("mod2", 5), a["final_g_2"], out, rows=s["rows2"], dest=s["dest"], gates=s["gate2"])


INPUTS = ["x", "c", "ctx", "c_ctx", "w_mod", "b_mod", "norm1_g", "w_in", "conv_w", "a_log", "dt_bias", "gdn_norm_g", "lam_q1",
          "lam_k1", "lam_q2", "lam_k2", "da_subln_g", "w_out", "norm2_g", "w_router", "w_gate", "w_up", "w_down", "final_g",
          "c_2", "w_mod_2", "b_mod_2", "norm1_g_2", "w_in_2", "conv_w_2", "conv_b_2", "w_rg_a_2", "b_rg_a_2", "w_rg_x_2",
          "b_rg_x_2", "lru_lambda_2", "kv_norm_g_2", "w_uk_2", "w_uv_2", "w_rnn_out_2", "w_att_out_2", "w_out_2", "norm2_g_2",
          "w_group_2", "b_group_2", "w_expert_2", "b_expert_2", "moe_w1_2", "moe_w3_2", "moe_w2_2", "final_g_2"]


def kernel(**inputs):
    import concourse.bacc as bacc
    from concourse.bass_utils import run_bass_kernel_spmd

    nc = bacc.Bacc("TRN2", target_bir_lowering=False, num_devices=1)
    arrays, a, c = {}, {}, {}
    for name in INPUTS:
        arrays[f"in_{name}"] = np.ascontiguousarray(inputs[name])
        a[name] = nc.dram_tensor(f"in_{name}", arrays[f"in_{name}"].shape, F32, kind="ExternalInput").ap()
    for name, value in constants().items():
        arrays[f"const_{name}"] = value
        c[name] = nc.dram_tensor(f"const_{name}", value.shape, F32, kind="ExternalInput").ap()
    s = {name: nc.dram_tensor(f"scratch_{name}", shape, dt).ap() for name, (shape, dt) in SCRATCH.items()}
    out = nc.dram_tensor("out", [SEQ, D], F32, kind="ExternalOutput").ap()
    build(nc, a, c, s, out)
    r = run_bass_kernel_spmd(nc, [arrays], core_ids=[0])
    return np.asarray(r.results[0]["out"]).reshape(1, SEQ, D)
```

```python
from contextlib import ExitStack

import numpy as np

import concourse.bass as bass
from concourse import mybir

F32 = mybir.dt.float32
F32R = mybir.dt.float32r
I32 = mybir.dt.int32
U32 = mybir.dt.uint32
ALU = mybir.AluOpType
ACT = mybir.ActivationFunctionType
AX = mybir.AxisListType
P = 128
BANK = 512
EPS = 1e-6
TOP_BITS = -4096

D = 1024
KD = D // P
SEQ = 1024
CTX = 256
T1 = CTX + SEQ
HEADS1 = 4
NMOD = 6 * D
NEG = -1e30


class Phase:

    def __init__(self, nc, name):
        self.nc, self.name = nc, name

    def __enter__(self):
        self.stack = ExitStack()
        self.stack.__enter__()
        self.sems = []
        self.passed = self.sem("passed")
        return self

    def __exit__(self, *e):
        if e[0] is not None:
            return False
        self.stack.close()
        self.nc.clear_and_free_semaphores(self.sems)
        self.nc.all_engine_barrier()
        return False

    def sb(self, name, shape, dt=F32):
        return self.stack.enter_context(self.nc.sbuf_tensor(f"{self.name}_{name}", shape, dt))

    def ps(self, name, shape):
        return self.stack.enter_context(self.nc.psum_tensor(f"{self.name}_{name}", shape, F32))

    def sem(self, name):
        s = self.nc.alloc_semaphore(f"{self.name}_{name}")
        self.sems.append(s)
        return s


def columns(row):
    return row.rearrange("(k p) -> p k", p=P)


def on_all(row, n=P):
    return row.rearrange("(a d) -> a d", a=1).to_broadcast([n, row.shape[0]])


def split(dve, x, top, rest, bits):
    dve.tensor_scalar(bits, x.bitcast(I32), TOP_BITS, None, ALU.bitwise_and)
    dve.drain()
    dve.tensor_copy(top, bits.bitcast(F32))
    dve.tensor_tensor(rest, x, bits.bitcast(F32), ALU.subtract)
    return dve.drain()


def split_products(pe, n, left, right, outs, ready=None):
    for kk in range(n):
        if ready is not None:
            ready(kk)
        l_top, l_rest = left(kk)
        for g, out in enumerate(outs):
            r_top, r_rest = right(kk, g)
            pe.matmul(out, l_top, r_top, start=(kk == 0), stop=False)
            pe.matmul(out, l_top, r_rest, start=False, stop=False)
            last = pe.matmul(out, l_rest, r_top, start=False, stop=(kk == n - 1))
    return last


def modulation(nc, name, conds, w, b, out):
    n = len(conds)
    COLS = BANK
    steps = NMOD // COLS
    w_v = w.rearrange("(k p) n -> p k n", p=P)
    with Phase(nc, name) as ph:
        c_in = ph.sb("c_in", [P, n, KD])
        c_act = ph.sb("c_act", [P, KD, n])
        w_buf = ph.sb("w", [P, 2, KD, COLS])
        bias = ph.sb("bias", [n, NMOD])
        rows = ph.sb("rows", [n, NMOD])
        acc = ph.ps("acc", [P, 2, BANK])
        inputs_in = ph.sem("inputs_in")
        silu_done = ph.sem("silu_done")
        w_in = [ph.sem("w_in0"), ph.sem("w_in1")]
        w_used = ph.sem("w_used")
        acc_ready = ph.sem("acc_ready")
        acc_free = ph.sem("acc_free")
        stored = ph.sem("stored")
        with nc.Block() as block:

            @block.sync
            def _(sp):
                for i in range(n):
                    sp.dma_start(c_in[:, i, :], columns(conds[i]), allow_slow_non_contiguous=True).then_inc(inputs_in, 16)
                sp.dma_start(bias[:, :], on_all(b, n)).then_inc(inputs_in, 16)
                with sp.Fori(0, steps // 2) as i:
                    for half in range(2):
                        sp.wait_ge(w_used, i * 2 + half + 1)
                        sp.dma_start(w_buf[:, half], w_v[:, :, bass.ds(i * (2 * COLS) + half * COLS, COLS)]).then_inc(w_in[half], 16)
                sp.wait_ge(acc_free, steps + 2)
                sp.dma_start(out, rows[:, :]).then_inc(stored, 16)
                sp.wait_ge(stored, 16)

            @block.scalar
            def _(act):
                act.wait_ge(inputs_in, 16 * (n + 1))
                for i in range(n):
                    last = act.activation(c_act[:, :, i], c_in[:, i, :], ACT.Silu)
                last.then_inc(silu_done, 1)

            @block.tensor
            def _(pe):
                pe.sem_inc(w_used, 2)
                pe.wait_ge(silu_done, 1)
                with pe.Fori(0, steps // 2) as i:
                    for half in range(2):
                        pe.wait_ge(w_in[half], i * 16 + 16)
                        pe.wait_ge(acc_free, i * 2 + half + 1)
                        for k in range(KD):
                            last = pe.matmul(acc[0:n, half, :], c_act[:, k, :], w_buf[:, half, k, :],
                                             start=(k == 0), stop=(k == KD - 1))
                        last.then_inc(acc_ready, 1)
                        pe.wait_ge(acc_ready, i * 2 + half + 1)
                        pe.sem_inc(w_used, 1)

            @block.vector
            def _(dve):
                dve.sem_inc(acc_free, 2)
                dve.wait_ge(inputs_in, 16 * (n + 1))
                with dve.Fori(0, steps // 2) as i:
                    for half in range(2):
                        at = bass.ds(i * (2 * COLS) + half * COLS, COLS)
                        dve.wait_ge(acc_ready, i * 2 + half + 1)
                        dve.tensor_tensor(rows[:, at], acc[0:n, half, :], bias[:, at], ALU.add).then_inc(acc_free, 1)


def norm_transpose(nc, name, k, src, g, shift, scale, out_t, out_n=None):
    n = src.shape[0] // P
    out_v = out_t.rearrange("(k p) t -> p k t", p=P)
    with Phase(nc, name) as ph:
        gain = ph.sb("gain", [P, KD])
        sh = ph.sb("sh", [P, KD])
        sc = ph.sb("sc", [P, KD])
        x = ph.sb("x", [P, 2, D])
        sq = ph.sb("sq", [P, D])
        xn = ph.sb("xn", [P, 2, D])
        ss = ph.sb("ss", [P, 2])
        ms = ph.sb("ms", [P, 2])
        rstd = ph.sb("rstd", [P, 2])
        ht = ph.sb("ht", [P, 2, KD, P])
        turned = ph.ps("turned", [P, 2, KD, P])
        vecs_in = ph.sem("vecs_in")
        gain_done = ph.sem("gain_done")
        x_in = [ph.sem("x_in0"), ph.sem("x_in1")]
        sq_done = ph.sem("sq_done")
        ms_done = ph.sem("ms_done")
        rstd_done = ph.sem("rstd_done")
        xn_done = ph.sem("xn_done")
        turned_ready = ph.sem("turned_ready")
        ht_dve = ph.sem("ht_dve")
        ht_act = ph.sem("ht_act")
        t_out = [ph.sem("t_out0"), ph.sem("t_out1")]
        n_out = [ph.sem("n_out0"), ph.sem("n_out1")]
        with nc.Block() as block:

            @block.sync
            def _(sp):
                for dst, row in ((gain, g), (sh, shift), (sc, scale)):
                    sp.dma_start(dst[:, :], columns(row), allow_slow_non_contiguous=True).then_inc(vecs_in, 16)
                with sp.Fori(0, n // 2) as i:
                    for half in range(2):
                        sp.wait_ge(xn_done, i * 2 + half + 1)
                        sp.dma_start(x[:, half, :], src[bass.ds(i * (2 * P) + half * P, P), :]).then_inc(x_in[half], 16)

            @block.scalar
            def _(act):
                act.wait_ge(gain_done, 1)
                with act.Fori(0, n // 2) as i:
                    for half in range(2):
                        t = i * 2 + half
                        act.wait_ge(x_in[half], i * 16 + 16)
                        act.wait_ge(xn_done, t + 1)
                        act.wait_ge(sq_done, t + 1)
                        act.activation(sq[:, :], x[:, half, :], ACT.Square, accum_out=ss[:, half:half + 1]).then_inc(sq_done, 1)
                        act.wait_ge(turned_ready, t + 1)
                        act.wait_ge(t_out[half], i * 16 + 16)
                        for c in range(KD // 2, KD):
                            last = act.activation(ht[:, half, c, :], turned[:, half, c, :], ACT.Identity,
                                                  bias=sh[:, c:c + 1], scale=gain[:, c:c + 1])
                        last.then_inc(ht_act, 1)
                        act.wait_ge(ht_act, t + 3)
                        act.wait_ge(ht_dve, t + 3)
                        act.dma_start(out_v[:, :, bass.ds(t * P, P)], ht[:, half]).then_inc(t_out[half], 16)
                        if out_n is not None:
                            act.dma_start(out_n[bass.ds(t * P, P), :], xn[:, half, :]).then_inc(n_out[half], 16)
                for half in range(2):
                    act.wait_ge(t_out[half], 16 * (n // 2) + 16)
                    if out_n is not None:
                        act.wait_ge(n_out[half], 16 * (n // 2) + 16)

            @block.gpsimd
            def _(pool):
                with pool.Fori(0, n // 2) as i:
                    for half in range(2):
                        t = i * 2 + half
                        pool.wait_ge(sq_done, t + 2)
                        pool.sem_inc(ph.passed, 1)
                        pool.tensor_scalar(ms[:, half:half + 1], ss[:, half:half + 1], 1.0 / D, EPS, ALU.mult, ALU.add).then_inc(ms_done, 1)
                        pool.wait_ge(ms_done, t + 1)
                        pool.tensor_tensor(rstd[:, half:half + 1], ms[:, half:half + 1], k.minus_half[:, :], ALU.pow).then_inc(rstd_done, 1)

            @block.vector
            def _(dve):
                dve.sem_inc(xn_done, 2)
                dve.sem_inc(sq_done, 1)
                dve.sem_inc(ht_dve, 2)
                dve.sem_inc(ht_act, 2)
                for half in range(2):
                    dve.sem_inc(t_out[half], 16)
                    dve.sem_inc(n_out[half], 16)
                dve.wait_ge(vecs_in, 48)
                dve.scalar_tensor_tensor(gain[:, :], sc[:, :], 1.0, gain[:, :], ALU.add, ALU.mult).then_inc(gain_done, 1)
                dve.wait_ge(gain_done, 1)
                with dve.Fori(0, n // 2) as i:
                    for half in range(2):
                        t = i * 2 + half
                        dve.wait_ge(rstd_done, t + 1)
                        if out_n is not None:
                            dve.wait_ge(n_out[half], i * 16 + 16)
                        dve.tensor_scalar(xn[:, half, :], x[:, half, :], rstd[:, half:half + 1], None, ALU.mult).then_inc(xn_done, 1)
                        dve.wait_ge(turned_ready, t + 1)
                        dve.wait_ge(t_out[half], i * 16 + 16)
                        for c in range(KD // 2):
                            last = dve.tensor_scalar(ht[:, half, c, :], turned[:, half, c, :], gain[:, c:c + 1], sh[:, c:c + 1],
                                                     ALU.mult, ALU.add)
                        last.then_inc(ht_dve, 1)

            @block.tensor
            def _(pe):
                with pe.Fori(0, n // 2) as i:
                    for half in range(2):
                        t = i * 2 + half
                        pe.wait_ge(xn_done, t + 3)
                        pe.wait_ge(ht_dve, t + 1)
                        pe.wait_ge(ht_act, t + 1)
                        for c in range(KD):
                            last = pe.transpose(turned[:, half, c, :], xn[:, half, c * P:(c + 1) * P], k.ident[:, :])
                        last.then_inc(turned_ready, 1)


def gemm_t(nc, name, act_t, w, out_t, gate_t=None, add_t=None):
    K, T = act_t.shape
    cols = w.shape[1]
    kc = K // P
    W = 2 * P
    steps = cols // W
    assert cols % W == 0
    pieces = [(a, min(BANK, T - a)) for a in range(0, T, BANK)]
    nb = len(pieces)
    act_pieces = [] if gate_t is not None else pieces[: nb // 2]
    dve_pieces = pieces if gate_t is not None else pieces[nb // 2:]
    w_v = w.rearrange("(k p) n -> p k n", p=P)
    with Phase(nc, name) as ph:
        x_buf = ph.sb("x_buf", [P, 4, T])
        x_top = ph.sb("x_top", [P, kc, T], F32R)
        x_rest = ph.sb("x_rest", [P, kc, T], F32R)
        w_buf = ph.sb("w", [P, 2, kc, W])
        w_top = ph.sb("w_top", [P, 2, kc, W], F32R)
        w_rest = ph.sb("w_rest", [P, 2, kc, W], F32R)
        bits = ph.sb("bits", [P, max(kc * W, T)], I32)
        o = ph.sb("o", [P, 2, T])
        acc = ph.ps("acc", [P, 2, nb * BANK])
        x_in = [ph.sem(f"x_in{i}") for i in range(kc)]
        x_split = ph.sem("x_split")
        w_split = ph.sem("w_split")
        w_in = [ph.sem("w_in0"), ph.sem("w_in1")]
        w_used = ph.sem("w_used")
        acc_ready = ph.sem("acc_ready")
        o_act = ph.sem("o_act")
        o_dve = ph.sem("o_dve")
        stored = [ph.sem("stored0"), ph.sem("stored1")]
        if gate_t is not None:
            gate = ph.sb("gate", [P, 2, T])
            sig = ph.sb("sig", [P, 2, T])
            gate_in = [ph.sem("gate_in0"), ph.sem("gate_in1")]
            sig_done = ph.sem("sig_done")
        if add_t is not None:
            add = ph.sb("add", [P, 2, T])
            add_in = [ph.sem("add_in0"), ph.sem("add_in1")]
        with nc.Block() as block:

            @block.sync
            def _(sp):
                with sp.Fori(0, steps // 2) as i:
                    for half in range(2):
                        sp.wait_ge(w_used, i * 2 + half + 1)
                        sp.dma_start(w_buf[:, half], w_v[:, :, bass.ds(i * (2 * W) + half * W, W)]).then_inc(w_in[half], 16)
                if steps % 2:
                    sp.wait_ge(w_used, steps)
                    sp.dma_start(w_buf[:, 0], w_v[:, :, (steps - 1) * W:steps * W]).then_inc(w_in[0], 16)

            @block.tensor
            def _(pe):
                pe.sem_inc(w_used, 2)

                def step(j, half):
                    pe.wait_ge(w_split, j + 1)
                    for c in range(2):
                        b = j * 2 + c
                        pe.wait_ge(o_act, b + 1)
                        pe.wait_ge(o_dve, b + 1)
                        cs = slice(c * P, (c + 1) * P)
                        last = split_products(pe, kc, lambda kk: (w_top[:, half, kk, cs], w_rest[:, half, kk, cs]),
                                              lambda kk, g: (x_top[:, kk, pieces[g][0]:sum(pieces[g])], x_rest[:, kk, pieces[g][0]:sum(pieces[g])]),
                                              [acc[:, c, a:a + m] for a, m in pieces], lambda kk: pe.wait_ge(x_split, kk + 1))
                        last.then_inc(acc_ready, 1)
                    pe.wait_ge(acc_ready, j * 2 + 2)
                    pe.sem_inc(w_used, 1)

                with pe.Fori(0, steps // 2) as i:
                    for half in range(2):
                        step(i * 2 + half, half)
                if steps % 2:
                    step(steps - 1, 0)

            @block.scalar
            def _(act):
                for c in range(kc):
                    if c >= 4:
                        act.wait_ge(x_split, c - 3)
                    act.dma_start(x_buf[:, c % 4, :], act_t[c * P:(c + 1) * P, :]).then_inc(x_in[c], 16)
                act.sem_inc(o_act, 2)
                for c in range(2):
                    act.sem_inc(stored[c], 16)

                with act.Fori(0, steps) as j:
                    for c in range(2):
                        b = j * 2 + c
                        if gate_t is not None:
                            act.wait_ge(gate_in[c], j * 16 + 16)
                            act.wait_ge(o_dve, b + 1)
                            act.activation(sig[:, c, :], gate[:, c, :], ACT.Sigmoid).then_inc(sig_done, 1)
                        act.wait_ge(acc_ready, b + 1)
                        act.wait_ge(stored[c], j * 16 + 16)
                        if act_pieces:
                            for a, m in act_pieces:
                                last = act.copy(o[:, c, a:a + m], acc[:, c, a:a + m])
                            last.then_inc(o_act, 1)
                        else:
                            act.sem_inc(o_act, 1)
                        act.wait_ge(o_act, b + 3)
                        act.wait_ge(o_dve, b + 3)
                        act.dma_start(out_t[bass.ds(b * P, P), :], o[:, c, :]).then_inc(stored[c], 16)
                for c in range(2):
                    act.wait_ge(stored[c], 16 * steps + 16)

            @block.vector
            def _(dve):
                dve.sem_inc(o_dve, 2)

                def split_w(i, half):
                    dve.wait_ge(w_in[half], i * 16 + 16)
                    split(dve, w_buf[:, half], w_top[:, half], w_rest[:, half],
                          bits[:, 0:kc * W].rearrange("p (k c) -> p k c", c=W)).then_inc(w_split, 1)

                def evacuate(j):
                    for c in range(2):
                        b = j * 2 + c
                        dve.wait_ge(acc_ready, b + 1)
                        dve.wait_ge(stored[c], j * 16 + 16)
                        if gate_t is not None:
                            dve.wait_ge(sig_done, b + 1)
                            if add_t is not None:
                                dve.wait_ge(add_in[c], j * 16 + 16)
                                for a, m in pieces:
                                    dve.tensor_tensor(o[:, c, a:a + m], acc[:, c, a:a + m], sig[:, c, a:a + m], ALU.mult)
                                dve.drain()
                                last = dve.tensor_tensor(o[:, c, :], o[:, c, :], add[:, c, :], ALU.add)
                            else:
                                for a, m in pieces:
                                    last = dve.tensor_tensor(o[:, c, a:a + m], acc[:, c, a:a + m], sig[:, c, a:a + m], ALU.mult)
                        else:
                            for a, m in dve_pieces:
                                last = dve.tensor_copy(o[:, c, a:a + m], acc[:, c, a:a + m])
                        last.then_inc(o_dve, 1)
                split_w(0, 0)
                for c in range(kc):
                    dve.wait_ge(x_in[c], 16)
                    split(dve, x_buf[:, c % 4, :], x_top[:, c, :], x_rest[:, c, :], bits[:, 0:T]).then_inc(x_split, 1)
                with dve.Fori(0, (steps - 1) // 2) as i:
                    split_w(i, 1)
                    evacuate(i * 2)
                    split_w(i + 1, 0)
                    evacuate(i * 2 + 1)
                if steps % 2 == 0:
                    split_w(steps // 2 - 1, 1)
                    evacuate(steps - 2)
                evacuate(steps - 1)

            if gate_t is not None:

                @block.gpsimd
                def _(pool):
                    with pool.Fori(0, steps) as j:
                        for c in range(2):
                            b = j * 2 + c
                            pool.wait_ge(o_dve, b + 1)
                            pool.dma_start(gate[:, c, :], gate_t[bass.ds(b * P, P), :]).then_inc(gate_in[c], 16)
                            if add_t is not None:
                                pool.dma_start(add[:, c, :], add_t[bass.ds(b * P, P), :]).then_inc(add_in[c], 16)


def gemm_tok(nc, name, act_t, w, out, n0=0, residual=None, gain=None):
    K, T = act_t.shape
    cols = sum(x.shape[1] for x in w)
    kc = K // P
    n = T // P - n0
    pieces = [(a, min(BANK, cols - a)) for a in range(0, cols, BANK)]
    nb = len(pieces)
    act_v = act_t.rearrange("(k p) t -> p k t", p=P)
    with Phase(nc, name) as ph:
        w_buf = ph.sb("w", [P, 4, cols])
        w_top = ph.sb("w_top", [P, kc, cols], F32R)
        w_rest = ph.sb("w_rest", [P, kc, cols], F32R)
        x = ph.sb("x", [P, 2, kc, P])
        x_top = ph.sb("x_top", [P, 2, kc, P], F32R)
        x_rest = ph.sb("x_rest", [P, 2, kc, P], F32R)
        bits = ph.sb("bits", [P, max(kc * P, cols)], I32)
        o = ph.sb("o", [P, 2, cols])
        acc = ph.ps("acc", [P, 2, nb * BANK])
        w_in = [ph.sem(f"w_in{i}") for i in range(kc)]
        w_split = ph.sem("w_split")
        x_split = ph.sem("x_split")
        x_in = [ph.sem("x_in0"), ph.sem("x_in1")]
        acc_ready = ph.sem("acc_ready")
        o_done = ph.sem("o_done")
        stored = [ph.sem("stored0"), ph.sem("stored1")]
        if residual is not None:
            res = ph.sb("res", [P, 2, cols])
            gn = ph.sb("gn", [P, cols])
            tmp = ph.sb("tmp", [P, cols])
            res_in = [ph.sem("res_in0"), ph.sem("res_in1")]
            gn_in = ph.sem("gn_in")
        with nc.Block() as block:

            @block.sync
            def _(sp):
                if residual is not None:
                    sp.dma_start(gn[:, :], on_all(gain)).then_inc(gn_in, 16)
                with sp.Fori(0, n // 2) as i:
                    for half in range(2):
                        t = i * 2 + half
                        sp.wait_ge(o_done, t + 1)
                        sp.dma_start(x[:, half], act_v[:, :, bass.ds((t + n0) * P, P)]).then_inc(x_in[half], 16)
                        if residual is not None:
                            sp.dma_start(res[:, half, :], residual[bass.ds(t * P, P), :]).then_inc(res_in[half], 16)

            @block.tensor
            def _(pe):
                with pe.Fori(0, n // 2) as i:
                    for half in range(2):
                        t = i * 2 + half
                        pe.wait_ge(x_split, t + 1)
                        pe.wait_ge(o_done, t + 1)
                        split_products(pe, kc, lambda kk: (x_top[:, half, kk, :], x_rest[:, half, kk, :]),
                                       lambda kk, g: (w_top[:, kk, pieces[g][0]:sum(pieces[g])], w_rest[:, kk, pieces[g][0]:sum(pieces[g])]),
                                       [acc[:, half, a:a + m] for a, m in pieces],
                                       lambda kk: pe.wait_ge(w_split, kk + 1)).then_inc(acc_ready, 1)

            @block.vector
            def _(dve):
                dve.sem_inc(o_done, 2)
                for half in range(2):
                    dve.sem_inc(stored[half], 16)
                if residual is not None:
                    dve.wait_ge(gn_in, 16)

                def split_x(i, half):
                    dve.wait_ge(x_in[half], i * 16 + 16)
                    split(dve, x[:, half], x_top[:, half], x_rest[:, half],
                          bits[:, 0:kc * P].rearrange("p (k t) -> p k t", t=P)).then_inc(x_split, 1)

                def evacuate(i, half):
                    dve.wait_ge(acc_ready, i * 2 + half + 1)
                    dve.wait_ge(stored[half], i * 16 + 16)
                    if residual is not None:
                        dve.wait_ge(res_in[half], i * 16 + 16)
                        dve.sem_inc(ph.passed, 1)
                        dve.drain()
                        for a, m in pieces:
                            dve.tensor_tensor(tmp[:, a:a + m], acc[:, half, a:a + m], gn[:, a:a + m], ALU.mult)
                        dve.drain()
                        last = dve.tensor_tensor(o[:, half, :], tmp[:, :], res[:, half, :], ALU.add)
                    else:
                        for a, m in pieces:
                            last = dve.tensor_copy(o[:, half, a:a + m], acc[:, half, a:a + m])
                    last.then_inc(o_done, 1)
                split_x(0, 0)
                for kk in range(kc):
                    dve.wait_ge(w_in[kk], 16 * len(w))
                    split(dve, w_buf[:, kk % 4, :], w_top[:, kk, :], w_rest[:, kk, :], bits[:, 0:cols]).then_inc(w_split, 1)
                with dve.Fori(0, n // 2 - 1) as i:
                    split_x(i, 1)
                    evacuate(i, 0)
                    split_x(i + 1, 0)
                    evacuate(i, 1)
                split_x(n // 2 - 1, 1)
                evacuate(n // 2 - 1, 0)
                evacuate(n // 2 - 1, 1)

            @block.scalar
            def _(act):
                for kk in range(kc):
                    at = 0
                    if kk >= 4:
                        act.wait_ge(w_split, kk - 3)
                    for x_w in w:
                        act.dma_start(w_buf[:, kk % 4, at:at + x_w.shape[1]], x_w[kk * P:(kk + 1) * P, :]).then_inc(w_in[kk], 16)
                        at += x_w.shape[1]
                with act.Fori(0, n // 2) as i:
                    for half in range(2):
                        t = i * 2 + half
                        act.wait_ge(o_done, t + 3)
                        act.dma_start(out[bass.ds(t * P, P), :], o[:, half, :]).then_inc(stored[half], 16)
                for half in range(2):
                    act.wait_ge(stored[half], 16 * (n // 2) + 16)


LAM_INIT = 0.8 - 0.6
DA_D = 64
QT = SEQ // P
KT1 = T1 // P


def pipelined(eng, n, first, second):
    first(0, 0)
    with eng.Fori(0, (n - 2) // 2) as i:
        for half in range(2):
            first(i * 2 + half + 1, 1 - half)
            second(i * 2 + half, half)
    first(n - 1, 1)
    second(n - 2, 0)
    second(n - 1, 1)


def diff_attention(nc, name, k, p_t, v, lam, rope_cos, rope_sin, o_da):
    H = HEADS1
    N = H * QT
    SC = DA_D ** -0.5
    LAT = T1 - CTX
    S_PIECES = [(a, min(BANK, T1 - a)) for a in range(0, T1, BANK)]
    GROUPS = [(0, 4), (4, 8), (8, 10)]
    with Phase(nc, name) as ph:
        q = ph.sb("q", [P, H, SEQ])
        kk = ph.sb("k", [P, H, T1])
        vv = ph.sb("v", [P, KT1, H * P])
        cos = ph.sb("cos", [P, SEQ])
        sin = ph.sb("sin", [P, SEQ])
        rot = ph.sb("rot", [P, SEQ])
        lv = ph.sb("lv", [P, 4, DA_D])
        lp = ph.sb("lp", [P, 2, DA_D])
        ls = ph.sb("ls", [P, 2])
        le = ph.sb("le", [P, 2])
        neglam = ph.sb("neglam", [P, 1])
        qz = ph.sb("qz", [P, 2, 2, P])
        p = ph.sb("p", [P, 2, T1])
        a = ph.sb("a", [P, 2, T1])
        a_t = ph.sb("a_t", [P, KT1, P])
        mx = ph.sb("mx", [P, 2, 2])
        nm = ph.sb("nm", [P, 2, 2])
        l = ph.sb("l", [P, 2, 2])
        rl = ph.sb("rl", [P, 2, 2])
        c = ph.sb("c", [P, 2])
        o_all = ph.sb("o_all", [P, N, P])
        S = [ph.ps("S0", [P, 3 * BANK]), ph.ps("S1", [P, 3 * BANK])]
        turned = ph.ps("turned", [P, BANK])
        O = ph.ps("O", [P, BANK])
        loaded = ph.sem("loaded")
        rot_ready = ph.sem("rot_ready")
        rope_done = ph.sem("rope_done")
        lam_sums = ph.sem("lam_sums")
        lam_exp = ph.sem("lam_exp")
        zeroed = ph.sem("zeroed")
        qz_ready = ph.sem("qz_ready")
        S_ready = [ph.sem("S0_ready"), ph.sem("S1_ready")]
        max_done = [ph.sem("max0_done"), ph.sem("max1_done")]
        exp_done = [ph.sem("exp0_done"), ph.sem("exp1_done")]
        a_done = ph.sem("a_done")
        turned_ready = ph.sem("turned_ready")
        a_t_done = ph.sem("a_t_done")
        O_ready = ph.sem("O_ready")
        O_used = ph.sem("O_used")
        stored = ph.sem("stored")
        with nc.Block() as block:

            @block.sync
            def _(sp):
                sp.dma_start(cos[:, :], rope_cos).then_inc(loaded, 16)
                sp.dma_start(sin[:, :], rope_sin).then_inc(loaded, 16)
                for i, row in enumerate(lam):
                    sp.dma_start(lv[:, i, :], on_all(row)).then_inc(loaded, 16)
                sp.dma_start(q[:, :, :], p_t[0:H * P, CTX:T1].rearrange("(h p) t -> p h t", p=P)).then_inc(loaded, 16)
                sp.dma_start(kk[:, :, :], p_t[H * P:2 * H * P, :].rearrange("(h p) t -> p h t", p=P)).then_inc(loaded, 16)
                sp.dma_start(vv[:, :, :], v.rearrange("(t p) e -> p t e", p=P)).then_inc(loaded, 16)
                sp.wait_ge(O_used, N + 1)
                o_v = o_da.rearrange("(t p) (h e) -> h p t e", p=P, e=P)
                for h in range(H):
                    sp.dma_start(o_v[h], o_all[:, h * QT:(h + 1) * QT, :]).then_inc(stored, 16)
                sp.wait_ge(stored, 16 * H)

            @block.gpsimd
            def _(pool):
                pool.memset(qz[64:128, :, 0, :], 0.0)
                pool.memset(qz[0:64, :, 1, :], 0.0).then_inc(zeroed, 1)
                pool.wait_ge(zeroed, 1)
                pool.wait_ge(rope_done, 2 * H)
                with pool.Fori(0, N // 2) as i:
                    for half in range(2):
                        pool.wait_ge(S_ready[1], i * 2 + half + 1)
                        at = bass.ds(i * (2 * P) + half * P, P)
                        q_flat = q[:, :, :].rearrange("p h t -> p (h t)")
                        pool.tensor_copy(qz[0:64, half, 0, :], q_flat[0:64, at])
                        pool.tensor_copy(qz[64:128, half, 1, :], q_flat[64:128, at]).then_inc(qz_ready, 1)

            @block.tensor
            def _(pe):
                pe.wait_ge(loaded, 16 * 9)
                for j in range(2 * H):
                    if j >= 1:
                        pe.wait_ge(rope_done, j)
                    src = q[:, j // 2, :] if j % 2 == 0 else kk[:, j // 2, CTX:T1]
                    for b in range(SEQ // BANK):
                        last = pe.matmul(S[0][:, b * BANK:(b + 1) * BANK], k.rope_swap[:, :], src[:, b * BANK:(b + 1) * BANK],
                                         start=True, stop=True)
                    last.then_inc(rot_ready, 1)
                pe.sem_inc(S_ready[1], 2)
                pe.wait_ge(rope_done, 2 * H)
                k_flat = kk[:, :, :].rearrange("p h t -> p (h t)")
                v_flat = vv[:, :, :].rearrange("p t e -> p (t e)")

                def scores(s, par):
                    pe.wait_ge(qz_ready, s + 1)
                    h = s // QT
                    for i in range(2):
                        pe.wait_ge(exp_done[i], s + 1)
                        for at, m in S_PIECES:
                            last = pe.matmul(S[i][:, at:at + m], qz[:, par, i, :], k_flat[:, bass.ds(h * T1 + at, m)],
                                             start=True, stop=True)
                        last.then_inc(S_ready[i], 1)

                def values(s, par):
                    h = s // QT
                    pe.wait_ge(a_done, s + 1)

                    def turn(g):
                        lo, hi = GROUPS[g]
                        pe.wait_ge(a_t_done, s * 3 + g + 1)
                        for b in range(lo, hi):
                            last = pe.transpose(turned[:, (b - lo) * P:(b - lo + 1) * P], a[:, par, b * P:(b + 1) * P], k.ident[:, :])
                        last.then_inc(turned_ready, 1)

                    def product(g):
                        lo, hi = GROUPS[g]
                        pe.wait_ge(a_t_done, s * 3 + g + 2)
                        for b in range(lo, hi):
                            last = pe.matmul(O[:, 0:P], a_t[:, b, :], v_flat[:, bass.ds(h * P + b * (H * P), P)],
                                             start=(b == 0), stop=(b == KT1 - 1))
                        if g == 2:
                            last.then_inc(O_ready, 1)
                    turn(0)
                    turn(1)
                    pe.wait_ge(O_used, s + 1)
                    product(0)
                    turn(2)
                    product(1)
                    product(2)
                pipelined(pe, N, scores, values)

            @block.vector
            def _(dve):
                dve.wait_ge(loaded, 16 * 9)
                for i in range(2):
                    dve.tensor_tensor(lp[:, i, :], lv[:, 2 * i, :], lv[:, 2 * i + 1, :], ALU.mult)
                dve.drain()
                for i in range(2):
                    last = dve.reduce_sum(ls[:, i:i + 1], lp[:, i, :], axis=AX.X)
                last.then_inc(lam_sums, 1)
                for j in range(2 * H):
                    src = q[:, j // 2, :] if j % 2 == 0 else kk[:, j // 2, CTX:T1]
                    dve.wait_ge(rot_ready, j + 1)
                    dve.drain()
                    for b in range(SEQ // BANK):
                        cc = slice(b * BANK, (b + 1) * BANK)
                        dve.tensor_tensor(rot[:, cc], S[0][:, cc], sin[:, cc], ALU.mult)
                    dve.tensor_tensor(src, src, cos[:, :], ALU.mult)
                    dve.drain()
                    dve.tensor_tensor(src, src, rot[:, :], ALU.add).then_inc(rope_done, 1)
                dve.wait_ge(lam_exp, 1)
                dve.scalar_tensor_tensor(neglam[:, :], le[:, 1:2], -LAM_INIT, le[:, 0:1], ALU.add, ALU.subtract)
                dve.drain()
                dve.sem_inc(O_used, 1)

                def maxima(s, par):
                    for i in range(2):
                        dve.wait_ge(S_ready[i], s + 1 + 2 * i)
                        dve.reduce_max(mx[:, par, i:i + 1], S[i][:, 0:T1], axis=AX.X)
                        dve.drain()
                        dve.tensor_scalar(nm[:, par, i:i + 1], mx[:, par, i:i + 1], -SC, None, ALU.mult).then_inc(max_done[i], 1)

                def combine(s, par):
                    dve.wait_ge(exp_done[0], s + 2)
                    dve.wait_ge(exp_done[1], s + 2)
                    dve.reciprocal(rl[:, par, :], l[:, par, :])
                    dve.drain()
                    dve.scalar_tensor_tensor(c[:, par:par + 1], l[:, par, 0:1], neglam[:, :], rl[:, par, 1:2], ALU.mult, ALU.mult)
                    dve.drain()
                    dve.scalar_tensor_tensor(a[:, par, :], p[:, 1, :], c[:, par:par + 1], p[:, 0, :], ALU.mult, ALU.add).then_inc(a_done, 1)

                def first(s, par):
                    maxima(s, par)
                    combine(s, par)

                def second(s, par):
                    dve.wait_ge(O_ready, s + 1)
                    dve.tensor_scalar(o_all[:, :, :].rearrange("p n e -> p (n e)")[:, bass.ds(s * P, P)], O[:, 0:P],
                                      rl[:, par, 0:1], None, ALU.mult).then_inc(O_used, 1)
                pipelined(dve, N, first, second)

            @block.scalar
            def _(act):
                act.wait_ge(lam_sums, 1)
                act.activation(le[:, :], ls[:, :], ACT.Exp).then_inc(lam_exp, 1)
                act.sem_inc(exp_done[0], 1)
                act.sem_inc(exp_done[1], 1)
                act.sem_inc(a_t_done, 1)

                def exp(s, par, i):
                    act.wait_ge(max_done[i], s + 1)
                    if i == 0:
                        act.wait_ge(a_done, s) if not (isinstance(s, int) and s == 0) else None
                    act.activation(p[:, i, :], S[i][:, 0:T1], ACT.Exp, bias=nm[:, par, i:i + 1], scale=SC,
                                   accum_out=l[:, par, i:i + 1]).then_inc(exp_done[i], 1)

                def copies(s):
                    for g, (lo, hi) in enumerate(GROUPS):
                        act.wait_ge(turned_ready, s * 3 + g + 1)
                        if g == 0 and not (isinstance(s, int) and s == 0):
                            act.wait_ge(O_ready, s)
                        act.copy(a_t[:, lo:hi, :], turned[:, 0:(hi - lo) * P].rearrange("p (b q) -> p b q", q=P)).then_inc(a_t_done, 1)
                exp(0, 0, 0)
                exp(0, 0, 1)

                def step(s, par):
                    exp(s + 1, 1 - par, 0)
                    copies(s)
                    exp(s + 1, 1 - par, 1)
                step(0, 0)
                with act.Fori(0, (N - 2) // 2) as i:
                    step(i * 2 + 1, 1)
                    step(i * 2 + 2, 0)
                copies(N - 1)


H2 = 4
NCB = 12
GQ = H2 * P


def short_conv_l2(nc, name, k, x_t, conv_w, out_t):
    PADC = CTX + 2
    LEN = PADC + SEQ + 2
    PIECES = [(a, min(BANK, T1 - a)) for a in range(0, T1, BANK)]
    NORM = 2 * H2
    with Phase(nc, name) as ph:
        w = ph.sb("w", [P, 3, NCB])
        x = ph.sb("x", [P, 2, LEN])
        y = ph.sb("y", [P, 2, LEN])
        act_all = ph.sb("act_all", [P, NCB, T1])
        sq = ph.sb("sq", [P, NORM, T1])
        eps = ph.sb("eps", [P, 1])
        sums = ph.ps("sums", [P, 2, 4 * BANK])
        w_in = ph.sem("w_in")
        x_in = [ph.sem("x_in0"), ph.sem("x_in1")]
        padded = ph.sem("padded")
        y_done = ph.sem("y_done")
        silu_done = ph.sem("silu_done")
        sq_done = ph.sem("sq_done")
        sums_ready = ph.sem("sums_ready")
        log_done = ph.sem("log_done")
        root_done = ph.sem("root_done")
        unit_done = ph.sem("unit_done")
        stored = ph.sem("stored")

        def whole(ap, j):
            return ap[:, bass.ds(j, 1), :].rearrange("p a t -> p (a t)")
        with nc.Block() as block:

            @block.sync
            def _(sp):
                for i in range(3):
                    sp.dma_start(w[:, i, :], columns(conv_w[i]), allow_slow_non_contiguous=True).then_inc(w_in, 16)
                sp.wait_ge(padded, 1)
                with sp.Fori(0, NCB // 2) as i:
                    for half in range(2):
                        j = i * 2 + half
                        sp.wait_ge(y_done, j + 1)
                        rows = x_t[bass.ds(j * P, P), :]
                        sp.dma_start(x[:, half, 1:1 + CTX], rows[:, 0:CTX]).then_inc(x_in[half], 16)
                        sp.dma_start(x[:, half, PADC + 1:PADC + 1 + SEQ], rows[:, CTX:T1]).then_inc(x_in[half], 16)
                with sp.Fori(0, NORM) as j:
                    sp.wait_ge(unit_done, j + 3)
                    sp.dma_start(out_t[bass.ds(j * P, P), :], act_all[:, bass.ds(j, 1), :].rearrange("p a t -> p (a t)")).then_inc(stored, 16)
                sp.dma_start(out_t[NORM * P:NCB * P, :].rearrange("(c p) t -> p c t", p=P), act_all[:, NORM:NCB, :]).then_inc(stored, 16)
                sp.wait_ge(stored, 16 * (NORM + 1))

            @block.vector
            def _(dve):
                for half in range(2):
                    dve.memset(x[:, half, :], 0.0)
                dve.memset(eps[:, :], EPS)
                dve.drain().then_inc(padded, 1)
                dve.sem_inc(y_done, 2)
                dve.wait_ge(w_in, 48)
                with dve.Fori(0, NCB // 2) as i:
                    for half in range(2):
                        j = i * 2 + half
                        n = LEN - 2
                        tap = [w[:, m, bass.ds(j, 1)] for m in range(3)]
                        out = y[:, half, 1:1 + n]
                        dve.wait_ge(x_in[half], i * 32 + 32)
                        dve.wait_ge(silu_done, j + 1)
                        dve.tensor_scalar(out, x[:, half, 0:n], tap[0], None, ALU.mult)
                        dve.drain()
                        dve.scalar_tensor_tensor(out, x[:, half, 1:1 + n], tap[1], out, ALU.mult, ALU.add)
                        dve.drain()
                        dve.scalar_tensor_tensor(out, x[:, half, 2:2 + n], tap[2], out, ALU.mult, ALU.add).then_inc(y_done, 1)
                dve.sem_inc(unit_done, 2)
                for lo, scale in ((0, float(P) ** -0.5), (H2, 1.0)):
                    with dve.Fori(0, H2 // 2) as i:
                        for half in range(2):
                            j = i * 2 + half + lo
                            dve.wait_ge(root_done, j + 1)
                            blk = act_all[:, bass.ds(j, 1), :].rearrange("p a t -> p (a t)")
                            dve.scalar_tensor_tensor(blk, blk, scale, whole(sq, j), ALU.mult, ALU.mult).then_inc(unit_done, 1)

            @block.scalar
            def _(act):
                act.sem_inc(silu_done, 2)

                def silu(j, half):
                    act.wait_ge(y_done, j + 3)
                    blk = whole(act_all, j)
                    act.activation(blk[:, 0:CTX], y[:, half, 1:1 + CTX], ACT.Silu)
                    act.activation(blk[:, CTX:T1], y[:, half, PADC + 1:PADC + 1 + SEQ], ACT.Silu).then_inc(silu_done, 1)
                with act.Fori(0, NCB // 2) as i:
                    for half in range(2):
                        silu(i * 2 + half, half)
                with act.Fori(0, NORM // 2) as i:
                    for half in range(2):
                        j = i * 2 + half
                        act.wait_ge(sums_ready, j + 1)
                        act.activation(whole(sq, j), sums[:, half, 0:T1], ACT.Ln, bias=eps[:, 0:1]).then_inc(log_done, 1)
                with act.Fori(0, NORM) as j:
                    act.wait_ge(log_done, j + 3)
                    act.activation(whole(sq, j), whole(sq, j), ACT.Exp, scale=-0.5).then_inc(root_done, 1)

            @block.gpsimd
            def _(pool):
                with pool.Fori(0, NORM) as j:
                    pool.wait_ge(silu_done, j + 3)
                    pool.tensor_tensor(whole(sq, j), whole(act_all, j), whole(act_all, j), ALU.mult).then_inc(sq_done, 1)

            @block.tensor
            def _(pe):
                pe.sem_inc(log_done, 2)
                with pe.Fori(0, NORM // 2) as i:
                    for half in range(2):
                        j = i * 2 + half
                        pe.wait_ge(sq_done, j + 1)
                        pe.wait_ge(log_done, j + 1)
                        for a, m in PIECES:
                            last = pe.matmul(sums[:, half, a:a + m], k.ones[:, :], whole(sq, j)[:, a:a + m], start=True, stop=True)
                        last.then_inc(sums_ready, 1)


def delta_rule(nc, name, k, g_t, gv, a_log, dt_bias, masks, o_dir):
    NT = T1 // P
    NC = CTX // P
    HW = H2 * P
    DH = 2 * H2
    LV = 7
    with Phase(nc, name) as ph:
        mask = ph.sb("mask", [P, 2, LV * P])
        raw = ph.sb("raw", [P, NT, 2 * DH])
        par = ph.sb("par", [P, 2, DH])
        ea = ph.sb("ea", [P, DH])
        gg = ph.sb("g", [P, NT, DH])
        beta = ph.sb("beta", [P, NT, DH])
        t1 = ph.sb("t1", [P, NT, DH])
        t2 = ph.sb("t2", [P, NT, DH])
        t3 = ph.sb("t3", [P, NT, DH])
        G = ph.sb("G", [P, NT, DH])
        L = ph.sb("L", [P, NT, DH])
        beG = ph.sb("beG", [P, NT, DH])
        kdec = ph.sb("kdec", [P, NT, DH])
        eL = ph.sb("eL", [P, NT, DH])
        B = [[ph.ps(f"b{d}{i}", [P, BANK]) for i in range(4)] for d in range(2)]
        W = []
        for d in range(2):
            W.append({n: ph.sb(f"{n}{d}", [P, HW]) for n in
                      ("gb", "bb", "D", "dec", "eGr", "dm", "Nt", "AQ", "qd", "T", "Tt", "U", "kt", "kbg", "kd", "vt",
                       "vb", "Wt", "u", "o", "S")})
            W[d]["x"] = ph.sb(f"x{d}", [P, NCB, P])
            W[d]["Em"] = ph.sb(f"Em{d}", [P, LV, HW])
        ins_in = ph.sem("ins_in")
        zeroed = ph.sem("zeroed")
        soft = ph.sem("soft")
        gates = ph.sem("gates")
        sums = ph.sem("sums")
        exps = ph.sem("exps")
        vecs = ph.sem("vecs")

        def both(n):
            return [ph.sem(f"{n}{d}") for d in range(2)]
        x_in, bcast, rows, gram, eG, dec = (both(n) for n in ("x_in", "bcast", "rows", "gram", "eG", "dec"))
        D_done, made, kt_ready, kt_copied, vt_ready, vt_copied = (
            both(n) for n in ("D_done", "made", "kt_ready", "kt_copied", "vt_ready", "vt_copied"))
        scaled, em, T_ready, T_copied, U_ready, U_copied = (
            both(n) for n in ("scaled", "em", "T_ready", "T_copied", "U_ready", "U_copied"))
        TET_ready, Tt_done, W_ready, W_copied, u_ready, u_copied = (
            both(n) for n in ("TET_ready", "Tt_done", "W_ready", "W_copied", "u_ready", "u_copied"))
        out_ready, o_copied, S_done, stored = (both(n) for n in ("out_ready", "o_copied", "S_done", "stored"))
        g_v = g_t.rearrange("(c p) t -> p c t", p=P)

        def each_chunk(eng, body):
            for lo, cnt in ((0, NC), (NC, NT - NC)):
                with eng.Fori(0, cnt) as s:
                    body(s + lo, (s + lo, (2 * lo + cnt - 1) - (s + lo)))

        def head(ap, h):
            return ap[:, h * P:(h + 1) * P]

        def heads(ap):
            return ap[:, :].rearrange("p (h m) -> p h m", m=P)

        def of_chunk(ap, t, d):
            return ap[:, bass.ds(t, 1), d * H2:(d + 1) * H2].rearrange("p a h -> p (a h)")
        with nc.Block() as block:

            @block.sync
            def _(sp):
                for d in range(2):
                    sp.dma_start(mask[:, d, :], masks[d]).then_inc(ins_in, 16)
                sp.dma_start(raw[:, :, :], gv.rearrange("(t p) c -> p t c", p=P)).then_inc(ins_in, 16)
                sp.dma_start(par[:, 0, :], on_all(a_log)).then_inc(ins_in, 16)
                sp.dma_start(par[:, 1, :], on_all(dt_bias)).then_inc(ins_in, 16)

                def body(n, tile):
                    for d in range(2):
                        sp.wait_ge(vt_ready[d], n + 1)
                        sp.wait_ge(made[d], n + 1)
                        sp.sem_inc(ph.passed, 1)
                        sp.dma_start(W[d]["x"][:, :, :], g_v[:, :, bass.ds(tile[d] * P, P)]).then_inc(x_in[d], 16)
                each_chunk(sp, body)

            @block.gpsimd
            def _(pool):
                for d in range(2):
                    last = pool.memset(W[d]["S"][:, :], 0.0)
                last.then_inc(zeroed, 1)
                pool.wait_ge(vecs, 1)

                def scale(d, dst, src, by, t):
                    return pool.tensor_tensor(heads(W[d][dst]), heads(W[d][src]),
                                              of_chunk(by, t, d).rearrange("p (h m) -> p h m", m=1).to_broadcast([P, H2, P]), ALU.mult)

                def body(n, tile):
                    for d in range(2):
                        pool.wait_ge(rows[d], n + 1)
                        pool.sem_inc(ph.passed, 1)
                        for dst, src in (("gb", gg), ("bb", beta)):
                            last = pool.tensor_copy(heads(W[d][dst]), of_chunk(src, tile[d], d).rearrange("p (h m) -> p h m", m=1).to_broadcast([P, H2, P]))
                        last.then_inc(bcast[d], 1)
                    for d in range(2):
                        pool.wait_ge(out_ready[d], n + 1)
                        pool.wait_ge(kt_copied[d], n + 1)
                        pool.sem_inc(ph.passed, 1)
                        scale(d, "kbg", "kt", beG, tile[d])
                        scale(d, "kd", "kt", kdec, tile[d])
                        pool.wait_ge(vt_copied[d], n + 1)
                        pool.sem_inc(ph.passed, 1)
                        scale(d, "vb", "vt", beta, tile[d]).then_inc(scaled[d], 1)
                each_chunk(pool, body)

            @block.tensor
            def _(pe):
                pe.wait_ge(gates, 1)
                for d in range(2):
                    pe.matmul(B[d][0][:, 0:NT * H2].rearrange("p (t h) -> p t h", h=H2), k.upto[d], gg[:, :, d * H2:(d + 1) * H2],
                              start=True, stop=True)
                pe.matmul(B[0][1][:, 0:NT * DH], k.ones[:, :], gg[:, :, :].rearrange("p t c -> p (t c)"), start=True, stop=True).then_inc(sums, 1)
                pe.wait_ge(vecs, 1)
                pe.wait_ge(zeroed, 1)
                for d in range(2):
                    for s in (rows, out_ready, vt_ready):
                        pe.sem_inc(s[d], 1)

                def product(bank, lhs, rhs, d, done):
                    for h in range(H2):
                        last = pe.matmul(head(B[d][bank], h), lhs(h), rhs(h), start=True, stop=True)
                    last.then_inc(done, 1)

                def turn(bank, src, d, done):
                    for h in range(H2):
                        last = pe.transpose(head(B[d][bank], h), src(h), k.ident[:, :])
                    last.then_inc(done, 1)

                def body(n, tile):
                    def t(d, name):
                        return lambda h: head(W[d][name], h)

                    def x(d, part):
                        return lambda h: W[d]["x"][:, part * H2 + h, :]
                    for d in range(2):
                        pe.wait_ge(bcast[d], n + 1)
                        pe.wait_ge(o_copied[d], n + 1)
                        for h in range(H2):
                            pe.matmul(head(B[d][0], h), head(W[d]["gb"], h), k.upto[d], start=True, stop=True)
                        product(1, t(d, "bb"), lambda h: k.ident[:, :], d, rows[d])
                    for d in range(2):
                        pe.wait_ge(x_in[d], n * 16 + 16)
                        pe.wait_ge(S_done[d], n + 1)
                        for h in range(H2):
                            pe.matmul(head(B[d][2], h), x(d, 1)(h), x(d, 1)(h), start=True, stop=True)
                        product(3, x(d, 1), x(d, 0), d, gram[d])
                    for d in range(2):
                        pe.wait_ge(eG[d], n + 1)
                        pe.wait_ge(D_done[d], n + 1)
                        turn(0, x(d, 1), d, kt_ready[d])
                    for d in range(2):
                        pe.wait_ge(made[d], n + 2)
                        turn(3, x(d, 2), d, vt_ready[d])
                    for d in range(2):
                        pe.wait_ge(Tt_done[d], n * LV + 1)
                        turn(2, t(d, "Tt"), d, T_ready[d])
                    for lv in range(1, LV):
                        for d in range(2):
                            pe.wait_ge(em[d], n * LV + lv + 1)
                            pe.wait_ge(T_copied[d], n * (LV - 1) + lv)
                            product(1, lambda h: W[d]["Em"][:, lv, h * P:(h + 1) * P], t(d, "T"), d, U_ready[d])
                        for d in range(2):
                            pe.wait_ge(U_copied[d], n * (LV - 1) + lv)
                            product(2, t(d, "U"), t(d, "Tt"), d, TET_ready[d])
                        if lv < LV - 1:
                            for d in range(2):
                                pe.wait_ge(Tt_done[d], n * LV + lv + 1)
                                pe.wait_ge(kt_copied[d], n + 1)
                                turn(0, t(d, "Tt"), d, T_ready[d])
                    for d in range(2):
                        pe.wait_ge(Tt_done[d], n * LV + LV)
                        pe.wait_ge(scaled[d], n + 1)
                        product(1, t(d, "kbg"), t(d, "Tt"), d, W_ready[d])
                    for d in range(2):
                        pe.wait_ge(W_copied[d], n + 1)
                        for h in range(H2):
                            pe.matmul(head(B[d][2], h), head(W[d]["Tt"], h), head(W[d]["vb"], h), start=True, stop=False)
                            last = pe.matmul(head(B[d][2], h), head(W[d]["Wt"], h), head(W[d]["S"], h), start=False, stop=True)
                        last.then_inc(u_ready[d], 1)
                    for d in range(2):
                        pe.wait_ge(u_copied[d], n + 1)
                        pe.wait_ge(T_copied[d], n * (LV - 1) + LV - 1)
                        for h in range(H2):
                            pe.matmul(head(B[d][3], h), head(W[d]["kd"], h), head(W[d]["u"], h), start=True, stop=True)
                        for h in range(H2):
                            pe.matmul(head(B[d][0], h), head(W[d]["qd"], h), head(W[d]["S"], h), start=True, stop=False)
                            last = pe.matmul(head(B[d][0], h), head(W[d]["AQ"], h), head(W[d]["u"], h), start=False, stop=True)
                        last.then_inc(out_ready[d], 1)
                each_chunk(pe, body)

            @block.vector
            def _(dve):
                dve.wait_ge(ins_in, 16 * 5)
                per_chunk = lambda a: a.rearrange("p (t c) -> p t c", t=1).to_broadcast([P, NT, DH])
                dve.tensor_tensor(t1[:, :, :], raw[:, :, 0:DH], per_chunk(par[:, 1, :]), ALU.add)
                dve.drain()
                dve.tensor_scalar(t2[:, :, :], t1[:, :, :], -1.0, None, ALU.mult)
                dve.drain()
                dve.tensor_tensor(t2[:, :, :], t2[:, :, :], t1[:, :, :], ALU.min).then_inc(soft, 1)
                dve.wait_ge(soft, 2)
                dve.tensor_scalar(t1[:, :, :], t1[:, :, :], 0.0, None, ALU.max)
                dve.drain()
                dve.tensor_tensor(t1[:, :, :], t1[:, :, :], t2[:, :, :], ALU.add)
                dve.tensor_scalar(beta[:, :, :], t3[:, :, :], 1.0, None, ALU.add)
                dve.drain()
                dve.reciprocal(beta[:, :, :], beta[:, :, :])
                dve.scalar_tensor_tensor(gg[:, :, :], t1[:, :, :], -1.0, per_chunk(ea[:, :]), ALU.mult, ALU.mult)
                dve.drain().then_inc(gates, 1)
                dve.wait_ge(sums, 1)
                for d in range(2):
                    dve.tensor_copy(G[:, :, d * H2:(d + 1) * H2], B[d][0][:, 0:NT * H2].rearrange("p (t h) -> p t h", h=H2))
                dve.tensor_copy(L[:, :, :], B[0][1][:, 0:NT * DH].rearrange("p (t c) -> p t c", c=DH))
                dve.drain()
                dve.tensor_tensor(kdec[:, :, :], L[:, :, :], G[:, :, :], ALU.subtract)
                dve.drain().then_inc(exps, 1)
                dve.wait_ge(exps, 2)
                dve.tensor_tensor(beG[:, :, :], beG[:, :, :], beta[:, :, :], ALU.mult)
                dve.drain().then_inc(vecs, 1)
                for d in range(2):
                    for s in (made, S_done):
                        dve.sem_inc(s[d], 1)

                def body(n, tile):
                    for d in range(2):
                        w, b = W[d], B[d]
                        dve.wait_ge(rows[d], n + 2)
                        dve.sem_inc(ph.passed, 1)
                        for h in range(H2):
                            last = dve.tensor_scalar(head(w["D"], h), head(b[0], h), of_chunk(G, tile[d], d)[:, h:h + 1], 0.0,
                                                     ALU.subtract, ALU.min)
                        last.then_inc(D_done[d], 1)
                    for d in range(2):
                        w, b = W[d], B[d]
                        m3 = mask[:, d, :].rearrange("p (l m) -> p l m", m=P)
                        dve.wait_ge(dec[d], n + 1)
                        dve.wait_ge(gram[d], n + 1)
                        dve.tensor_tensor(w["dm"][:, :], w["dec"][:, :], b[1][:, :], ALU.mult)
                        dve.tensor_tensor(w["AQ"][:, :], b[3][:, :], w["dec"][:, :], ALU.mult)
                        dve.tensor_tensor(heads(w["qd"]), w["x"][:, 0:H2, :], heads(w["eGr"]), ALU.mult)
                        dve.drain()
                        dve.tensor_tensor(w["Nt"][:, :], b[2][:, :], w["dm"][:, :], ALU.mult)
                        dve.tensor_tensor(heads(w["AQ"]), heads(w["AQ"]), k.upto[d].rearrange("p (h m) -> p h m", h=1).to_broadcast([P, H2, P]), ALU.mult)
                        dve.drain().then_inc(made[d], 1)
                        for lv in range(LV):
                            dve.tensor_tensor(w["Em"][:, lv, :].rearrange("p (h m) -> p h m", m=P), heads(w["Nt"]),
                                              m3[:, lv:lv + 1, :].to_broadcast([P, H2, P]), ALU.mult).then_inc(em[d], 1)
                            if lv == 0:
                                dve.drain()
                                dve.tensor_tensor(heads(w["Tt"]), k.ident[:, :].rearrange("p (h m) -> p h m", h=1).to_broadcast([P, H2, P]),
                                                  w["Em"][:, 0, :].rearrange("p (h m) -> p h m", m=P), ALU.subtract).then_inc(Tt_done[d], 1)
                    for lv in range(1, LV):
                        for d in range(2):
                            dve.wait_ge(TET_ready[d], n * (LV - 1) + lv)
                            dve.tensor_tensor(W[d]["Tt"][:, :], W[d]["Tt"][:, :], B[d][2][:, :], ALU.subtract).then_inc(Tt_done[d], 1)
                    for d in range(2):
                        dve.wait_ge(u_ready[d], n + 1)
                        dve.tensor_copy(W[d]["u"][:, :], B[d][2][:, :]).then_inc(u_copied[d], 1)
                    for d in range(2):
                        dve.wait_ge(out_ready[d], n + 2)
                        for h in range(H2):
                            last = dve.scalar_tensor_tensor(head(W[d]["S"], h), head(W[d]["S"], h), of_chunk(eL, tile[d], d)[:, h:h + 1],
                                                            head(B[d][3], h), ALU.mult, ALU.add)
                        last.then_inc(S_done[d], 1)
                each_chunk(dve, body)

            @block.scalar
            def _(act):
                act.wait_ge(ins_in, 16 * 5)
                act.wait_ge(soft, 1)
                act.activation(t2[:, :, :], t2[:, :, :], ACT.Exp)
                act.activation(t3[:, :, :], raw[:, :, DH:2 * DH], ACT.Exp, scale=-1.0)
                act.activation(ea[:, :], par[:, 0, :], ACT.Exp)
                act.drain()
                act.activation(t2[:, :, :], t2[:, :, :], ACT.Ln, bias=1.0)
                act.drain().then_inc(soft, 1)
                act.wait_ge(exps, 1)
                act.activation(beG[:, :, :], G[:, :, :], ACT.Exp)
                act.activation(kdec[:, :, :], kdec[:, :, :], ACT.Exp)
                act.activation(eL[:, :, :], L[:, :, :], ACT.Exp)
                act.drain().then_inc(exps, 1)
                for d in range(2):
                    act.sem_inc(o_copied[d], 1)
                    act.sem_inc(stored[d], 16)

                def body(n, tile):
                    for d in range(2):
                        w, b = W[d], B[d]
                        act.wait_ge(D_done[d], n + 1)
                        act.wait_ge(made[d], n + 1)
                        act.activation(w["eGr"][:, :], b[0][:, :], ACT.Exp).then_inc(eG[d], 1)
                        act.activation(w["dec"][:, :], w["D"][:, :], ACT.Exp).then_inc(dec[d], 1)
                    for d in range(2):
                        act.wait_ge(kt_ready[d], n + 1)
                        act.copy(W[d]["kt"][:, :], B[d][0][:, :]).then_inc(kt_copied[d], 1)
                    for d in range(2):
                        act.wait_ge(vt_ready[d], n + 2)
                        act.copy(W[d]["vt"][:, :], B[d][3][:, :]).then_inc(vt_copied[d], 1)
                    for d in range(2):
                        act.wait_ge(T_ready[d], n * (LV - 1) + 1)
                        act.copy(W[d]["T"][:, :], B[d][2][:, :]).then_inc(T_copied[d], 1)
                    for lv in range(1, LV):
                        for d in range(2):
                            act.wait_ge(U_ready[d], n * (LV - 1) + lv)
                            act.copy(W[d]["U"][:, :], B[d][1][:, :]).then_inc(U_copied[d], 1)
                        if lv < LV - 1:
                            for d in range(2):
                                act.wait_ge(T_ready[d], n * (LV - 1) + lv + 1)
                                act.copy(W[d]["T"][:, :], B[d][0][:, :]).then_inc(T_copied[d], 1)
                    for d in range(2):
                        act.wait_ge(W_ready[d], n + 1)
                        act.mul(W[d]["Wt"][:, :], B[d][1][:, :], -1.0).then_inc(W_copied[d], 1)
                    for d in range(2):
                        act.wait_ge(out_ready[d], n + 2)
                        act.wait_ge(stored[d], n * 16 + 16)
                        act.copy(W[d]["o"][:, :], B[d][0][:, :]).then_inc(o_copied[d], 1)
                        act.wait_ge(o_copied[d], n + 2)
                        act.dma_start(o_dir[d][bass.ds(tile[d] * P, P), :], W[d]["o"][:, :]).then_inc(stored[d], 16)
                each_chunk(act, body)
                for d in range(2):
                    act.wait_ge(stored[d], 16 * NT + 16)


N_EXP1 = 16
CAP1 = 2 * SEQ // N_EXP1
NT2 = SEQ // P


def mix_norm(nc, name, k, o_da, o_dir, gate, subln_g, gdn_g, mix_t):
    H = HEADS1 + H2
    HW = H * P
    mix_v = mix_t.rearrange("(h p) t -> p h t", p=P)
    with Phase(nc, name) as ph:
        y = ph.sb("y", [P, 2, H, P])
        back = ph.sb("back", [P, 2, H2 * P])
        gt = ph.sb("gt", [P, 2, H2 * P])
        sg = ph.sb("sg", [P, 2, H2 * P])
        sq = ph.sb("sq", [P, H, P])
        ss = ph.sb("ss", [P, 2, H])
        ms = ph.sb("ms", [P, 2, H])
        rstd = ph.sb("rstd", [P, 2, H])
        g = ph.sb("g", [P, 2, P])
        ht = ph.sb("ht", [P, 2, H, P])
        turned = ph.ps("turned", [P, 2, HW])
        g_in = ph.sem("g_in")
        x_in = [ph.sem("x_in0"), ph.sem("x_in1")]
        silu_done = ph.sem("silu_done")
        ss_done = ph.sem("ss_done")
        ms_done = ph.sem("ms_done")
        rstd_done = ph.sem("rstd_done")
        y_done = ph.sem("y_done")
        turned_ready = ph.sem("turned_ready")
        ht_dve = ph.sem("ht_dve")
        ht_act = ph.sem("ht_act")
        stored = [ph.sem("stored0"), ph.sem("stored1")]
        with nc.Block() as block:

            @block.sync
            def _(sp):
                sp.dma_start(g[:, 0, :], on_all(subln_g)).then_inc(g_in, 16)
                sp.dma_start(g[:, 1, :], on_all(gdn_g)).then_inc(g_in, 16)
                with sp.Fori(0, NT2 // 2) as i:
                    for half in range(2):
                        t = i * 2 + half
                        rows = bass.ds(t * P, P)
                        lat = bass.ds(t * P + CTX, P)
                        sp.wait_ge(turned_ready, t + 1)
                        sp.dma_start(y[:, half, 0:HEADS1, :], o_da[rows, :].rearrange("p (h e) -> p h e", e=P)).then_inc(x_in[half], 16)
                        sp.dma_start(y[:, half, HEADS1:H, :], o_dir[0][lat, :].rearrange("p (h e) -> p h e", e=P)).then_inc(x_in[half], 16)
                        sp.dma_start(back[:, half, :], o_dir[1][lat, :]).then_inc(x_in[half], 16)
                        sp.dma_start(gt[:, half, :], gate[lat, :]).then_inc(x_in[half], 16)

            @block.gpsimd
            def _(pool):
                with pool.Fori(0, NT2 // 2) as i:
                    for half in range(2):
                        t = i * 2 + half
                        pool.wait_ge(ss_done, t + 1)
                        pool.sem_inc(ph.passed, 1)
                        pool.tensor_scalar(ms[:, half, :], ss[:, half, :], 1.0 / P, EPS, ALU.mult, ALU.add).then_inc(ms_done, 1)
                        pool.wait_ge(ms_done, t + 1)
                        pool.tensor_tensor(rstd[:, half, :], ms[:, half, :], k.minus_half[:, :].to_broadcast([P, H]), ALU.pow).then_inc(rstd_done, 1)

            @block.vector
            def _(dve):
                dve.sem_inc(ht_dve, 2)
                for half in range(2):
                    dve.sem_inc(stored[half], 16)
                dve.wait_ge(g_in, 32)
                dve.tensor_scalar(g[:, 0, :], g[:, 0, :], 1.0 - LAM_INIT, None, ALU.mult)
                dve.drain()
                with dve.Fori(0, NT2 // 2) as i:
                    for half in range(2):
                        t = i * 2 + half
                        delta = y[:, half, HEADS1:H, :]
                        dve.wait_ge(x_in[half], i * 64 + 64)
                        dve.tensor_tensor(delta, delta, back[:, half, :].rearrange("p (h e) -> p h e", e=P), ALU.add)
                        dve.drain()
                        dve.tensor_tensor(sq[:, :, :], y[:, half], y[:, half], ALU.mult)
                        dve.drain()
                        dve.reduce_sum(ss[:, half, :], sq[:, :, :], axis=AX.X).then_inc(ss_done, 1)
                        dve.wait_ge(rstd_done, t + 1)
                        dve.tensor_tensor(y[:, half], y[:, half], rstd[:, half, :].rearrange("p (h e) -> p h e", e=1).to_broadcast([P, H, P]), ALU.mult)
                        dve.drain()
                        for part in range(2):
                            yy = y[:, half, part * HEADS1:(part + 1) * HEADS1, :]
                            last = dve.tensor_tensor(yy, yy, g[:, part:part + 1, :].to_broadcast([P, HEADS1, P]), ALU.mult)
                        dve.drain()
                        dve.wait_ge(silu_done, t + 1)
                        dve.tensor_tensor(delta, delta, sg[:, half, :].rearrange("p (h e) -> p h e", e=P), ALU.mult)
                        dve.drain().then_inc(y_done, 1)
                        dve.wait_ge(turned_ready, t + 3)
                        dve.wait_ge(stored[half], i * 16 + 16)
                        dve.tensor_copy(ht[:, half, 0:4, :], turned[:, half, 0:4 * P].rearrange("p (h e) -> p h e", e=P)).then_inc(ht_dve, 1)

            @block.scalar
            def _(act):
                act.sem_inc(ht_act, 2)
                with act.Fori(0, NT2 // 2) as i:
                    for half in range(2):
                        t = i * 2 + half
                        act.wait_ge(x_in[half], i * 64 + 64)
                        act.wait_ge(turned_ready, t + 1)
                        act.activation(sg[:, half, :], gt[:, half, :], ACT.Silu).then_inc(silu_done, 1)
                        act.wait_ge(turned_ready, t + 3)
                        act.wait_ge(stored[half], i * 16 + 16)
                        act.copy(ht[:, half, 4:8, :], turned[:, half, 4 * P:8 * P].rearrange("p (h e) -> p h e", e=P)).then_inc(ht_act, 1)
                        act.wait_ge(ht_act, t + 3)
                        act.wait_ge(ht_dve, t + 3)
                        act.dma_start(mix_v[:, :, bass.ds(t * P, P)], ht[:, half]).then_inc(stored[half], 16)
                for half in range(2):
                    act.wait_ge(stored[half], 16 * (NT2 // 2) + 16)

            @block.tensor
            def _(pe):
                pe.sem_inc(turned_ready, 2)
                with pe.Fori(0, NT2 // 2) as i:
                    for half in range(2):
                        t = i * 2 + half
                        pe.wait_ge(y_done, t + 1)
                        pe.wait_ge(ht_dve, t + 1)
                        pe.wait_ge(ht_act, t + 1)
                        for h in range(H):
                            last = pe.transpose(turned[:, half, h * P:(h + 1) * P], y[:, half, h, :], k.ident[:, :])
                        last.then_inc(turned_ready, 1)


def expert_choice(nc, name, k, h_t, w_router, idx_out, gate_out):
    ROUNDS = CAP1 // 8
    with Phase(nc, name) as ph:
        h = ph.sb("h", [P, KD, SEQ])
        w = ph.sb("w", [P, KD, N_EXP1])
        e = ph.sb("e", [P, NT2, N_EXP1])
        m = ph.sb("m", [P, NT2])
        s = ph.sb("s", [P, NT2])
        aff = ph.sb("aff", [N_EXP1, SEQ])
        top = ph.sb("top", [N_EXP1, CAP1])
        idx = ph.sb("idx", [N_EXP1, CAP1], U32)
        logits = ph.ps("logits", [P, BANK])
        aff_t = ph.ps("aff_t", [N_EXP1, 2 * BANK])
        loaded = ph.sem("loaded")
        logits_ready = ph.sem("logits_ready")
        centred = ph.sem("centred")
        exp_done = ph.sem("exp_done")
        soft_done = ph.sem("soft_done")
        aff_ready = ph.sem("aff_ready")
        chosen = ph.sem("chosen")
        stored = ph.sem("stored")
        with nc.Block() as block:

            @block.sync
            def _(sp):
                sp.dma_start(w[:, :, :], w_router.rearrange("(k p) e -> p k e", p=P)).then_inc(loaded, 16)
                for c in range(KD):
                    sp.dma_start(h[:, c, :], h_t[c * P:(c + 1) * P, :]).then_inc(loaded, 16)
                sp.wait_ge(chosen, 1)
                sp.dma_start(idx_out, idx[:, :]).then_inc(stored, 16)
                sp.dma_start(gate_out, top[:, :]).then_inc(stored, 16)
                sp.wait_ge(stored, 32)

            @block.tensor
            def _(pe):
                pe.wait_ge(loaded, 16 * (KD + 1))
                for t in range(NT2):
                    for c in range(KD):
                        last = pe.matmul(logits[:, t * N_EXP1:(t + 1) * N_EXP1], h[:, c, t * P:(t + 1) * P], w[:, c, :],
                                         start=(c == 0), stop=(c == KD - 1))
                last.then_inc(logits_ready, 1)
                pe.wait_ge(soft_done, 1)
                for t in range(NT2):
                    last = pe.transpose(aff_t[:, t * P:(t + 1) * P], e[:, t, :], k.ident[:, :])
                last.then_inc(aff_ready, 1)

            @block.scalar
            def _(act):
                act.wait_ge(centred, 1)
                act.activation(e[:, :, :], e[:, :, :], ACT.Exp).then_inc(exp_done, 1)

            @block.vector
            def _(dve):
                lg = logits[:, 0:NT2 * N_EXP1].rearrange("p (t e) -> p t e", e=N_EXP1)
                wide = lambda a: a[:, :].rearrange("p (t e) -> p t e", e=1).to_broadcast([P, NT2, N_EXP1])
                dve.wait_ge(logits_ready, 1)
                dve.reduce_max(m[:, :], lg, axis=AX.X)
                dve.drain()
                dve.tensor_tensor(e[:, :, :], lg, wide(m), ALU.subtract).then_inc(centred, 1)
                dve.wait_ge(exp_done, 1)
                dve.reduce_sum(s[:, :], e[:, :, :], axis=AX.X)
                dve.drain()
                dve.reciprocal(s[:, :], s[:, :])
                dve.drain()
                dve.tensor_tensor(e[:, :, :], e[:, :, :], wide(s), ALU.mult).then_inc(soft_done, 1)
                dve.wait_ge(aff_ready, 1)
                for b in range(2):
                    dve.tensor_copy(aff[:, b * BANK:(b + 1) * BANK], aff_t[:, b * BANK:(b + 1) * BANK])
                dve.drain()
                for r in range(ROUNDS):
                    at = slice(8 * r, 8 * r + 8)
                    dve.max(top[:, at], aff[:, :])
                    dve.drain()
                    dve.max_index(idx[:, at], top[:, at], aff[:, :])
                    dve.drain()
                    dve.match_replace(aff[:, :], top[:, at], aff[:, :], -1.0)
                    dve.drain()
                dve.sem_inc(chosen, 1)


def experts(nc, name, k, blocks, tok_of, x_n, g, shift, scale, w_gate, w_up, w_down, expert_of=None, first=0,
            used=None, gates=None, acc=None, rows_out=None):
    FF = w_gate.shape[2]
    FH = FF // BANK
    KF = FF // P
    WC = KD * BANK
    NW = 2 * FH + (KF * D) // WC
    DH_ = (KF * D) // WC
    DC = D // DH_
    SETS = 2 if 2 * NW * WC * 4 <= 100 * 1024 else 1
    wg_v = w_gate.rearrange("e (k p) f -> e p k f", p=P)
    wu_v = w_up.rearrange("e (k p) f -> e p k f", p=P)
    wd_v = w_down.rearrange("e (k p) n -> e p k n", p=P)
    with Phase(nc, name) as ph:
        gain = ph.sb("gain", [P, KD])
        sh = ph.sb("sh", [P, KD])
        sc = ph.sb("sc", [P, KD])
        w = [[ph.sb(f"w{i}_{j}", [P, WC]) for j in range(NW)] for i in range(SETS)]
        ib_all = ph.sb("idx_all", [P, blocks], U32)
        gb_all = ph.sb("gates_all", [P, blocks])
        ib = ph.sb("idx", [P, 2], U32)
        ob = ph.sb("out_idx", [P, 2], U32)
        gb = ph.sb("gates", [P, 2])
        xe = ph.sb("xe", [P, 2, D])
        xt = ph.sb("xt", [P, KD, P])
        sg = ph.sb("sg", [P, BANK])
        hid = ph.sb("hid", [P, FF])
        hid_t = ph.sb("hid_t", [P, KF, P])
        y = ph.sb("y", [P, 2, D])
        tab = ph.sb("tab", [1, 64], I32)
        up_ps = [ph.ps(f"up{i}", [P, 2, BANK]) for i in range(FH)]
        t_hid = ph.ps("t_hid", [P, BANK])
        t_x = ph.ps("t_x", [P, BANK])
        y_ps = ph.ps("y_ps", [P, D])
        vecs_in = ph.sem("vecs_in")
        tab_in = ph.sem("tab_in")
        gain_done = ph.sem("gain_done")
        w_in = [[ph.sem(f"w_in{i}_{j}") for j in range(NW)] for i in range(SETS)]
        w_used = [ph.sem(f"w_used{i}") for i in range(NW)]
        idx_in = ph.sem("idx_in")
        copied = ph.sem("copied")
        gates_done = ph.sem("gates_done")
        xe_in = [ph.sem("xe_in0"), ph.sem("xe_in1")]
        x_turned = ph.sem("x_turned")
        xt_done = ph.sem("xt_done")
        silu_done = ph.sem("silu_done")
        hid_done = ph.sem("hid_done")
        hid_turned = ph.sem("hid_turned")
        hid_t_done = ph.sem("hid_t_done")
        y_ready = w_used[NW - 1]
        y_act = ph.sem("y_act")
        y_dve = ph.sem("y_dve")
        stored = ph.sem("stored")
        y_free = ph.sem("y_free")

        def over_blocks(eng, body):
            count = None
            if used is not None:
                eng.wait_ge(tab_in, 16 if expert_of is None else 32)
                count = eng.value_load(tab[0:1, 62:63], min_val=0, max_val=blocks)
            with eng.Fori(0, blocks // 2) as i:
                for par in range(2):
                    b = i * 2 + par
                    if used is None:
                        body(b, i, par)
                    else:
                        with eng.If(b < count):
                            body(b, i, par)

        def over_steps(eng, first_step, step, last_step):
            first_step()
            with eng.Fori(0, blocks // 2 - 1) as i:
                step(i * 2 + 1, i, 1)
                step(i * 2 + 2, i + 1, 0)
            last_step()

        def loaded(b, i, par):
            return (par, i * 16 + 16) if SETS == 2 else (0, b * 16 + 16)
        last_i = blocks // 2 - 1
        with nc.Block() as block:

            @block.sync
            def _(sp):
                for dst, row in ((gain, g), (sh, shift), (sc, scale)):
                    sp.dma_start(dst[:, :], columns(row), allow_slow_non_contiguous=True).then_inc(vecs_in, 16)

                sp.dma_start(ib_all[:, :], tok_of.rearrange("b p -> p b"), allow_slow_non_contiguous=True).then_inc(idx_in, 16)
                if gates is not None:
                    sp.dma_start(gb_all[:, :], gates.rearrange("b p -> p b"), allow_slow_non_contiguous=True).then_inc(idx_in, 16)

                def fill(b, par, j, src, dst):
                    sp.wait_ge(w_used[j], b + 1)
                    sp.sem_inc(ph.passed, 1)
                    sp.dma_start(dst, src).then_inc(w_in[par % SETS][j], 16)

                def fill_up(b, e, par):
                    at = bass.ds(e, 1)
                    for f in range(FH):
                        fc = slice(f * BANK, (f + 1) * BANK)
                        for j, src in ((2 * f, wg_v), (2 * f + 1, wu_v)):
                            fill(b, par, j, src[at, :, :, fc].rearrange("a p k f -> p (a k) f"),
                                 w[par % SETS][j][:, :].rearrange("p (k f) -> p k f", f=BANK))

                def fill_down(b, e, par):
                    at = bass.ds(e, 1)
                    for c in range(DH_):
                        fill(b, par, 2 * FH + c, wd_v[at, :, :, c * DC:(c + 1) * DC].rearrange("a p k n -> p (a k) n"),
                             w[par % SETS][2 * FH + c][:, :].rearrange("p (k n) -> p k n", n=DC))

                def body(b, i, par):
                    e = b
                    if expert_of is not None:
                        e = sp.value_load(tab[0:1, bass.ds(b, 1)], min_val=0, max_val=w_gate.shape[0] - 1)
                    fill_up(b, e, par)
                    fill_down(b, e, par)
                if used is not None or expert_of is not None:
                    if expert_of is not None:
                        sp.dma_start(tab[0:1, 0:blocks], expert_of).then_inc(tab_in, 16)
                        sp.wait_ge(tab_in, 16)
                    if used is not None:
                        sp.dma_start(tab[0:1, 62:63], used).then_inc(tab_in, 16)
                        sp.wait_ge(tab_in, 32)
                if used is not None:
                    over_blocks(sp, body)
                else:
                    def step(b, i, par):
                        fill_up(b, b, par)
                        fill_down(b - 1, b - 1, 1 - par)

                    def last_step():
                        step(blocks - 1, last_i, 1)
                        fill_down(blocks - 1, blocks - 1, 1)
                    over_steps(sp, lambda: fill_up(0, 0, 0), step, last_step)

            @block.gpsimd
            def _(pool):
                pool.wait_ge(idx_in, 32 if gates is not None else 16)

                def gather(b, par):
                    pool.wait_ge(x_turned, 2 * b + 2)
                    pool.sem_inc(ph.passed, 1)
                    pool.tensor_copy(ib[:, par:par + 1], ib_all[:, bass.ds(b, 1)])
                    pool.drain()
                    pool.indirect_dma_start(out=xe[:, par, :], out_offset=None, in_=x_n,
                                            in_offset=bass.IndirectOffsetOnAxis(ap=ib[:, par:par + 1], axis=0)).then_inc(xe_in[par], 16)

                def prepare_store(b, par):
                    if gates is not None:
                        pool.tensor_copy(ob[:, par:par + 1], ib_all[:, bass.ds(b, 1)])
                        pool.tensor_copy(gb[:, par:par + 1], gb_all[:, bass.ds(b, 1)])
                        pool.drain()
                        pool.sem_inc(gates_done, 1)

                def store(b, par):
                    pool.wait_ge(y_act, b + 3)
                    pool.wait_ge(y_dve, b + 3)
                    pool.sem_inc(ph.passed, 1)
                    if acc is not None:
                        pool.indirect_dma_start(out=acc, out_offset=bass.IndirectOffsetOnAxis(ap=ob[:, par:par + 1], axis=0),
                                                in_=y[:, par, :], in_offset=None, compute_op=ALU.add).then_inc(stored, 16)
                    else:
                        pool.dma_start(rows_out[bass.ds((b + first) * P, P), :], y[:, par, :]).then_inc(stored, 16)

                def end_store(b):
                    pool.wait_ge(stored, b * 16 + 16)
                    pool.sem_inc(y_free, 1)
                if used is not None:
                    def body(b, i, par):
                        gather(b, par)
                        prepare_store(b, par)
                        store(b, par)
                        end_store(b)
                    over_blocks(pool, body)
                else:
                    def step(b, par, more=True):
                        if more:
                            gather(b + 2, par)
                        end_store(b - 2)
                        prepare_store(b, par)
                        store(b - 1, 1 - par)
                    gather(0, 0)
                    prepare_store(0, 0)
                    gather(1, 1)
                    gather(2, 0)
                    gather(3, 1)
                    prepare_store(1, 1)
                    store(0, 0)
                    with pool.Fori(1, blocks // 2 - 1) as i:
                        step(i * 2, 0)
                        step(i * 2 + 1, 1)
                    step(blocks - 2, 0, more=False)
                    step(blocks - 1, 1, more=False)
                    end_store(blocks - 2)
                    store(blocks - 1, 1)
                    end_store(blocks - 1)

            @block.tensor
            def _(pe):
                for j in range(NW):
                    pe.sem_inc(w_used[j], SETS)
                pe.sem_inc(x_turned, 4)
                pe.sem_inc(hid_turned, FH)
                pe.sem_inc(y_free, 2)

                def turn_x(b, par, c):
                    pe.wait_ge(xt_done, 2 * b + c + 1)
                    for q in range(4 * c, 4 * c + 4):
                        last = pe.transpose(t_x[:, (q - 4 * c) * P:(q - 4 * c + 1) * P], xe[:, par, q * P:(q + 1) * P], k.ident[:, :])
                    last.then_inc(x_turned, 1)

                def turn_hid(b, f):
                    pe.wait_ge(hid_done, FH * b + f + 1 + FH)
                    pe.wait_ge(hid_t_done, FH * b + f + 1)
                    for q in range(4):
                        last = pe.transpose(t_hid[:, q * P:(q + 1) * P], hid[:, (4 * f + q) * P:(4 * f + q + 1) * P], k.ident[:, :])
                    last.then_inc(hid_turned, 1)

                def up(b, i, par):
                    at, value = loaded(b, i, par)
                    for f in range(FH):
                        pe.wait_ge(hid_done, FH * b + f + 1)
                        for j in range(2):
                            pe.wait_ge(w_in[at][2 * f + j], value)
                            if f == 0 and j == 0:
                                pe.wait_ge(xt_done, 2 * b + 3)
                            for kk in range(KD):
                                last = pe.matmul(up_ps[f][:, j, :], xt[:, kk, :], w[at][2 * f + j][:, kk * BANK:(kk + 1) * BANK],
                                                 start=(kk == 0), stop=(kk == KD - 1))
                            last.then_inc(w_used[2 * f + j], 1)

                def down(b, i, par, between=None):
                    at, value = loaded(b, i, par)
                    pe.wait_ge(y_act, b + 2)
                    pe.wait_ge(y_dve, b + 2)
                    pe.wait_ge(hid_t_done, FH * b + FH + 1)
                    for n in range(0, D, BANK):
                        c, a = n // DC, n % DC
                        if a == 0:
                            pe.wait_ge(w_in[at][2 * FH + c], value)
                        for kk in range(KF):
                            last = pe.matmul(y_ps[:, n:n + BANK], hid_t[:, kk, :],
                                             w[at][2 * FH + c][:, kk * DC + a:kk * DC + a + BANK], start=(kk == 0), stop=(kk == KF - 1))
                        if a + BANK == DC:
                            last.then_inc(w_used[2 * FH + c], 1)
                        if n == 0 and between is not None:
                            between()

                def turn_all_hid(b):
                    for f in range(FH):
                        turn_hid(b, f)

                def turn_x0(b, i, par):
                    pe.wait_ge(xe_in[par], i * 16 + 16)
                    turn_x(b, par, 0)
                if used is not None:
                    def body(b, i, par):
                        turn_x0(b, i, par)
                        turn_x(b, par, 1)
                        up(b, i, par)
                        turn_all_hid(b)
                        down(b, i, par)
                    over_blocks(pe, body)
                else:
                    def first_step():
                        turn_x0(0, 0, 0)
                        turn_x(0, 0, 1)
                        up(0, 0, 0)
                        turn_x0(1, 0, 1)
                        turn_x(1, 1, 1)
                        turn_all_hid(0)

                    def step(b, i, par):
                        before, after = (i, i + 1) if par else (i - 1, i)
                        up(b, i, par)
                        turn_x0(b + 1, after, 1 - par)
                        down(b - 1, before, 1 - par, lambda: turn_x(b + 1, 1 - par, 1))
                        turn_all_hid(b)

                    def last_step():
                        up(blocks - 1, last_i, 1)
                        down(blocks - 2, last_i, 0)
                        turn_all_hid(blocks - 1)
                        down(blocks - 1, last_i, 1)
                    over_steps(pe, first_step, step, last_step)

            @block.scalar
            def _(act):
                act.sem_inc(hid_t_done, 1)
                act.sem_inc(y_act, 2)

                def silu(b):
                    for f in range(FH):
                        act.wait_ge(w_used[2 * f], b + 1 + SETS)
                        act.wait_ge(hid_done, FH * b + f + FH)
                        act.activation(sg[:, :], up_ps[f][:, 0, :], ACT.Silu).then_inc(silu_done, 1)

                def copy_hid(b):
                    act.wait_ge(y_ready, b + SETS)
                    for f in range(FH):
                        act.wait_ge(hid_turned, FH * b + f + 1 + FH)
                        act.copy(hid_t[:, 4 * f:4 * f + 4, :], t_hid[:, :].rearrange("p (k t) -> p k t", t=P)).then_inc(hid_t_done, 1)

                def result(b, par):
                    act.wait_ge(y_ready, b + 1 + SETS)
                    act.wait_ge(y_free, b + 1)
                    scale_ = 1.0
                    if gates is not None:
                        act.wait_ge(gates_done, b + 1)
                        scale_ = gb[:, par:par + 1]
                    act.activation(y[:, par, 0:BANK], y_ps[:, 0:BANK], ACT.Copy, scale=scale_).then_inc(y_act, 1)
                if used is not None:
                    def body(b, i, par):
                        silu(b)
                        copy_hid(b)
                        result(b, par)
                    over_blocks(act, body)
                else:
                    def first_step():
                        silu(0)
                        copy_hid(0)

                    def step(b, i, par):
                        silu(b)
                        result(b - 1, 1 - par)
                        copy_hid(b)

                    def last_step():
                        step(blocks - 1, last_i, 1)
                        result(blocks - 1, 1)
                    over_steps(act, first_step, step, last_step)

            @block.vector
            def _(dve):
                dve.wait_ge(vecs_in, 48)
                dve.scalar_tensor_tensor(gain[:, :], sc[:, :], 1.0, gain[:, :], ALU.add, ALU.mult)
                dve.drain()
                dve.sem_inc(xt_done, 1)
                dve.sem_inc(hid_done, FH)
                dve.sem_inc(y_dve, 2)

                def modulate(b):
                    dve.wait_ge(w_used[2 * FH - 1], b + SETS)
                    for c in range(2):
                        dve.wait_ge(x_turned, 2 * b + c + 5)
                        for q in range(4):
                            kk = 4 * c + q
                            last = dve.tensor_scalar(xt[:, kk, :], t_x[:, q * P:(q + 1) * P], gain[:, kk:kk + 1], sh[:, kk:kk + 1], ALU.mult, ALU.add)
                        last.then_inc(xt_done, 1)

                def products(b):
                    for f in range(FH):
                        dve.wait_ge(silu_done, FH * b + f + 1)
                        dve.wait_ge(w_used[2 * f + 1], b + 1 + SETS)
                        dve.wait_ge(hid_turned, FH * b + f + 1)
                        dve.tensor_tensor(hid[:, f * BANK:(f + 1) * BANK], up_ps[f][:, 1, :], sg[:, :], ALU.mult).then_inc(hid_done, 1)

                def result(b, par):
                    dve.wait_ge(y_ready, b + 1 + SETS)
                    dve.wait_ge(y_free, b + 1)
                    out = y[:, par, BANK:D]
                    if gates is not None:
                        dve.wait_ge(gates_done, b + 1)
                        dve.tensor_scalar(out, y_ps[:, BANK:D], gb[:, par:par + 1], None, ALU.mult).then_inc(y_dve, 1)
                    else:
                        dve.tensor_copy(out, y_ps[:, BANK:D]).then_inc(y_dve, 1)
                if used is not None:
                    def body(b, i, par):
                        modulate(b)
                        products(b)
                        result(b, par)
                    over_blocks(dve, body)
                else:
                    def first_step():
                        modulate(0)
                        products(0)
                        modulate(1)

                    def step(b, i, par):
                        products(b)
                        modulate(b + 1)
                        result(b - 1, 1 - par)

                    def last_step():
                        products(blocks - 1)
                        result(blocks - 2, 0)
                        result(blocks - 1, 1)
                    over_steps(dve, first_step, step, last_step)


def finish(nc, name, k, x1, gain, g, out, acc=None, rows=None, dest=None, gates=None):
    with Phase(nc, name) as ph:
        gn = ph.sb("gain", [P, D])
        gg = ph.sb("g", [P, D])
        x = ph.sb("x", [P, 2, D])
        m = ph.sb("m", [P, 2, D])
        m2 = ph.sb("m2", [P, 2, D])
        sq = ph.sb("sq", [P, D])
        ss = ph.sb("ss", [P, 2])
        ms = ph.sb("ms", [P, 2])
        rstd = ph.sb("rstd", [P, 2])
        o = ph.sb("o", [P, 2, D])
        dst = ph.sb("dest", [P, 2 * NT2], U32)
        gt = ph.sb("gates", [P, 2 * NT2])
        ib = ph.sb("ib", [P, 4], U32)
        rows_in = ph.sem("rows_in")
        x_in = [ph.sem("x_in0"), ph.sem("x_in1")]
        m_in = [ph.sem("m_in0"), ph.sem("m_in1")]
        ib_done = ph.sem("ib_done")
        x_done = ph.sem("x_done")
        sq_done = ph.sem("sq_done")
        ms_done = ph.sem("ms_done")
        rstd_done = ph.sem("rstd_done")
        o_done = ph.sem("o_done")
        stored = [ph.sem("stored0"), ph.sem("stored1")]
        M_IN = 16 if acc is not None else 32
        with nc.Block() as block:

            @block.sync
            def _(sp):
                sp.dma_start(gn[:, :], on_all(gain)).then_inc(rows_in, 16)
                sp.dma_start(gg[:, :], on_all(g)).then_inc(rows_in, 16)
                if acc is None:
                    sp.dma_start(dst[:, :], dest).then_inc(rows_in, 16)
                    sp.dma_start(gt[:, :], gates).then_inc(rows_in, 16)
                with sp.Fori(0, NT2 // 2) as i:
                    for half in range(2):
                        t = i * 2 + half
                        sp.wait_ge(o_done, t + 1)
                        sp.dma_start(x[:, half, :], x1[bass.ds(t * P, P), :]).then_inc(x_in[half], 16)
                        if acc is not None:
                            sp.dma_start(m[:, half, :], acc[bass.ds(t * P, P), :]).then_inc(m_in[half], 16)

            @block.gpsimd
            def _(pool):
                if acc is None:
                    pool.wait_ge(rows_in, 64)

                def gather(t, half):
                    pool.wait_ge(o_done, t + 1)
                    for c in range(2):
                        last = pool.tensor_copy(ib[:, 2 * half + c:2 * half + c + 1], dst[:, bass.ds(t * 2 + c, 1)])
                    last.then_inc(ib_done, 1)
                    pool.wait_ge(ib_done, t + 1)
                    pool.sem_inc(ph.passed, 1)
                    for c, buf in enumerate((m, m2)):
                        pool.indirect_dma_start(out=buf[:, half, :], out_offset=None, in_=rows,
                                                in_offset=bass.IndirectOffsetOnAxis(ap=ib[:, 2 * half + c:2 * half + c + 1], axis=0)).then_inc(m_in[half], 16)
                with pool.Fori(0, NT2 // 2) as i:
                    if acc is None:
                        for half in range(2):
                            gather(i * 2 + half, half)
                    for half in range(2):
                        t = i * 2 + half
                        pool.wait_ge(sq_done, t + 1)
                        pool.sem_inc(ph.passed, 1)
                        pool.tensor_scalar(ms[:, half:half + 1], ss[:, half:half + 1], 1.0 / D, EPS, ALU.mult, ALU.add).then_inc(ms_done, 1)
                        pool.wait_ge(ms_done, t + 1)
                        pool.tensor_tensor(rstd[:, half:half + 1], ms[:, half:half + 1], k.minus_half[:, :], ALU.pow).then_inc(rstd_done, 1)

            @block.scalar
            def _(act):
                with act.Fori(0, NT2 // 2) as i:
                    for half in range(2):
                        t = i * 2 + half
                        act.wait_ge(x_done, t + 1)
                        act.wait_ge(o_done, t + 1)
                        act.activation(sq[:, :], x[:, half, :], ACT.Square, accum_out=ss[:, half:half + 1]).then_inc(sq_done, 1)
                        act.wait_ge(o_done, t + 3)
                        act.dma_start(out[bass.ds(t * P, P), :], o[:, half, :]).then_inc(stored[half], 16)
                for half in range(2):
                    act.wait_ge(stored[half], 16 * (NT2 // 2) + 16)

            @block.vector
            def _(dve):
                dve.sem_inc(o_done, 2)
                for half in range(2):
                    dve.sem_inc(stored[half], 16)
                dve.wait_ge(rows_in, 32 if acc is not None else 64)
                with dve.Fori(0, NT2 // 2) as i:
                    for half in range(2):
                        t = i * 2 + half
                        dve.wait_ge(x_in[half], i * 16 + 16)
                        dve.wait_ge(m_in[half], i * M_IN + M_IN)
                        if acc is None:
                            dve.tensor_scalar(m[:, half, :], m[:, half, :], gt[:, bass.ds(t * 2, 1)], None, ALU.mult)
                            dve.drain()
                            dve.scalar_tensor_tensor(m[:, half, :], m2[:, half, :], gt[:, bass.ds(t * 2 + 1, 1)], m[:, half, :], ALU.mult, ALU.add)
                            dve.drain()
                        dve.tensor_tensor(m[:, half, :], m[:, half, :], gn[:, :], ALU.mult)
                        dve.drain()
                        dve.tensor_tensor(x[:, half, :], x[:, half, :], m[:, half, :], ALU.add).then_inc(x_done, 1)
                        dve.wait_ge(rstd_done, t + 1)
                        dve.wait_ge(stored[half], i * 16 + 16)
                        dve.scalar_tensor_tensor(o[:, half, :], x[:, half, :], rstd[:, half:half + 1], gg[:, :], ALU.mult, ALU.mult).then_inc(o_done, 1)


D_RNN = 1280
RB = D_RNN // P
LRU_C = 8.0
HEADS2 = 8
KV_RANK = 256
IDX_H = 8
IDX_D = 64
TOPK = 256
IDX_SCALE = IDX_D ** -0.5 * IDX_H ** -0.5
ATT_SCALE = float(P) ** -0.5
STRUCK = -3.0e38


def rg_lru(nc, name, k, x_t, gr_t, conv_w, conv_b, w_a, b_a, w_x, b_x, lam, y_t):
    TAPS = conv_w.shape[0]
    PAD = TAPS - 1
    with Phase(nc, name) as ph:
        cw = ph.sb("cw", [P, TAPS, RB])
        vec = {n: ph.sb(n, [P, RB]) for n in ("cb", "ba", "bx", "lam", "e", "hs")}
        x = ph.sb("x", [P, 2, PAD + SEQ])
        xc = ph.sb("xc", [P, 2, SEQ])
        wa = ph.sb("wa", [P, 2, P])
        wx = ph.sb("wx", [P, 2, P])
        tr = ph.sb("tr", [P, 2, SEQ])
        gel = ph.sb("gelu", [P, RB, SEQ])
        a = ph.sb("a", [P, RB, SEQ])
        th = ph.sb("th", [P, RB, SEQ])
        ix = ph.sb("ix", [P, RB, SEQ])
        r_ps = ph.ps("r", [P, 2, SEQ])
        i_ps = ph.ps("i", [P, 2, SEQ])
        vecs_in = ph.sem("vecs_in")
        gr_in = ph.sem("gr_in")
        padded = ph.sem("padded")
        soft = ph.sem("soft")
        x_in = [ph.sem("x_in0"), ph.sem("x_in1")]
        conv_done = ph.sem("conv_done")
        gates_ready = ph.sem("gates_ready")
        tanh_done = ph.sem("tanh_done")
        s_done = ph.sem("s_done")
        ix_done = ph.sem("ix_done")
        a_done = ph.sem("a_done")
        root_done = ph.sem("root_done")
        y_done = ph.sem("y_done")
        stored = ph.sem("stored")

        def blk(ap, j):
            return ap[:, bass.ds(j, 1), :].rearrange("p a t -> p (a t)")
        with nc.Block() as block:

            @block.sync
            def _(sp):
                for i in range(TAPS):
                    sp.dma_start(cw[:, i, :], columns(conv_w[i]), allow_slow_non_contiguous=True).then_inc(vecs_in, 16)
                for n, row in (("cb", conv_b), ("ba", b_a), ("bx", b_x), ("lam", lam)):
                    sp.dma_start(vec[n][:, :], columns(row), allow_slow_non_contiguous=True).then_inc(vecs_in, 16)
                sp.dma_start(gel[:, :, :], gr_t.rearrange("(c p) t -> p c t", p=P)).then_inc(gr_in, 16)
                sp.wait_ge(padded, 1)
                with sp.Fori(0, RB // 2) as i:
                    for par in range(2):
                        j = i * 2 + par
                        sp.wait_ge(ix_done, j + 1)
                        sp.dma_start(x[:, par, PAD:PAD + SEQ], x_t[bass.ds(j * P, P), :]).then_inc(x_in[par], 16)
                        sp.dma_start(wa[:, par, :], w_a[bass.ds(j, 1)].rearrange("a c d -> c (a d)")).then_inc(x_in[par], 16)
                        sp.dma_start(wx[:, par, :], w_x[bass.ds(j, 1)].rearrange("a c d -> c (a d)")).then_inc(x_in[par], 16)
                with sp.Fori(0, RB) as j:
                    sp.wait_ge(y_done, j + 1)
                    sp.dma_start(y_t[bass.ds(j * P, P), :], blk(ix, j)).then_inc(stored, 16)
                sp.wait_ge(stored, 16 * RB)

            @block.vector
            def _(dve):
                for par in range(2):
                    dve.memset(x[:, par, 0:PAD], 0.0)
                dve.drain().then_inc(padded, 1)
                dve.sem_inc(ix_done, 2)
                dve.wait_ge(vecs_in, 16 * (TAPS + 4))
                dve.tensor_scalar(vec["e"][:, :], vec["lam"][:, :], -1.0, None, ALU.mult)
                dve.tensor_scalar(vec["ba"][:, :], vec["ba"][:, :], 0.5, None, ALU.mult)
                dve.tensor_scalar(vec["bx"][:, :], vec["bx"][:, :], 0.5, None, ALU.mult)
                dve.drain()
                dve.tensor_scalar(vec["hs"][:, :], vec["e"][:, :], 0.0, None, ALU.max)
                dve.tensor_tensor(vec["e"][:, :], vec["e"][:, :], vec["lam"][:, :], ALU.min)
                dve.drain().then_inc(soft, 1)
                dve.wait_ge(soft, 2)
                dve.tensor_tensor(vec["hs"][:, :], vec["hs"][:, :], vec["e"][:, :], ALU.add)
                dve.drain()
                dve.tensor_scalar(vec["hs"][:, :], vec["hs"][:, :], LRU_C / 2, None, ALU.mult)
                dve.drain()
                with dve.Fori(0, RB // 2) as i:
                    for par in range(2):
                        j = i * 2 + par
                        tap = [cw[:, m, bass.ds(j, 1)] for m in range(TAPS)]
                        hs = vec["hs"][:, bass.ds(j, 1)]
                        dve.wait_ge(x_in[par], i * 48 + 48)
                        dve.tensor_scalar(xc[:, par, :], x[:, par, 0:SEQ], tap[0], vec["cb"][:, bass.ds(j, 1)], ALU.mult, ALU.add)
                        dve.drain()
                        for m in range(1, TAPS):
                            dve.scalar_tensor_tensor(xc[:, par, :], x[:, par, m:m + SEQ], tap[m], xc[:, par, :], ALU.mult, ALU.add)
                            dve.drain()
                        dve.sem_inc(conv_done, 1)
                        dve.wait_ge(tanh_done, j + 1)
                        dve.tensor_scalar(blk(th, j), tr[:, par, :], hs, hs, ALU.mult, ALU.add).then_inc(s_done, 1)
                        dve.scalar_tensor_tensor(blk(ix, j), blk(ix, j), 1.0, xc[:, par, :], ALU.add, ALU.mult).then_inc(ix_done, 1)
                with dve.Fori(0, RB) as j:
                    dve.wait_ge(root_done, j + 1)
                    dve.scalar_tensor_tensor(blk(th, j), blk(a, j), 1.0, blk(th, j), ALU.add, ALU.mult)
                    dve.drain()
                    dve.scalar_tensor_tensor(blk(ix, j), blk(ix, j), 0.5, blk(th, j), ALU.mult, ALU.mult)
                    dve.drain()
                    dve.tensor_tensor_scan(blk(th, j), blk(a, j), blk(ix, j), 0.0, ALU.mult, ALU.add)
                    dve.drain()
                    dve.tensor_tensor(blk(ix, j), blk(th, j), blk(gel, j), ALU.mult).then_inc(y_done, 1)

            @block.tensor
            def _(pe):
                with pe.Fori(0, RB // 2) as i:
                    for par in range(2):
                        j = i * 2 + par
                        pe.wait_ge(conv_done, j + 1)
                        pe.wait_ge(ix_done, j + 1)
                        for ps, wt in ((r_ps, wa), (i_ps, wx)):
                            for b in range(0, SEQ, BANK):
                                last = pe.matmul(ps[:, par, b:b + BANK], wt[:, par, :], xc[:, par, b:b + BANK], start=True, stop=True)
                        last.then_inc(gates_ready, 1)

            @block.scalar
            def _(act):
                act.wait_ge(gr_in, 16)
                act.activation(gel[:, :, :], gel[:, :, :], ACT.Gelu_apprx_tanh)
                act.wait_ge(soft, 1)
                act.activation(vec["e"][:, :], vec["e"][:, :], ACT.Exp)
                act.drain()
                act.activation(vec["e"][:, :], vec["e"][:, :], ACT.Ln, bias=1.0)
                act.drain().then_inc(soft, 1)
                with act.Fori(0, RB // 2) as i:
                    for par in range(2):
                        j = i * 2 + par
                        act.wait_ge(gates_ready, j + 1)
                        act.activation(tr[:, par, :], r_ps[:, par, :], ACT.Tanh, bias=vec["ba"][:, bass.ds(j, 1)], scale=0.5)
                        act.activation(blk(ix, j), i_ps[:, par, :], ACT.Tanh, bias=vec["bx"][:, bass.ds(j, 1)], scale=0.5).then_inc(tanh_done, 1)
                        act.wait_ge(s_done, j + 1)
                        act.activation(blk(a, j), blk(th, j), ACT.Exp, scale=-1.0)
                        act.drain()
                        act.activation(blk(th, j), blk(th, j), ACT.Tanh, scale=0.5).then_inc(a_done, 1)
                act.wait_ge(a_done, RB)
                with act.Fori(0, RB) as j:
                    act.activation(blk(th, j), blk(th, j), ACT.Sqrt).then_inc(root_done, 1)


def kv_norm(nc, name, k, c_t, g, out_t):
    R = KV_RANK // P
    with Phase(nc, name) as ph:
        c = ph.sb("c", [P, R, SEQ])
        sq = ph.sb("sq", [P, R, SEQ])
        root = ph.sb("root", [P, SEQ])
        gg = ph.sb("g", [P, R])
        eps = ph.sb("eps", [P, 1])
        sums = ph.ps("sums", [P, SEQ])
        loaded = ph.sem("loaded")
        sq_done = ph.sem("sq_done")
        sums_ready = ph.sem("sums_ready")
        root_done = ph.sem("root_done")
        done = ph.sem("done")
        stored = ph.sem("stored")
        with nc.Block() as block:

            @block.sync
            def _(sp):
                sp.dma_start(c[:, :, :], c_t.rearrange("(r p) t -> p r t", p=P)).then_inc(loaded, 16)
                sp.dma_start(gg[:, :], columns(g), allow_slow_non_contiguous=True).then_inc(loaded, 16)
                sp.wait_ge(done, 1)
                sp.dma_start(out_t.rearrange("(r p) t -> p r t", p=P), c[:, :, :]).then_inc(stored, 16)
                sp.wait_ge(stored, 16)

            @block.vector
            def _(dve):
                dve.memset(eps[:, :], EPS)
                dve.wait_ge(loaded, 32)
                dve.tensor_tensor(sq[:, :, :], c[:, :, :], c[:, :, :], ALU.mult)
                dve.drain().then_inc(sq_done, 1)
                dve.wait_ge(root_done, 1)
                dve.reciprocal(root[:, :], root[:, :])
                dve.drain()
                for r in range(R):
                    dve.scalar_tensor_tensor(c[:, r, :], c[:, r, :], gg[:, r:r + 1], root[:, :], ALU.mult, ALU.mult)
                dve.drain().then_inc(done, 1)

            @block.tensor
            def _(pe):
                pe.wait_ge(sq_done, 1)
                for b in range(0, SEQ, BANK):
                    for r in range(R):
                        last = pe.matmul(sums[:, b:b + BANK], k.ones[:, :], sq[:, r, b:b + BANK], start=(r == 0), stop=(r == R - 1))
                last.then_inc(sums_ready, 1)

            @block.scalar
            def _(act):
                act.wait_ge(sums_ready, 1)
                act.activation(root[:, :], sums[:, :], ACT.Sqrt, bias=eps[:, 0:1], scale=1.0 / KV_RANK).then_inc(root_done, 1)


def sparse_attention(nc, name, k, q_t, k_t, v, qi_t, kw, dist, causal, slopes, att_t):
    H = HEADS2
    assert IDX_H == H and TOPK % (8 * H) == 0 and TOPK == 2 * P
    FIRST = TOPK // P
    ROUNDS = TOPK // (8 * H)
    with Phase(nc, name) as ph:
        kk = ph.sb("k", [P, H, SEQ])
        vv = ph.sb("v", [P, NT2, H * P])
        sl = ph.sb("sl", [P, H])
        q = ph.sb("q", [P, 2, H, P])
        kwt = ph.sb("kw", [P, NT2, IDX_D + IDX_H])
        kk2 = ph.sb("kk2", [P, NT2, 2, IDX_D])
        wi = ph.sb("wi", [P, NT2, IDX_H])
        ki = ph.sb("ki", [P, SEQ])
        qi = ph.sb("qi", [P, 2, IDX_H // 2, P])
        dn = ph.sb("dn", [P, SEQ])
        cm = ph.sb("cm", [P, P])
        rel = ph.sb("rel", [P, 2, SEQ])
        score = ph.sb("score", [P, 2, SEQ])
        top = ph.sb("top", [P, 8])
        dm = ph.sb("dm", [P, 2, SEQ])
        bias = ph.sb("bias", [P, 2, SEQ])
        X = ph.sb("X", [P, 2, SEQ])
        p = ph.sb("p", [P, 2, SEQ])
        p_t = ph.sb("p_t", [P, NT2, P])
        mx = ph.sb("mx", [P, 2])
        nm = ph.sb("nm", [P, 2])
        l = ph.sb("l", [P, 2])
        rl = ph.sb("rl", [P, 2])
        o = ph.sb("o", [P, H, P])
        ot = ph.sb("ot", [P, 2, H, P])
        S = ph.ps("S", [P, 2, SEQ])
        T = ph.ps("T", [P, 2, BANK])
        O = ph.ps("O", [P, BANK])
        IS = ph.ps("IS", [P, BANK])
        small_in = ph.sem("small_in")
        loaded = ph.sem("loaded")
        tile_in = [ph.sem("tile_in0"), ph.sem("tile_in1")]
        qi_in = [ph.sem("qi_in0"), ph.sem("qi_in1")]
        kk2_done = ph.sem("kk2_done")
        ki_turned = ph.sem("ki_turned")
        ki_done = ph.sem("ki_done")
        IS_ready = ph.sem("IS_ready")
        rel_done = ph.sem("rel_done")
        score_done = ph.sem("score_done")
        dm_done = ph.sem("dm_done")
        head_in = ph.sem("head_in")
        S_ready = ph.sem("S_ready")
        X_done = ph.sem("X_done")
        max_done = ph.sem("max_done")
        p_done = ph.sem("p_done")
        turned = ph.sem("turned")
        copied = ph.sem("copied")
        O_ready = ph.sem("O_ready")
        o_done = ph.sem("o_done")
        o_turned = ph.sem("o_turned")
        ot_done = ph.sem("ot_done")
        stored = [ph.sem("stored0"), ph.sem("stored1")]
        att_v = att_t.rearrange("(h p) t -> p h t", p=P)
        groups = [[(a, min(a + 4, t + 1)) for a in range(0, t + 1, 4)] for t in range(NT2)]
        before = [H * sum(len(g) for g in groups[:t]) + 2 * t for t in range(NT2 + 1)]
        banks = [[(a, min(a + BANK, (t + 1 + FIRST) * P)) for a in range(0, (t + 1 + FIRST) * P, BANK)] if t + FIRST < NT2 else []
                 for t in range(NT2)]
        banks_before = [H * sum(len(g) for g in banks[:t]) for t in range(NT2)]

        def over_heads(eng, first, second, beside=None, between=None, before_first=None):
            def step(h, par, more=True):
                if before_first is not None:
                    before_first(h, par)
                if more:
                    first(h + 1, 1 - par)
                if between is not None:
                    between()
                second(h, par)
                if beside is not None:
                    beside(h, par)
            first(0, 0)
            for h in range(H):
                step(h, h % 2, more=h < H - 1)
        with nc.Block() as block:

            @block.sync
            def _(sp):
                sp.dma_start(kwt[:, :, :], kw.rearrange("(t p) c -> p t c", p=P)).then_inc(small_in, 16)
                sp.dma_start(dn[:, :], dist).then_inc(small_in, 16)
                sp.dma_start(cm[:, :], causal).then_inc(small_in, 16)
                sp.dma_start(sl[:, :], slopes).then_inc(loaded, 16)
                sp.dma_start(kk[:, :, :], k_t.rearrange("(h p) t -> p h t", p=P)).then_inc(loaded, 16)
                sp.dma_start(vv[:, :, :], v.rearrange("(t p) e -> p t e", p=P)).then_inc(loaded, 16)

                def load(t):
                    sp.dma_start(q[:, t % 2], q_t[:, t * P:(t + 1) * P].rearrange("(h p) t -> p h t", p=P)).then_inc(tile_in[t % 2], 16)

                def load_index(t):
                    sp.dma_start(qi[:, t % 2], qi_t[:, t * P:(t + 1) * P].rearrange("(c p) t -> p c t", p=P)).then_inc(qi_in[t % 2], 16)
                for t in range(2):
                    load(t)
                    load_index(t + FIRST)
                for t in range(NT2):
                    if t < NT2 - 2:
                        sp.wait_ge(S_ready, H * (t + 1))
                        load(t + 2)
                    if t + 2 + FIRST < NT2:
                        sp.wait_ge(IS_ready, banks_before[t] + H * len(banks[t]))
                        load_index(t + 2 + FIRST)
                    sp.wait_ge(ot_done, 2 * t + 2)
                    sp.dma_start(att_v[:, :, t * P:(t + 1) * P], ot[:, t % 2]).then_inc(stored[t % 2], 16)
                for par in range(2):
                    sp.wait_ge(stored[par], 16 * NT2 // 2)

            @block.gpsimd
            def _(pool):
                pool.wait_ge(loaded, 48)
                for t in range(NT2):
                    W = (t + 1) * P
                    pool.wait_ge(dm_done, t + 1)
                    for h in range(H):
                        pool.wait_ge(X_done, h + t * H + 1)
                        pool.tensor_scalar(bias[:, h % 2, 0:W], dm[:, t % 2, 0:W], sl[:, h:h + 1], None, ALU.mult).then_inc(head_in, 1)

            @block.tensor
            def _(pe):
                pe.sem_inc(X_done, 2)
                pe.wait_ge(kk2_done, 1)
                for t in range(NT2):
                    last = pe.transpose(S[:, 0, t * P:(t + 1) * P], kk2[:, t].rearrange("p a c -> p (a c)"), k.ident[:, :])
                last.then_inc(ki_turned, 1)
                pe.wait_ge(ki_done, 1)
                pe.wait_ge(loaded, 48)
                for t in range(NT2):
                    W = (t + 1) * P
                    g = groups[t]
                    pe.wait_ge(tile_in[t % 2], 16 * (t // 2 + 1))

                    def scores(h, par):
                        n = h + t * H
                        pe.wait_ge(X_done, n + 1)
                        for b in range(0, W, BANK):
                            e = min(W, b + BANK)
                            last = pe.matmul(S[:, par, b:e], q[:, t % 2, h, :], kk[:, h, b:e], start=True, stop=True)
                        last.then_inc(S_ready, 1)

                    def index_scores(h, par, parts, j0):
                        rows = slice(IDX_D * par, IDX_D * par + IDX_D)
                        for j, (lo, hi) in enumerate(parts, j0):
                            if h == 0 and j == 0:
                                pe.wait_ge(qi_in[t % 2], 16 * (t // 2 + 1))
                            pe.wait_ge(rel_done, h * len(banks[t]) + (banks_before[t] + j + 1))
                            pe.matmul(IS[:, 0:hi - lo], qi[rows, t % 2, h // 2, :], ki[rows, lo:hi], start=True, stop=True).then_inc(IS_ready, 1)

                    def values(h, par):
                        n = h + t * H
                        pe.wait_ge(p_done, n + 1)
                        for j, (lo, hi) in enumerate(g):
                            pe.wait_ge(copied, h * len(g) + (before[t] + j + 1))
                            for b in range(lo, hi):
                                last = pe.transpose(T[:, j % 2, (b - lo) * P:(b - lo + 1) * P], p[:, par, b * P:(b + 1) * P], k.ident[:, :])
                            last.then_inc(turned, 1)
                        index_scores(h, par, banks[t][:1], 0)
                        pe.wait_ge(o_done, n + 1)
                        for j, (lo, hi) in enumerate(g):
                            pe.wait_ge(copied, h * len(g) + (before[t] + j + 3))
                            for b in range(lo, hi):
                                last = pe.matmul(O[:, 0:P], p_t[:, b, :], vv[:, b, h * P:(h + 1) * P],
                                                 start=(b == 0), stop=(b == t))
                        last.then_inc(O_ready, 1)

                    over_heads(pe, scores, values, lambda h, par: index_scores(h, par, banks[t][1:], 1))
                    pe.wait_ge(o_done, H * (t + 1) + 1)
                    pe.wait_ge(copied, before[t + 1])
                    for j in range(2):
                        for b in range(4):
                            last = pe.transpose(T[:, j, b * P:(b + 1) * P], o[:, 4 * j + b, :], k.ident[:, :])
                        last.then_inc(o_turned, 1)

            @block.scalar
            def _(act):
                act.sem_inc(copied, 2)
                act.wait_ge(ki_turned, 1)
                act.copy(ki[:, :], S[:, 0, :]).then_inc(ki_done, 1)
                act.sem_inc(rel_done, 1)
                for t in range(NT2):
                    W = (t + 1) * P
                    g = groups[t]

                    def first(h, par):
                        n = h + t * H
                        act.wait_ge(max_done, n + 1)
                        act.wait_ge(O_ready, n + 1)
                        act.activation(p[:, par, 0:W], X[:, par, 0:W], ACT.Exp, bias=nm[:, par:par + 1], scale=ATT_SCALE,
                                       accum_out=l[:, par:par + 1]).then_inc(p_done, 1)

                    def second(h, par):
                        n = h + t * H
                        act.wait_ge(O_ready, n + 2)
                        for j, (lo, hi) in enumerate(g):
                            act.wait_ge(turned, h * len(g) + (before[t] - 2 * t + j + 1))
                            act.copy(p_t[:, lo:hi, :], T[:, j % 2, 0:(hi - lo) * P].rearrange("p (b q) -> p b q", q=P)).then_inc(copied, 1)

                    def index_relu(h, par):
                        act.wait_ge(score_done, h + (t * H + 1))
                        for j, (lo, hi) in enumerate(banks[t]):
                            act.wait_ge(IS_ready, h * len(banks[t]) + (banks_before[t] + j + 1))
                            act.activation(rel[:, par, lo:hi], IS[:, 0:hi - lo], ACT.Relu).then_inc(rel_done, 1)
                    over_heads(act, first, lambda h, par: None, index_relu if banks[t] else None, before_first=second)
                    for j in range(2):
                        act.wait_ge(o_turned, 2 * t + j + 1)
                        if t >= 2 and j == 0:
                            act.wait_ge(stored[t % 2], 16 * (t // 2))
                        act.copy(ot[:, t % 2, 4 * j:4 * j + 4, :], T[:, j, :].rearrange("p (h q) -> p h q", q=P)).then_inc(ot_done, 1)
                    act.wait_ge(ot_done, 2 * t + 2)
                    act.sem_inc(copied, 2)

            @block.vector
            def _(dve):
                dve.sem_inc(O_ready, 2)
                dve.sem_inc(o_done, 1)
                dve.sem_inc(score_done, 2)
                dve.wait_ge(small_in, 48)
                for c in range(2):
                    dve.tensor_copy(kk2[:, :, c, :], kwt[:, :, 0:IDX_D])
                dve.drain().then_inc(kk2_done, 1)
                dve.tensor_scalar(wi[:, :, :], kwt[:, :, IDX_D:], IDX_SCALE, None, ALU.mult)
                for t in range(FIRST):
                    dve.tensor_scalar(dm[:, t, 0:(t + 1) * P], dn[:, 0:(t + 1) * P], -float(t * P), None, ALU.add)
                    dve.drain()
                    diag = slice(t * P, (t + 1) * P)
                    dve.tensor_tensor(dm[:, t, diag], dm[:, t, diag], cm[:, :], ALU.add)
                    dve.drain().then_inc(dm_done, 1)
                for t in range(NT2):
                    W = (t + 1) * P
                    scoring = bool(banks[t])
                    selecting = FIRST <= t + 1 < NT2
                    new = score[:, t % 2, 0:(t + FIRST + 1) * P] if scoring else None
                    sel = score[:, (t + 1) % 2, 0:W + P] if selecting else None
                    if scoring:
                        dve.memset(new, 0.0)
                        dve.drain()
                    if selecting:
                        dve.tensor_tensor(score[:, (t + 1) % 2, W:W + P], score[:, (t + 1) % 2, W:W + P], cm[:, :], ALU.add)
                        dve.drain()

                    def first(h, par):
                        n = h + t * H
                        dve.wait_ge(S_ready, n + 1)
                        dve.wait_ge(head_in, n + 1)
                        dve.wait_ge(O_ready, n + 1)
                        dve.tensor_tensor_reduce(X[:, par, 0:W], S[:, par, 0:W], bias[:, par, 0:W], 1.0, NEG, ALU.add, ALU.max,
                                                 mx[:, par:par + 1]).then_inc(X_done, 1)
                        dve.drain()
                        dve.tensor_scalar(nm[:, par:par + 1], mx[:, par:par + 1], -ATT_SCALE, None, ALU.mult).then_inc(max_done, 1)

                    def second(h, par):
                        n = h + t * H
                        if t >= 1 and h == 0:
                            dve.wait_ge(o_turned, 2 * t)
                        dve.wait_ge(O_ready, n + 3)
                        dve.reciprocal(rl[:, par:par + 1], l[:, par:par + 1])
                        dve.drain()
                        dve.tensor_scalar(o[:, h, :], O[:, 0:P], rl[:, par:par + 1], None,
                                          ALU.mult).then_inc(o_done, 1)

                    def add_scores(h, par):
                        dve.wait_ge(rel_done, h * len(banks[t]) + (banks_before[t] + len(banks[t]) + 1))
                        dve.scalar_tensor_tensor(new, rel[:, par, 0:(t + FIRST + 1) * P], wi[:, t + FIRST, h:h + 1],
                                                 new, ALU.mult, ALU.add)
                        dve.drain().then_inc(score_done, 1)

                    def select():
                        for _ in range(ROUNDS):
                            dve.max(top[:, :], sel)
                            dve.drain()
                            dve.match_replace(sel, top[:, :], sel, STRUCK)
                            dve.drain()
                    over_heads(dve, first, second, add_scores if scoring else None, select if selecting else None)
                    if selecting:
                        dve.tensor_scalar(sel, sel, STRUCK, NEG, ALU.not_equal, ALU.mult)
                        dve.drain()
                        dve.wait_ge(head_in, H * t)
                        dve.scalar_tensor_tensor(dm[:, (t + 1) % 2, 0:W + P], dn[:, 0:W + P], -float((t + 1) * P), sel, ALU.add, ALU.add)
                        dve.drain().then_inc(dm_done, 1)


N_GROUP = 4
PER_GROUP = 8
N_EXP2 = N_GROUP * PER_GROUP
EXTRA = 2 * SEQ // P
N_BLOCKS2 = N_EXP2 + EXTRA


def route_top2(nc, name, k, h_t, w_group, w_expert, b_group, b_expert, tab, tok_of, dest_out, gate_out, extra_out, used_out):
    NL = N_GROUP + N_EXP2
    E = N_EXP2
    with Phase(nc, name) as ph:
        h = ph.sb("h", [P, KD, SEQ])
        w = ph.sb("w", [P, KD, NL])
        bias = ph.sb("bias", [P, NL])
        ct = ph.sb("ct", [P, P])
        L = ph.sb("L", [P, NT2, NL])
        ge = ph.sb("ge", [P, NT2, N_GROUP])
        gm = ph.sb("gm", [P, NT2])
        gw = ph.sb("gw", [P, NT2])
        goh = ph.sb("goh", [P, NT2, N_GROUP])
        em = ph.sb("em", [P, NT2, E])
        tmp = ph.sb("tmp", [P, NT2, E])
        e = [ph.sb(f"e{i}", [P, NT2]) for i in range(2)]
        oh = [ph.sb(f"oh{i}", [P, NT2, E]) for i in range(2)]
        both = ph.sb("both", [P, NT2, E])
        m = ph.sb("m", [P, NT2])
        d = ph.sb("d", [P, NT2])
        p1 = ph.sb("p1", [P, NT2])
        gate = ph.sb("gate", [P, NT2, 2])
        pos = ph.sb("pos", [P, NT2, E])
        posi = ph.sb("posi", [P, NT2, E], I32)
        q = ph.sb("q", [P, NT2, E])
        cnt = ph.sb("cnt", [P, E])
        cnti = ph.sb("cnti", [P, E], I32)
        xtra = ph.sb("xtra", [P, E])
        xin = ph.sb("xin", [P, E])
        zero = ph.sb("zero", [P, E])
        A = ph.sb("A", [P, E])
        destf = ph.sb("destf", [P, NT2, 2])
        dest = ph.sb("dest", [P, NT2, 2], U32)
        tok = ph.sb("tok", [P, NT2], U32)
        zrow = ph.sb("zrow", [P, N_BLOCKS2], U32)
        cmp = ph.sb("cmp", [1, EXTRA, E])
        xe = ph.sb("xe", [1, EXTRA])
        xei = ph.sb("xei", [1, EXTRA + 1], I32)
        logits = ph.ps("logits", [P, BANK])
        pos_ps = ph.ps("pos_ps", [P, BANK])
        cnt_ps = ph.ps("cnt_ps", [P, BANK])
        loaded = ph.sem("loaded")
        zeroed = ph.sem("zeroed")
        table_zero = ph.sem("table_zero")
        logits_ready = ph.sem("logits_ready")
        centred = ph.sem("centred")
        exp_done = ph.sem("exp_done")
        both_done = ph.sem("both_done")
        pos_ready = ph.sem("pos_ready")
        dest_done = ph.sem("dest_done")
        scattered = ph.sem("scattered")
        done = ph.sem("done")
        stored = ph.sem("stored")
        with nc.Block() as block:

            @block.sync
            def _(sp):
                sp.dma_start(w[:, :, 0:N_GROUP], w_group.rearrange("(k p) e -> p k e", p=P)).then_inc(loaded, 16)
                sp.dma_start(w[:, :, N_GROUP:NL], w_expert.rearrange("(k p) e -> p k e", p=P)).then_inc(loaded, 16)
                sp.dma_start(bias[:, 0:N_GROUP], on_all(b_group)).then_inc(loaded, 16)
                sp.dma_start(bias[:, N_GROUP:NL], on_all(b_expert)).then_inc(loaded, 16)
                sp.dma_start(ct[:, :], tab).then_inc(loaded, 16)
                for c in range(KD):
                    sp.dma_start(h[:, c, :], h_t[c * P:(c + 1) * P, :]).then_inc(loaded, 16)
                sp.wait_ge(zeroed, 1)
                sp.dma_start(tok_of.rearrange("(b p) a -> p (b a)", p=P), zrow[:, :], allow_slow_non_contiguous=True).then_inc(table_zero, 16)
                sp.wait_ge(done, 1)
                sp.dma_start(dest_out, dest[:, :, :].rearrange("p t c -> p (t c)")).then_inc(stored, 16)
                sp.dma_start(gate_out, gate[:, :, :].rearrange("p t c -> p (t c)")).then_inc(stored, 16)
                sp.dma_start(extra_out, xei[:, 0:EXTRA]).then_inc(stored, 16)
                sp.dma_start(used_out, xei[:, EXTRA:EXTRA + 1], allow_slow_non_contiguous=True).then_inc(stored, 16)
                sp.wait_ge(stored, 64)

            @block.tensor
            def _(pe):
                pe.wait_ge(loaded, 16 * (KD + 5))
                for t in range(NT2):
                    for c in range(KD):
                        last = pe.matmul(logits[:, t * NL:(t + 1) * NL], h[:, c, t * P:(t + 1) * P], w[:, c, :],
                                         start=(c == 0), stop=(c == KD - 1))
                last.then_inc(logits_ready, 1)
                pe.wait_ge(both_done, 1)
                for t in range(NT2):
                    for s in range(t + 1):
                        pe.matmul(pos_ps[:, t * E:(t + 1) * E], k.before[:, :] if s == t else k.ones[:, :], both[:, s, :],
                                  start=(s == 0), stop=(s == t))
                for s in range(NT2):
                    last = pe.matmul(cnt_ps[:, 0:E], k.ones[:, :], both[:, s, :], start=(s == 0), stop=(s == NT2 - 1))
                last.then_inc(pos_ready, 1)

            @block.scalar
            def _(act):
                act.wait_ge(centred, 1)
                act.activation(ge[:, :, :], ge[:, :, :], ACT.Exp)
                act.activation(d[:, :], d[:, :], ACT.Exp).then_inc(exp_done, 1)

            @block.gpsimd
            def _(pool):
                pool.memset(zrow[:, :], 0).then_inc(zeroed, 1)
                pool.wait_ge(table_zero, 16)
                pool.wait_ge(dest_done, 1)
                for t in range(NT2):
                    for c in range(2):
                        pool.indirect_dma_start(out=tok_of, out_offset=bass.IndirectOffsetOnAxis(ap=dest[:, t, c:c + 1], axis=0),
                                                in_=tok[:, t:t + 1], in_offset=None).then_inc(scattered, 16)
                pool.wait_ge(scattered, 16 * 2 * NT2)

            @block.vector
            def _(dve):
                def wide(a, n):
                    return a[:, :].rearrange("p (t e) -> p t e", e=1).to_broadcast([P, NT2, n])

                def const(lo, n, shape):
                    a = ct[:, lo:lo + n]
                    return a.rearrange("p (t e) -> p t e", t=1).to_broadcast(shape)

                def first_max(out, values, top, rank, n):
                    dve.tensor_tensor(out, values, wide(top, n), ALU.is_equal)
                    dve.drain()
                    dve.tensor_tensor(out, out, rank, ALU.mult)
                    dve.drain()
                    dve.reduce_max(m[:, :], out, axis=AX.X)
                    dve.drain()
                    dve.tensor_tensor(out, out, wide(m, n), ALU.is_equal)
                    dve.drain()
                dve.memset(zero[:, :], 0.0)
                dve.wait_ge(loaded, 16 * (KD + 5))
                dve.wait_ge(logits_ready, 1)
                dve.tensor_tensor(L[:, :, :], logits[:, 0:NT2 * NL].rearrange("p (t e) -> p t e", e=NL),
                                  bias[:, :].rearrange("p (t e) -> p t e", t=1).to_broadcast([P, NT2, NL]), ALU.add)
                dve.tensor_copy(tok[:, :], ct[:, 100:100 + NT2])
                dve.drain()
                gl = L[:, :, 0:N_GROUP]
                dve.reduce_max(gm[:, :], gl, axis=AX.X)
                dve.drain()
                dve.tensor_tensor(ge[:, :, :], gl, wide(gm, N_GROUP), ALU.subtract)
                first_max(goh[:, :, :], gl, gm, const(96, N_GROUP, [P, NT2, N_GROUP]), N_GROUP)
                for g in range(N_GROUP):
                    cols = slice(g * PER_GROUP, (g + 1) * PER_GROUP)
                    of_g = goh[:, :, g:g + 1].to_broadcast([P, NT2, PER_GROUP])
                    dve.tensor_tensor(em[:, :, cols], L[:, :, N_GROUP + g * PER_GROUP:N_GROUP + (g + 1) * PER_GROUP], of_g, ALU.mult)
                    dve.tensor_scalar(tmp[:, :, cols], of_g, -1.0, -NEG, ALU.add, ALU.mult)
                dve.drain()
                dve.tensor_tensor(em[:, :, :], em[:, :, :], tmp[:, :, :], ALU.add)
                dve.drain()
                for c in range(2):
                    dve.reduce_max(e[c][:, :], em[:, :, :], axis=AX.X)
                    dve.drain()
                    first_max(oh[c][:, :, :], em[:, :, :], e[c], const(32, E, [P, NT2, E]), E)
                    if c == 0:
                        dve.scalar_tensor_tensor(em[:, :, :], oh[0][:, :, :], 3.0 * NEG, em[:, :, :], ALU.mult, ALU.add)
                        dve.drain()
                dve.tensor_tensor(both[:, :, :], oh[0][:, :, :], oh[1][:, :, :], ALU.add)
                dve.tensor_tensor(d[:, :], e[1][:, :], e[0][:, :], ALU.subtract)
                dve.drain().then_inc(both_done, 1)
                dve.sem_inc(centred, 1)
                dve.wait_ge(exp_done, 1)
                dve.reduce_sum(gw[:, :], ge[:, :, :], axis=AX.X)
                dve.tensor_scalar(p1[:, :], d[:, :], 1.0, None, ALU.add)
                dve.drain()
                dve.reciprocal(gw[:, :], gw[:, :])
                dve.reciprocal(p1[:, :], p1[:, :])
                dve.drain()
                dve.tensor_tensor(p1[:, :], p1[:, :], gw[:, :], ALU.mult)
                dve.drain()
                dve.tensor_copy(gate[:, :, 0], p1[:, :])
                dve.tensor_tensor(gate[:, :, 1], p1[:, :], d[:, :], ALU.mult)
                dve.wait_ge(pos_ready, 1)
                pv = pos_ps[:, 0:NT2 * E].rearrange("p (t e) -> p t e", e=E)
                dve.tensor_copy(pos[:, :, :], pv)
                dve.tensor_copy(posi[:, :, :], pv)
                dve.tensor_scalar(cnt[:, :], cnt_ps[:, 0:E], -1.0, 0.0, ALU.add, ALU.max)
                dve.drain()
                dve.tensor_copy(cnti[:, :], cnt[:, :])
                dve.tensor_scalar(posi[:, :, :], posi[:, :, :], 7, None, ALU.arith_shift_right)
                dve.drain()
                dve.tensor_scalar(cnti[:, :], cnti[:, :], 7, None, ALU.arith_shift_right)
                dve.tensor_copy(q[:, :, :], posi[:, :, :])
                dve.drain()
                dve.tensor_copy(xtra[:, :], cnti[:, :])
                dve.drain()
                dve.tensor_tensor_scan(xin[:, :], xtra[:, :], zero[:, :], 0.0, ALU.add, ALU.add)
                dve.drain()
                dve.tensor_tensor(A[:, :], xin[:, :], xtra[:, :], ALU.subtract)
                dve.drain()
                dve.tensor_tensor(A[:, :], A[:, :], ct[:, 0:E], ALU.subtract)
                dve.drain()
                dve.tensor_scalar(A[:, :], A[:, :], float(E - 1), None, ALU.add)
                dve.drain()
                flat = lambda a: a.rearrange("p (t e) -> p t e", t=1).to_broadcast([P, NT2, E])
                dve.tensor_tensor(tmp[:, :, :], q[:, :, :], flat(A[:, :]), ALU.add)
                dve.drain()
                dve.scalar_tensor_tensor(tmp[:, :, :], q[:, :, :], 0.0, tmp[:, :, :], ALU.is_gt, ALU.mult)
                dve.drain()
                dve.tensor_tensor(tmp[:, :, :], tmp[:, :, :], q[:, :, :], ALU.subtract)
                dve.drain()
                dve.tensor_tensor(tmp[:, :, :], tmp[:, :, :], flat(ct[:, 0:E]), ALU.add)
                dve.drain()
                dve.scalar_tensor_tensor(pos[:, :, :], tmp[:, :, :], float(P), pos[:, :, :], ALU.mult, ALU.add)
                dve.drain()
                for c in range(2):
                    dve.tensor_tensor(tmp[:, :, :], oh[c][:, :, :], pos[:, :, :], ALU.mult)
                    dve.drain()
                    dve.reduce_sum(destf[:, :, c], tmp[:, :, :], axis=AX.X)
                    dve.drain()
                dve.tensor_copy(dest[:, :, :], destf[:, :, :])
                dve.drain().then_inc(dest_done, 1)
                dve.tensor_tensor(cmp[:, :, :], ct[0:1, 64:64 + EXTRA].rearrange("p (x e) -> p x e", e=1).to_broadcast([1, EXTRA, E]),
                                  xin[0:1, :].rearrange("p (x e) -> p x e", x=1).to_broadcast([1, EXTRA, E]), ALU.is_ge)
                dve.drain()
                dve.reduce_sum(xe[:, :], cmp[:, :, :], axis=AX.X)
                dve.drain()
                dve.tensor_scalar(xe[:, :], xe[:, :], float(E - 1), None, ALU.min)
                dve.drain()
                dve.tensor_copy(xei[:, 0:EXTRA], xe[:, :])
                dve.tensor_copy(xei[:, EXTRA:EXTRA + 1], xin[0:1, E - 1:E])
                dve.drain().then_inc(done, 1)


def constants():
    i32 = np.arange(P)
    row, col = np.meshgrid(i32, i32, indexing="ij")
    levels = []
    for lv in range(7):
        s = 2 ** lv
        levels.append((col // (2 * s) == row // (2 * s)) & (col // s == row // s + 1))
    upto = row <= col
    grid_w, axis = 64, DA_D // 2
    t = np.arange(SEQ)
    rows = (t // grid_w).astype(np.float32)
    cols = (t % grid_w).astype(np.float32)
    inv = np.power(np.float32(10000.0), -np.arange(0, axis, 2, dtype=np.float32) / np.float32(axis)).astype(np.float32)
    ang = np.stack([(rows if (p % DA_D) // axis == 0 else cols) * inv[p % (axis // 2)] for p in range(P)]).astype(np.float32)
    swap = np.zeros((P, P), np.float32)
    for p in range(P):
        lower = p % axis < axis // 2
        swap[p + axis // 2 if lower else p - axis // 2, p] = -1.0 if lower else 1.0
    slopes = 2.0 ** (-8.0 * np.arange(1, HEADS2 + 1) / HEADS2)
    tab = np.zeros((P, P), np.float32)
    tab[:, 0:32] = np.arange(32)
    tab[:, 32:64] = 32 - np.arange(32)
    tab[:, 64:96] = np.arange(32)
    tab[:, 96:100] = 4 - np.arange(4)
    tab[:, 100:100 + NT2] = np.arange(NT2)[None] * P + i32[:, None]
    out = {
        "ident": np.eye(P), "ones": np.ones((P, P)), "upto0": upto, "upto1": upto.T, "before": row < col,
        "rope_swap": swap, "rope_cos": np.cos(ang), "rope_sin": np.sin(ang),
        "levels0": np.concatenate(levels, 1), "levels1": np.concatenate([x.T for x in levels], 1),
        "causal": np.where(col <= row, 0.0, NEG), "dist": np.arange(SEQ)[None] - i32[:, None],
        "slopes": np.tile(slopes / ATT_SCALE, (P, 1)), "route_tab": tab,
    }
    return {n: np.ascontiguousarray(a, dtype=np.float32) for n, a in out.items()}


class Resident:
    pass


def load_resident(nc, stack, c):
    k = Resident()
    names = ("ident", "ones", "upto0", "upto1", "before", "rope_swap")
    t = {n: stack.enter_context(nc.sbuf_tensor(f"k_{n}", [P, P], F32)) for n in names}
    half = stack.enter_context(nc.sbuf_tensor("k_minus_half", [P, 1], F32))
    with Phase(nc, "resident") as ph:
        loaded = ph.sem("loaded")
        with nc.Block() as block:

            @block.sync
            def _(sp):
                for n in names:
                    sp.dma_start(t[n][:, :], c[n]).then_inc(loaded, 16)
                sp.wait_ge(loaded, 16 * len(names))

            @block.vector
            def _(dve):
                dve.memset(half[:, :], -0.5)
    k.ident, k.ones, k.before, k.rope_swap = t["ident"], t["ones"], t["before"], t["rope_swap"]
    k.upto = [t["upto0"][:, :], t["upto1"][:, :]]
    k.minus_half = half
    return k


def clear_rows(nc, name, out):
    n = out.shape[0] // P
    with Phase(nc, name) as ph:
        z = ph.sb("z", [P, D])
        zeroed = ph.sem("zeroed")
        stored = ph.sem("stored")
        with nc.Block() as block:

            @block.vector
            def _(dve):
                dve.memset(z[:, :], 0.0).then_inc(zeroed, 1)

            @block.sync
            def _(sp):
                sp.wait_ge(zeroed, 1)
                for t in range(n):
                    sp.dma_start(out[t * P:(t + 1) * P, :], z[:, :]).then_inc(stored, 16)
                sp.wait_ge(stored, 16 * n)


SCRATCH = {
    "mod1": ([2, NMOD], F32), "mod2": ([1, NMOD], F32),
    "h_t": ([D, T1], F32), "g_raw_t": ([3 * GQ, T1], F32), "qk_t": ([2 * HEADS1 * P, T1], F32),
    "vga": ([T1, 1040], F32), "g_t": ([3 * GQ, T1], F32), "o_da": ([SEQ, HEADS1 * P], F32),
    "o_fwd": ([T1, GQ], F32), "o_rev": ([T1, GQ], F32), "mix_t": ([D, SEQ], F32),
    "x1": ([SEQ, D], F32), "x1_n": ([SEQ, D], F32), "x1_t": ([D, SEQ], F32),
    "choice": ([N_EXP1, CAP1], U32), "affinity": ([N_EXP1, CAP1], F32), "moe1": ([SEQ, D], F32), "x2": ([SEQ, D], F32),
    "u_t": ([D, SEQ], F32), "p_t": ([4352, SEQ], F32), "merge_t": ([2048, SEQ], F32), "kw": ([SEQ, 72], F32),
    "c_t": ([KV_RANK, SEQ], F32), "k_t": ([D, SEQ], F32), "v": ([SEQ, D], F32),
    "rnn_t": ([D_RNN, SEQ], F32), "att_t": ([D, SEQ], F32), "ya_t": ([D, SEQ], F32), "yab_t": ([D, SEQ], F32),
    "h1": ([SEQ, D], F32), "h1_n": ([SEQ, D], F32), "h1_t": ([D, SEQ], F32),
    "tok_of": ([N_BLOCKS2 * P, 1], U32), "dest": ([P, 2 * NT2], U32), "gate2": ([P, 2 * NT2], F32),
    "extra": ([1, EXTRA], I32), "used": ([1, 1], I32), "rows2": ([N_BLOCKS2 * P, D], F32),
}


def build(nc, a, c, s, out):
    with ExitStack() as stack:
        k = load_resident(nc, stack, c)
        mod = lambda m, i, row=0: s[m][row, i * D:(i + 1) * D]
        modulation(nc, "mod1", [a["c"][0], a["c_ctx"]], a["w_mod"][0], a["b_mod"][0], s["mod1"])
        modulation(nc, "mod2", [a["c_2"][0]], a["w_mod_2"][0], a["b_mod_2"][0], s["mod2"])
        norm_transpose(nc, "norm_ctx", k, a["ctx"][0], a["norm1_g"][0], mod("mod1", 0, 1), mod("mod1", 1, 1), s["h_t"][:, 0:CTX])
        norm_transpose(nc, "norm_lat", k, a["x"][0], a["norm1_g"][0], mod("mod1", 0), mod("mod1", 1), s["h_t"][:, CTX:T1])
        w_in = a["w_in"][0]
        gemm_t(nc, "proj_qk", s["h_t"], w_in[:, 0:1024], s["qk_t"])
        gemm_t(nc, "proj_gdn", s["h_t"], w_in[:, 1536:3072], s["g_raw_t"])
        gemm_tok(nc, "proj_v", s["h_t"], [w_in[:, 1024:1536], w_in[:, 3072:3600]], s["vga"])
        diff_attention(nc, "da", k, s["qk_t"], s["vga"][:, 0:512], [a[n][0] for n in ("lam_q1", "lam_k1", "lam_q2", "lam_k2")],
                       c["rope_cos"], c["rope_sin"], s["o_da"])
        short_conv_l2(nc, "conv", k, s["g_raw_t"], a["conv_w"][0], s["g_t"])
        delta_rule(nc, "gdn", k, s["g_t"], s["vga"][:, 1024:1040], a["a_log"][0].rearrange("d h -> (d h)"),
                   a["dt_bias"][0].rearrange("d h -> (d h)"), [c["levels0"], c["levels1"]], [s["o_fwd"], s["o_rev"]])
        mix_norm(nc, "mix", k, s["o_da"], [s["o_fwd"], s["o_rev"]], s["vga"][:, 512:1024], a["da_subln_g"][0], a["gdn_norm_g"][0], s["mix_t"])
        gemm_tok(nc, "out1", s["mix_t"], [a["w_out"][0]], s["x1"], residual=a["x"][0], gain=mod("mod1", 2))
        norm_transpose(nc, "norm_moe1", k, s["x1"], a["norm2_g"][0], mod("mod1", 3), mod("mod1", 4), s["x1_t"], s["x1_n"])
        expert_choice(nc, "choose1", k, s["x1_t"], a["w_router"][0], s["choice"], s["affinity"])
        clear_rows(nc, "clear1", s["moe1"])
        experts(nc, "exp1", k, N_EXP1, s["choice"], s["x1_n"], a["norm2_g"][0], mod("mod1", 3), mod("mod1", 4),
                a["w_gate"][0], a["w_up"][0], a["w_down"][0], gates=s["affinity"], acc=s["moe1"])
        finish(nc, "fin1", k, s["x1"], mod("mod1", 5), a["final_g"], s["x2"], acc=s["moe1"])
        norm_transpose(nc, "norm2", k, s["x2"], a["norm1_g_2"][0], mod("mod2", 0), mod("mod2", 1), s["u_t"])
        w2 = a["w_in_2"][0]
        gemm_t(nc, "proj2", s["u_t"], w2[:, 0:4352], s["p_t"])
        gemm_t(nc, "proj2_merge", s["u_t"], w2[:, 4424:6472], s["merge_t"])
        gemm_tok(nc, "proj2_kw", s["u_t"], [w2[:, 4352:4424]], s["kw"])
        rg_lru(nc, "rnn", k, s["p_t"][0:D_RNN], s["p_t"][D_RNN:2 * D_RNN], a["conv_w_2"][0], a["conv_b_2"][0], a["w_rg_a_2"][0],
               a["b_rg_a_2"][0], a["w_rg_x_2"][0], a["b_rg_x_2"][0], a["lru_lambda_2"][0], s["rnn_t"])
        gemm_t(nc, "rnn_out", s["rnn_t"], a["w_rnn_out_2"][0], s["ya_t"], gate_t=s["merge_t"][0:D])
        kv_norm(nc, "kvn", k, s["p_t"][3584:3840], a["kv_norm_g_2"][0], s["c_t"])
        gemm_t(nc, "uk", s["c_t"], a["w_uk_2"][0].rearrange("r h d -> r (h d)"), s["k_t"])
        gemm_tok(nc, "uv", s["c_t"], [a["w_uv_2"][0].rearrange("r h d -> r (h d)")], s["v"])
        sparse_attention(nc, "dsa", k, s["p_t"][2560:3584], s["k_t"], s["v"], s["p_t"][3840:4352], s["kw"],
                         c["dist"], c["causal"], c["slopes"], s["att_t"])
        gemm_t(nc, "att_out", s["att_t"], a["w_att_out_2"][0], s["yab_t"], gate_t=s["merge_t"][D:2 * D], add_t=s["ya_t"])
        gemm_tok(nc, "out2", s["yab_t"], [a["w_out_2"][0]], s["h1"], residual=s["x2"], gain=mod("mod2", 2))
        norm_transpose(nc, "norm_moe2", k, s["h1"], a["norm2_g_2"][0], mod("mod2", 3), mod("mod2", 4), s["h1_t"], s["h1_n"])
        route_top2(nc, "route2", k, s["h1_t"], a["w_group_2"][0], a["w_expert_2"][0], a["b_group_2"][0], a["b_expert_2"][0],
                   c["route_tab"], s["tok_of"], s["dest"], s["gate2"], s["extra"], s["used"])
        toks = s["tok_of"].rearrange("(b p) a -> b (p a)", p=P)
        weights = [a[n][0] for n in ("moe_w1_2", "moe_w3_2", "moe_w2_2")]
        clear_rows(nc, "clear2", s["rows2"][N_EXP2 * P:])
        experts(nc, "exp2", k, N_EXP2, toks[0:N_EXP2], s["h1_n"], a["norm2_g_2"][0], mod("mod2", 3), mod("mod2", 4), *weights,
                rows_out=s["rows2"])
        experts(nc, "exp2x", k, EXTRA, toks[N_EXP2:N_BLOCKS2], s["h1_n"], a["norm2_g_2"][0], mod("mod2", 3), mod("mod2", 4), *weights,
                rows_out=s["rows2"], first=N_EXP2, expert_of=s["extra"], used=s["used"])
        finish(nc, "fin2", k, s["h1"], mod("mod2", 5), a["final_g_2"], out, rows=s["rows2"], dest=s["dest"], gates=s["gate2"])


INPUTS = ["x", "c", "ctx", "c_ctx", "w_mod", "b_mod", "norm1_g", "w_in", "conv_w", "a_log", "dt_bias", "gdn_norm_g", "lam_q1",
          "lam_k1", "lam_q2", "lam_k2", "da_subln_g", "w_out", "norm2_g", "w_router", "w_gate", "w_up", "w_down", "final_g",
          "c_2", "w_mod_2", "b_mod_2", "norm1_g_2", "w_in_2", "conv_w_2", "conv_b_2", "w_rg_a_2", "b_rg_a_2", "w_rg_x_2",
          "b_rg_x_2", "lru_lambda_2", "kv_norm_g_2", "w_uk_2", "w_uv_2", "w_rnn_out_2", "w_att_out_2", "w_out_2", "norm2_g_2",
          "w_group_2", "b_group_2", "w_expert_2", "b_expert_2", "moe_w1_2", "moe_w3_2", "moe_w2_2", "final_g_2"]


def kernel(**inputs):
    import concourse.bacc as bacc
    from concourse.bass_utils import run_bass_kernel_spmd

    nc = bacc.Bacc("TRN2", target_bir_lowering=False, num_devices=1)
    arrays, a, c = {}, {}, {}
    for name in INPUTS:
        arrays[f"in_{name}"] = np.ascontiguousarray(inputs[name])
        a[name] = nc.dram_tensor(f"in_{name}", arrays[f"in_{name}"].shape, F32, kind="ExternalInput").ap()
    for name, value in constants().items():
        arrays[f"const_{name}"] = value
        c[name] = nc.dram_tensor(f"const_{name}", value.shape, F32, kind="ExternalInput").ap()
    s = {name: nc.dram_tensor(f"scratch_{name}", shape, dt).ap() for name, (shape, dt) in SCRATCH.items()}
    out = nc.dram_tensor("out", [SEQ, D], F32, kind="ExternalOutput").ap()
    build(nc, a, c, s, out)
    r = run_bass_kernel_spmd(nc, [arrays], core_ids=[0])
    return np.asarray(r.results[0]["out"]).reshape(1, SEQ, D)
```
